# Optimizing a Trainium2 kernel written in Bass

```python
import math
import jax
import jax.numpy as jnp
from jax import lax
import numpy as np
import jax, jax.numpy as jnp

D_MODEL = 1024
BATCH = 1
SEQ = 256
DEPTH = 2

GRID_W = 64
CTX_LEN = 256
MIX_WIDTH = D_MODEL
A_WIDTH = MIX_WIDTH // 2
B_WIDTH = MIX_WIDTH - A_WIDTH
SHORT_CONV_W = 3
CONFORMER_CONV_W = 31
AB_IN = 3 * A_WIDTH + 2 * B_WIDTH
C_HEAD_DIM = 64
C_V_DIM = 2 * C_HEAD_DIM
C_HEADS = (MIX_WIDTH // 2) // C_V_DIM
C_QK = C_HEADS * 2 * C_HEAD_DIM
C_V = C_HEADS * C_V_DIM
HY_WIDTH = MIX_WIDTH - C_V
CD_IN = 2 * C_QK + C_V + 3 * HY_WIDTH
Q_BLOCK = 128
ROPE_THETA = 10000.0
HY_BANDS = 16
HY_EMB = 2 * HY_BANDS + 1
HY_ORDER = 64
HY_MIN_DECAY = math.log(1e-2) / 1.5
HY_MAX_DECAY = math.log(1e-2) / 0.3
N_EXPERTS = 16
EXPERT_FF = 1024
EC_CAPACITY = 2
NORM_EPS = 1e-6
SUBLN_EPS = 1e-5


def rms_norm(x, g, eps=NORM_EPS):
    xf = x.astype(jnp.float32)
    y = xf * lax.rsqrt(jnp.mean(jnp.square(xf), axis=-1, keepdims=True) + eps)
    return (y * g.astype(jnp.float32)).astype(x.dtype)

def layer_norm(x, g, b, eps=NORM_EPS):
    xf = x.astype(jnp.float32)
    mu = jnp.mean(xf, axis=-1, keepdims=True)
    var = jnp.mean(jnp.square(xf - mu), axis=-1, keepdims=True)
    y = (xf - mu) * lax.rsqrt(var + eps)
    return (y * g.astype(jnp.float32) + b.astype(jnp.float32)).astype(x.dtype)

def modulate(h, shift, scale):
    return h * (1 + scale) + shift

def depthwise_conv(u, w):
    k = w.shape[0]
    pad = (k - 1) // 2
    return lax.conv_general_dilated(
        u, w[:, None, :].astype(u.dtype), window_strides=(1,), padding=[(pad, pad)],
        dimension_numbers=('NWC', 'WIO', 'NWC'), feature_group_count=u.shape[-1])

def conv_mixers(u, w_in, conv_a, conv_b, conv_b_bias, ln_g, ln_b, w_out):
    p = u @ w_in
    gate_out, gate_in, val, glu_a, glu_g = jnp.split(
        p, [A_WIDTH, 2 * A_WIDTH, 3 * A_WIDTH, 3 * A_WIDTH + B_WIDTH], axis=-1)
    y_a = gate_out * depthwise_conv(gate_in * val, conv_a)
    z = depthwise_conv(glu_a * jax.nn.sigmoid(glu_g), conv_b) + conv_b_bias
    y_b = jax.nn.silu(layer_norm(z, ln_g, ln_b))
    return jnp.concatenate([y_a, y_b], axis=-1) @ w_out

def axial_rope_angles(seq_len):
    rows = seq_len // GRID_W
    row = jnp.repeat(jnp.arange(rows), GRID_W).astype(jnp.float32)
    col = jnp.tile(jnp.arange(GRID_W), rows).astype(jnp.float32)
    n_freq = C_HEAD_DIM // 4
    inv = ROPE_THETA ** (-jnp.arange(n_freq, dtype=jnp.float32) / n_freq)
    return row[:, None] * inv[None], col[:, None] * inv[None]

def rope_half(x, ang):
    cos = jnp.cos(ang)[None, :, None, None, :].astype(x.dtype)
    sin = jnp.sin(ang)[None, :, None, None, :].astype(x.dtype)
    x1, x2 = jnp.split(x, 2, axis=-1)
    return jnp.concatenate([x1 * cos - x2 * sin, x1 * sin + x2 * cos], axis=-1)

def axial_rope(x, ang_row, ang_col):
    xr, xc = jnp.split(x, 2, axis=-1)
    return jnp.concatenate([rope_half(xr, ang_row), rope_half(xc, ang_col)], axis=-1)

def split_q(p_q, g_q):
    b, l, _ = p_q.shape
    return rms_norm(p_q.reshape(b, l, C_HEADS, 2, C_HEAD_DIM), g_q)

def split_kv(p_kv, g_k):
    b, l, _ = p_kv.shape
    k, v = jnp.split(p_kv, [C_QK], axis=-1)
    k = rms_norm(k.reshape(b, l, C_HEADS, 2, C_HEAD_DIM), g_k)
    return k, v.reshape(b, l, C_HEADS, C_V_DIM)

def diff_attention(q, k, v, lam):
    s = jnp.einsum('bqhjd,bkhjd->bhjqk', q, k, preferred_element_type=jnp.float32) * (C_HEAD_DIM ** -0.5)
    p = jax.nn.softmax(s, axis=-1)
    a = p[:, :, 0] - lam * p[:, :, 1]
    return jnp.einsum('bhqk,bkhe->bqhe', a.astype(v.dtype), v)

def diff_attention_blocked(q, k, v, lam):
    b, l, h, _, dh = q.shape
    nb = l // Q_BLOCK
    qb = jnp.moveaxis(q.reshape(b, nb, Q_BLOCK, h, 2, dh), 1, 0)
    o = lax.map(lambda qi: diff_attention(qi, k, v, lam), qb)
    return jnp.moveaxis(o, 0, 1).reshape(b, l, h, C_V_DIM)

def diff_head_out(o, g_sub, lam_init):
    b, l = o.shape[:2]
    return (rms_norm(o, g_sub, SUBLN_EPS) * (1.0 - lam_init)).reshape(b, l, C_V)

def hyena_filter(seq_len, w1, b1, freq, w2, b2, w3):
    f32 = jnp.float32
    t = jnp.arange(seq_len, dtype=f32)
    t_unit = jnp.linspace(0.0, 1.0, seq_len)[:, None]
    bands = jnp.linspace(1e-4, HY_BANDS - 1, HY_BANDS)
    ang = (2.0 * math.pi / seq_len) * t[:, None] * bands[None]
    z = jnp.concatenate([t_unit, jnp.cos(ang), -jnp.sin(ang)], axis=-1)
    fr = freq.astype(f32)
    hid = jnp.sin(fr * (z @ w1.astype(f32) + b1.astype(f32)))
    hid = jnp.sin(fr * (hid @ w2.astype(f32) + b2.astype(f32)))
    h = hid @ w3.astype(f32)
    centre = seq_len // 2
    dist = jnp.abs(t - centre) / max(centre, 1)
    decay = jnp.abs(jnp.linspace(HY_MIN_DECAY, HY_MAX_DECAY, h.shape[-1]))
    return h * jnp.exp(-dist[:, None] * decay[None])

def fft_long_conv(u, h, bias):
    l = u.shape[1]
    n = 2 * l
    c0 = l // 2
    uf = jnp.fft.rfft(u.astype(jnp.float32), n=n, axis=1)
    hf = jnp.fft.rfft(h, n=n, axis=0)
    y = jnp.fft.irfft(uf * hf[None], n=n, axis=1)[:, c0:c0 + l]
    return (y + u.astype(jnp.float32) * bias.astype(jnp.float32)).astype(u.dtype)

def hyena_mixer(p_hy, conv_d, filt, bias):
    z = depthwise_conv(p_hy, conv_d)
    gate_out, gate_in, val = jnp.split(z, 3, axis=-1)
    return gate_out * fft_long_conv(gate_in * val, filt, bias)

def expert_choice_ffn(h, w_router, w_gate, w_up, w_down):
    b, n, d = h.shape
    cap = max(1, (EC_CAPACITY * n) // N_EXPERTS)
    aff = jax.nn.softmax((h @ w_router).astype(jnp.float32), axis=-1)
    g, idx = lax.top_k(jnp.swapaxes(aff, 1, 2), cap)
    xe = jax.vmap(lambda hb, ib: hb[ib])(h, idx)
    a = jnp.einsum('becd,edf->becf', xe, w_gate)
    up = jnp.einsum('becd,edf->becf', xe, w_up)
    y = jnp.einsum('becf,efd->becd', jax.nn.silu(a) * up, w_down) * g[..., None].astype(h.dtype)
    return jax.vmap(lambda ib, yb: jnp.zeros((n, d), h.dtype).at[ib.reshape(-1)].add(yb.reshape(-1, d)))(idx, y)

def first_inputs(seed: int = 0) -> dict:
    key = jax.random.key(seed)
    ks = iter(jax.random.split(key, 48))

    def nrm(shape, scale):
        return jax.random.normal(next(ks), shape, jnp.float32) * scale

    d = D_MODEL
    n_even = (DEPTH + 1) // 2
    n_odd = DEPTH // 2
    return {
        'x': nrm((BATCH, SEQ, d), 1.0),
        'c': nrm((BATCH, d), 1.0),
        'ctx': nrm((BATCH, CTX_LEN, d), 1.0),
        'c_ctx': nrm((d,), 1.0),
        'w_ada': nrm((DEPTH, d, 6 * d), 0.5 * d ** -0.5),
        'b_ada': nrm((DEPTH, 6 * d), 0.02),
        'g_mix': 1.0 + nrm((DEPTH, d), 0.1),
        'g_ffn': 1.0 + nrm((DEPTH, d), 0.1),
        'w_in_ab': nrm((n_even, d, AB_IN), d ** -0.5),
        'conv_a': nrm((n_even, SHORT_CONV_W, A_WIDTH), SHORT_CONV_W ** -0.5),
        'conv_b': nrm((n_even, CONFORMER_CONV_W, B_WIDTH), CONFORMER_CONV_W ** -0.5),
        'conv_b_bias': nrm((n_even, B_WIDTH), 0.02),
        'ln_b_g': 1.0 + nrm((n_even, B_WIDTH), 0.1),
        'ln_b_b': nrm((n_even, B_WIDTH), 0.02),
        'w_out_ab': nrm((n_even, MIX_WIDTH, d), MIX_WIDTH ** -0.5),
        'w_in_cd': nrm((n_odd, d, CD_IN), d ** -0.5),
        'g_q': 1.0 + nrm((n_odd, C_HEAD_DIM), 0.1),
        'g_k': 1.0 + nrm((n_odd, C_HEAD_DIM), 0.1),
        'lam_q1': nrm((n_odd, C_HEAD_DIM), 0.1),
        'lam_k1': nrm((n_odd, C_HEAD_DIM), 0.1),
        'lam_q2': nrm((n_odd, C_HEAD_DIM), 0.1),
        'lam_k2': nrm((n_odd, C_HEAD_DIM), 0.1),
        'g_subln': 1.0 + nrm((n_odd, C_V_DIM), 0.1),
        'conv_d': nrm((n_odd, SHORT_CONV_W, 3 * HY_WIDTH), SHORT_CONV_W ** -0.5),
        'hf_w1': nrm((n_odd, HY_EMB, HY_ORDER), HY_EMB ** -0.5),
        'hf_b1': nrm((n_odd, HY_ORDER), 0.1),
        'hf_freq': 1.0 + nrm((n_odd, HY_ORDER), 0.1),
        'hf_w2': nrm((n_odd, HY_ORDER, HY_ORDER), HY_ORDER ** -0.5),
        'hf_b2': nrm((n_odd, HY_ORDER), 0.1),
        'hf_w3': nrm((n_odd, HY_ORDER, HY_WIDTH), 0.02),
        'hf_bias': nrm((n_odd, HY_WIDTH), 0.1),
        'w_out_cd': nrm((n_odd, MIX_WIDTH, d), MIX_WIDTH ** -0.5),
        'w_router': nrm((DEPTH, d, N_EXPERTS), d ** -0.5),
        'w_gate': nrm((DEPTH, N_EXPERTS, d, EXPERT_FF), d ** -0.5),
        'w_up': nrm((DEPTH, N_EXPERTS, d, EXPERT_FF), d ** -0.5),
        'w_down': nrm((DEPTH, N_EXPERTS, EXPERT_FF, d), EXPERT_FF ** -0.5),
    }

def first_block(x, c, ctx, c_ctx, w_ada, b_ada, g_mix, g_ffn, w_in_ab, conv_a, conv_b, conv_b_bias,
              ln_b_g, ln_b_b, w_out_ab, w_in_cd, g_q, g_k, lam_q1, lam_k1, lam_q2, lam_k2, g_subln,
              conv_d, hf_w1, hf_b1, hf_freq, hf_w2, hf_b2, hf_w3, hf_bias, w_out_cd,
              w_router, w_gate, w_up, w_down):
    f32 = jnp.float32
    seq_lat = x.shape[1]
    seq_ctx = ctx.shape[1]
    ang_row, ang_col = axial_rope_angles(seq_lat)
    cond_lat = jax.nn.silu(c)
    cond_ctx = jax.nn.silu(c_ctx)[None]
    h_lat, h_ctx = x, ctx
    kv_cols = slice(C_QK, 2 * C_QK + C_V)
    hy_cols = slice(2 * C_QK + C_V, CD_IN)
    for l in range(DEPTH):
        last = l == DEPTH - 1
        odd = l % 2 == 1
        i = l // 2
        mod_lat = jnp.split((cond_lat @ w_ada[l] + b_ada[l])[:, None, :], 6, axis=-1)
        u_lat = modulate(rms_norm(h_lat, g_mix[l]), mod_lat[0], mod_lat[1])
        if odd or not last:
            mod_ctx = jnp.split((cond_ctx @ w_ada[l] + b_ada[l])[:, None, :], 6, axis=-1)
            u_ctx = modulate(rms_norm(h_ctx, g_mix[l]), mod_ctx[0], mod_ctx[1])
        if not odd:
            ab = (w_in_ab[i], conv_a[i], conv_b[i], conv_b_bias[i], ln_b_g[i], ln_b_b[i], w_out_ab[i])
            y_lat = conv_mixers(u_lat, *ab)
            if not last:
                y_ctx = conv_mixers(u_ctx, *ab)
        else:
            lam_init = 0.8 - 0.6 * math.exp(-0.3 * l)
            lam = (jnp.exp(jnp.sum(lam_q1[i].astype(f32) * lam_k1[i].astype(f32)))
                   - jnp.exp(jnp.sum(lam_q2[i].astype(f32) * lam_k2[i].astype(f32))) + lam_init)
            w_in = w_in_cd[i]
            p_lat = u_lat @ w_in
            q_l = axial_rope(split_q(p_lat[..., :C_QK], g_q[i]), ang_row, ang_col)
            k_l, v_l = split_kv(p_lat[..., kv_cols], g_k[i])
            k_l = axial_rope(k_l, ang_row, ang_col)
            if last:
                k_c, v_c = split_kv(u_ctx @ w_in[:, kv_cols], g_k[i])
            else:
                p_ctx = u_ctx @ w_in
                q_c = split_q(p_ctx[..., :C_QK], g_q[i])
                k_c, v_c = split_kv(p_ctx[..., kv_cols], g_k[i])
            k_all = jnp.concatenate([k_c, k_l], axis=1)
            v_all = jnp.concatenate([v_c, v_l], axis=1)
            o_lat = diff_attention_blocked(q_l, k_all, v_all, lam)
            filt_lat = hyena_filter(seq_lat, hf_w1[i], hf_b1[i], hf_freq[i], hf_w2[i], hf_b2[i], hf_w3[i])
            y_hy_lat = hyena_mixer(p_lat[..., hy_cols], conv_d[i], filt_lat, hf_bias[i])
            y_lat = jnp.concatenate([diff_head_out(o_lat, g_subln[i], lam_init), y_hy_lat], axis=-1) @ w_out_cd[i]
            if not last:
                o_ctx = diff_attention(q_c, k_c, v_c, lam)
                filt_ctx = hyena_filter(seq_ctx, hf_w1[i], hf_b1[i], hf_freq[i], hf_w2[i], hf_b2[i], hf_w3[i])
                y_hy_ctx = hyena_mixer(p_ctx[..., hy_cols], conv_d[i], filt_ctx, hf_bias[i])
                y_ctx = jnp.concatenate([diff_head_out(o_ctx, g_subln[i], lam_init), y_hy_ctx], axis=-1) @ w_out_cd[i]
        h_lat = h_lat + mod_lat[2] * y_lat
        u2 = modulate(rms_norm(h_lat, g_ffn[l]), mod_lat[3], mod_lat[4])
        h_lat = h_lat + mod_lat[5] * expert_choice_ffn(u2, w_router[l], w_gate[l], w_up[l], w_down[l])
        if not last:
            h_ctx = h_ctx + mod_ctx[2] * y_ctx
            u2c = modulate(rms_norm(h_ctx, g_ffn[l]), mod_ctx[3], mod_ctx[4])
            h_ctx = h_ctx + mod_ctx[5] * expert_choice_ffn(u2c, w_router[l], w_gate[l], w_up[l], w_down[l])
    return h_lat


DEPTH_2 = 4

N_MIXERS = 3
D_FF = 4 * D_MODEL
ROPE_BASE = 10000.0
EPS = 1e-6
NEG_INF = -1e30

MLA_HEADS = 8
MLA_Q_RANK = 256
MLA_KV_RANK = 128
MLA_NOPE = 128
MLA_ROPE = 64
MLA_V = 128

SB_HEADS = 16
SB_HEAD_DIM = D_MODEL // SB_HEADS

RET_HEADS = 4
RET_KEY_DIM = D_MODEL // RET_HEADS
RET_VAL_DIM = 2 * D_MODEL // RET_HEADS
RET_CHUNK = 128

N_MLA_LAYERS = (DEPTH_2 + 2) // 3
N_SB_LAYERS = (DEPTH_2 + 1) // 3
N_RET_LAYERS = DEPTH_2 // 3


def rms_norm_2(x, g):
    xf = x.astype(jnp.float32)
    y = xf * lax.rsqrt(jnp.mean(xf * xf, axis=-1, keepdims=True) + EPS)
    return (y * g.astype(jnp.float32)).astype(x.dtype)

def modulate_2(x, shift, scale):
    return x * (1.0 + scale[:, None, :]) + shift[:, None, :]

def rope_tables(positions, dim):
    inv_freq = ROPE_BASE ** (-jnp.arange(0, dim, 2, dtype=jnp.float32) / dim)
    ang = positions.astype(jnp.float32)[..., None] * inv_freq
    return jnp.cos(ang)[:, :, None, :], jnp.sin(ang)[:, :, None, :]

def apply_rope(t, cos, sin):
    t1, t2 = jnp.split(t, 2, axis=-1)
    cos = cos.astype(t.dtype)
    sin = sin.astype(t.dtype)
    return jnp.concatenate([t1 * cos - t2 * sin, t2 * cos + t1 * sin], axis=-1)

def to_blocks(t, size):
    b, s, h, d = t.shape
    return t.reshape(b, s // size, size, h, d).transpose(1, 0, 2, 3, 4)

def from_blocks(t):
    nb, b, size, h, d = t.shape
    return t.transpose(1, 0, 2, 3, 4).reshape(b, nb * size, h, d)

def blocked_causal_softmax(q, k, v, scale):
    k_pos = jnp.arange(k.shape[1])
    qb = to_blocks(q, Q_BLOCK)

    def one_block(args):
        q_blk, b_idx = args
        q_pos = b_idx * Q_BLOCK + jnp.arange(Q_BLOCK)
        s = jnp.einsum('bqhd,bkhd->bhqk', q_blk, k).astype(jnp.float32) * scale
        s = jnp.where(k_pos[None, :] <= q_pos[:, None], s, NEG_INF)
        p = jax.nn.softmax(s, axis=-1).astype(v.dtype)
        return jnp.einsum('bhqk,bkhd->bqhd', p, v)

    o = lax.map(one_block, (qb, jnp.arange(qb.shape[0])))
    return from_blocks(o)

def mla_mixer(h, positions, w_in, q_norm, kv_norm, w_q_up, w_kv_up, w_out):
    b, s, _ = h.shape
    q_lat, kv_lat, k_pe = jnp.split(h @ w_in, [MLA_Q_RANK, MLA_Q_RANK + MLA_KV_RANK], axis=-1)
    cos, sin = rope_tables(positions, MLA_ROPE)
    q = (rms_norm_2(q_lat, q_norm) @ w_q_up).reshape(b, s, MLA_HEADS, MLA_NOPE + MLA_ROPE)
    q_nope, q_pe = jnp.split(q, [MLA_NOPE], axis=-1)
    q = jnp.concatenate([q_nope, apply_rope(q_pe, cos, sin)], axis=-1)
    kv = (rms_norm_2(kv_lat, kv_norm) @ w_kv_up).reshape(b, s, MLA_HEADS, MLA_NOPE + MLA_V)
    k_nope, v = jnp.split(kv, [MLA_NOPE], axis=-1)
    k_pe = apply_rope(k_pe[:, :, None, :], cos, sin)
    k = jnp.concatenate([k_nope, jnp.broadcast_to(k_pe, (b, s, MLA_HEADS, MLA_ROPE))], axis=-1)
    o = blocked_causal_softmax(q, k, v, (MLA_NOPE + MLA_ROPE) ** -0.5)
    return o.reshape(b, s, MLA_HEADS * MLA_V) @ w_out

def stick_breaking_mixer(h, w_in, w_out):
    b, s, _ = h.shape
    q, k, v = jnp.split(h @ w_in, 3, axis=-1)
    q = q.reshape(b, s, SB_HEADS, SB_HEAD_DIM)
    k = k.reshape(b, s, SB_HEADS, SB_HEAD_DIM)
    v = v.reshape(b, s, SB_HEADS, SB_HEAD_DIM)
    scale = SB_HEAD_DIM ** -0.5
    k_pos = jnp.arange(s)
    qb = to_blocks(q, Q_BLOCK)

    def one_block(args):
        q_blk, b_idx = args
        q_pos = b_idx * Q_BLOCK + jnp.arange(Q_BLOCK)
        z = jnp.einsum('bqhd,bkhd->bhqk', q_blk, k).astype(jnp.float32) * scale
        strict = k_pos[None, :] < q_pos[:, None]
        log_1m = jnp.where(strict, jax.nn.log_sigmoid(-z), 0.0)
        suffix = lax.cumsum(log_1m, axis=3, reverse=True) - log_1m
        a = jnp.where(strict, jnp.exp(jax.nn.log_sigmoid(z) + suffix), 0.0).astype(v.dtype)
        return jnp.einsum('bhqk,bkhd->bqhd', a, v)

    o = from_blocks(lax.map(one_block, (qb, jnp.arange(qb.shape[0]))))
    return o.reshape(b, s, SB_HEADS * SB_HEAD_DIM) @ w_out

def retention_mixer(h, positions, w_in, gn_g, w_out):
    b, s, _ = h.shape
    hk = RET_HEADS * RET_KEY_DIM
    hv = RET_HEADS * RET_VAL_DIM
    q, k, v, g = jnp.split(h @ w_in, [hk, 2 * hk, 2 * hk + hv], axis=-1)
    cos, sin = rope_tables(positions, RET_KEY_DIM)
    q = apply_rope(q.reshape(b, s, RET_HEADS, RET_KEY_DIM), cos, sin).astype(jnp.float32)
    k = apply_rope(k.reshape(b, s, RET_HEADS, RET_KEY_DIM), cos, sin).astype(jnp.float32) * (RET_KEY_DIM ** -0.5)
    v = v.reshape(b, s, RET_HEADS, RET_VAL_DIM).astype(jnp.float32)

    log_gamma = jnp.log(1.0 - 2.0 ** (-5.0 - jnp.arange(RET_HEADS, dtype=jnp.float32)))
    idx = jnp.arange(RET_CHUNK, dtype=jnp.float32)
    diff = idx[:, None] - idx[None, :]
    decay = jnp.where(diff[None] >= 0, jnp.exp(jnp.maximum(diff, 0.0)[None] * log_gamma[:, None, None]), 0.0)
    xi = jnp.exp((idx[:, None] + 1.0) * log_gamma[None, :])
    zeta = jnp.exp((RET_CHUNK - 1.0 - idx)[:, None] * log_gamma[None, :])
    g_chunk = jnp.exp(RET_CHUNK * log_gamma)

    def step(state, inp):
        qc, kc, vc = inp
        sc = jnp.einsum('bihd,bjhd->bhij', qc, kc) * decay[None]
        inner = jnp.einsum('bhij,bjhv->bihv', sc, vc)
        cross = jnp.einsum('bihd,bhdv->bihv', qc, state) * xi[None, :, :, None]
        state = state * g_chunk[None, :, None, None] + jnp.einsum('bjhd,bjhv->bhdv', kc * zeta[None, :, :, None], vc)
        return state, inner + cross

    state0 = jnp.zeros((b, RET_HEADS, RET_KEY_DIM, RET_VAL_DIM), jnp.float32)
    _, o = lax.scan(step, state0, (to_blocks(q, RET_CHUNK), to_blocks(k, RET_CHUNK), to_blocks(v, RET_CHUNK)))
    o = from_blocks(o)
    o = o * lax.rsqrt(jnp.mean(o * o, axis=-1, keepdims=True) + EPS)
    o = o.reshape(b, s, hv) * gn_g.astype(jnp.float32)
    o = (jax.nn.silu(g.astype(jnp.float32)) * o).astype(h.dtype)
    return o @ w_out

def second_inputs(seed: int = 0) -> dict:
    key = jax.random.key(seed)
    ks = jax.random.split(key, 24)

    def dense(k, shape, fan_in, gain=1.0):
        return jax.random.normal(k, shape, jnp.float32) * (gain * fan_in ** -0.5)

    def gains(k, shape):
        return 1.0 + 0.05 * jax.random.normal(k, shape, jnp.float32)

    hk = RET_HEADS * RET_KEY_DIM
    hv = RET_HEADS * RET_VAL_DIM
    return {
        "x": jax.random.normal(ks[0], (BATCH, SEQ, D_MODEL), jnp.float32),
        "c": jax.random.normal(ks[1], (BATCH, D_MODEL), jnp.float32),
        "positions": jnp.broadcast_to(jnp.arange(SEQ, dtype=jnp.int32), (BATCH, SEQ)),
        "ada_w": dense(ks[2], (DEPTH_2, D_MODEL, 6 * D_MODEL), D_MODEL, 0.5),
        "ada_b": 0.01 * jax.random.normal(ks[3], (DEPTH_2, 6 * D_MODEL), jnp.float32),
        "norm_g": gains(ks[4], (DEPTH_2, 4, D_MODEL)),
        "ffn_w1": dense(ks[5], (DEPTH_2, D_MODEL, D_FF), D_MODEL),
        "ffn_w2": dense(ks[6], (DEPTH_2, D_FF, D_MODEL), D_FF),
        "mla_w_in": dense(ks[7], (N_MLA_LAYERS, D_MODEL, MLA_Q_RANK + MLA_KV_RANK + MLA_ROPE), D_MODEL),
        "mla_q_norm": gains(ks[8], (N_MLA_LAYERS, MLA_Q_RANK)),
        "mla_kv_norm": gains(ks[9], (N_MLA_LAYERS, MLA_KV_RANK)),
        "mla_w_q_up": dense(ks[10], (N_MLA_LAYERS, MLA_Q_RANK, MLA_HEADS * (MLA_NOPE + MLA_ROPE)), MLA_Q_RANK),
        "mla_w_kv_up": dense(ks[11], (N_MLA_LAYERS, MLA_KV_RANK, MLA_HEADS * (MLA_NOPE + MLA_V)), MLA_KV_RANK),
        "mla_w_out": dense(ks[12], (N_MLA_LAYERS, MLA_HEADS * MLA_V, D_MODEL), MLA_HEADS * MLA_V),
        "sb_w_in": dense(ks[13], (N_SB_LAYERS, D_MODEL, 3 * SB_HEADS * SB_HEAD_DIM), D_MODEL),
        "sb_w_out": dense(ks[14], (N_SB_LAYERS, SB_HEADS * SB_HEAD_DIM, D_MODEL), SB_HEADS * SB_HEAD_DIM),
        "ret_w_in": dense(ks[15], (N_RET_LAYERS, D_MODEL, 2 * hk + 2 * hv), D_MODEL),
        "ret_gn_g": gains(ks[16], (N_RET_LAYERS, hv)),
        "ret_w_out": dense(ks[17], (N_RET_LAYERS, hv, D_MODEL), hv),
    }

def second_block(x, c, positions, ada_w, ada_b, norm_g, ffn_w1, ffn_w2,
              mla_w_in, mla_q_norm, mla_kv_norm, mla_w_q_up, mla_w_kv_up, mla_w_out,
              sb_w_in, sb_w_out, ret_w_in, ret_gn_g, ret_w_out):
    cond = jax.nn.silu(c)
    for i in range(DEPTH_2):
        mod = cond @ ada_w[i] + ada_b[i]
        sh_a, sc_a, g_a, sh_f, sc_f, g_f = jnp.split(mod, 6, axis=-1)

        h = modulate_2(rms_norm_2(x, norm_g[i, 0]), sh_a, sc_a)
        kind, j = i % N_MIXERS, i // N_MIXERS
        if kind == 0:
            y = mla_mixer(h, positions, mla_w_in[j], mla_q_norm[j], mla_kv_norm[j],
                          mla_w_q_up[j], mla_w_kv_up[j], mla_w_out[j])
        elif kind == 1:
            y = stick_breaking_mixer(h, sb_w_in[j], sb_w_out[j])
        else:
            y = retention_mixer(h, positions, ret_w_in[j], ret_gn_g[j], ret_w_out[j])
        x = x + g_a[:, None, :] * rms_norm_2(y, norm_g[i, 1])

        h = modulate_2(rms_norm_2(x, norm_g[i, 2]), sh_f, sc_f)
        y = jnp.square(jax.nn.relu(h @ ffn_w1[i])) @ ffn_w2[i]
        x = x + g_f[:, None, :] * rms_norm_2(y, norm_g[i, 3])
    return x


def setup_inputs(seed=0):
    out = dict(first_inputs(seed))
    for name, value in second_inputs(seed + 1).items():
        if name != "x":
            out[name + "_2"] = value
    return out


def reference(
    x, c, ctx, c_ctx, w_ada, b_ada, g_mix, g_ffn, w_in_ab, conv_a, conv_b, conv_b_bias, ln_b_g,
    ln_b_b, w_out_ab, w_in_cd, g_q, g_k, lam_q1, lam_k1, lam_q2, lam_k2, g_subln, conv_d, hf_w1,
    hf_b1, hf_freq, hf_w2, hf_b2, hf_w3, hf_bias, w_out_cd, w_router, w_gate, w_up, w_down, c_2,
    positions_2, ada_w_2, ada_b_2, norm_g_2, ffn_w1_2, ffn_w2_2, mla_w_in_2, mla_q_norm_2,
    mla_kv_norm_2, mla_w_q_up_2, mla_w_kv_up_2, mla_w_out_2, sb_w_in_2, sb_w_out_2, ret_w_in_2,
    ret_gn_g_2, ret_w_out_2,
):
    x = first_block(
        x, c, ctx, c_ctx, w_ada, b_ada, g_mix, g_ffn, w_in_ab, conv_a, conv_b, conv_b_bias,
        ln_b_g, ln_b_b, w_out_ab, w_in_cd, g_q, g_k, lam_q1, lam_k1, lam_q2, lam_k2, g_subln,
        conv_d, hf_w1, hf_b1, hf_freq, hf_w2, hf_b2, hf_w3, hf_bias, w_out_cd, w_router, w_gate,
        w_up, w_down,
    )
    return second_block(
        x, c_2, positions_2, ada_w_2, ada_b_2, norm_g_2, ffn_w1_2, ffn_w2_2, mla_w_in_2,
        mla_q_norm_2, mla_kv_norm_2, mla_w_q_up_2, mla_w_kv_up_2, mla_w_out_2, sb_w_in_2,
        sb_w_out_2, ret_w_in_2, ret_gn_g_2, ret_w_out_2,
    )


_drawn_inputs = setup_inputs


def setup_inputs(seed=0):
    import zlib

    import numpy as np

    out = dict(_drawn_inputs(seed))
    spreads = {}
    factors = {'conv_b_bias': 7.072,
     'ln_b_g': 2.911,
     'ln_b_b': 8.0,
     'g_q': 5.385,
     'g_k': 6.194,
     'lam_q2': 8.0,
     'lam_k2': 6.723,
     'g_subln': 3.47,
     'hf_b1': 3.829,
     'hf_freq': 5.315,
     'hf_b2': 2.871,
     'mla_q_norm_2': 8.0,
     'mla_kv_norm_2': 2.779,
     'ret_gn_g_2': 4.836}
    for name, (base, spread) in spreads.items():
        noise = np.random.default_rng([zlib.crc32(name.encode()), seed]).standard_normal(out[name].shape)
        drawn = base * np.exp(spread * noise) if base else spread * noise
        out[name] = jnp.asarray(drawn.astype(out[name].dtype))
    for name, factor in factors.items():
        out[name] = (out[name] * factor).astype(out[name].dtype)
    return out
```

```python
import math
from contextlib import ExitStack

import numpy as np

import concourse.bass as bass
from concourse import mybir

F32 = mybir.dt.float32
BF16 = mybir.dt.bfloat16
I32 = mybir.dt.int32
ALU = mybir.AluOpType
ACT = mybir.ActivationFunctionType
AX = mybir.AxisListType

P = 128
D = 1024
KC = D // P
N = 256
TC = N // P
E = 16
CAP = 32
RING = 6
SLOT = 4096
FF = 4096
EPS = 1e-6
SUBLN_EPS = 1e-5
LAM_INIT = 0.8 - 0.6 * math.exp(-0.3)
NEG = -1e30
TWO_PI = 2.0 * math.pi
ROUND = 12582912.0
PI_A = 6.28125
PI_B = float(np.float32(np.float64(TWO_PI) - PI_A).view(np.uint32) & np.uint32(0xFFFFF000))
PI_B = float(np.array([int(PI_B)], np.uint32).view(np.float32)[0])
PI_C = float(np.float32(np.float64(TWO_PI) - PI_A - PI_B))
PI_SAFE = 3.1415925


def shape_constants():
    f = np.float32
    ident = np.eye(P, dtype=f)
    iota = np.tile(np.arange(CAP, dtype=f), (P, 1))
    row = np.arange(P)
    inv_mla = (10000.0 ** (-np.arange(0, 64, 2, dtype=f) / f(64))).astype(f)
    inv_ret = (10000.0 ** (-np.arange(0, 256, 2, dtype=f) / f(256))).astype(f)
    invf = np.stack([inv_mla[row % 32], inv_ret[row]], axis=1)
    base = np.concatenate([ident, iota, invf], axis=1)

    t = np.arange(N)
    before = np.stack([(t[None, :] < (tc * P + row)[:, None]) for tc in range(TC)], axis=1).astype(f)

    theta = TWO_PI * (np.arange(N) + 0.5) / (2 * N)
    fwd = np.concatenate([np.cos(np.outer(t, theta)), -np.sin(np.outer(t, theta))], axis=1)
    fwd = fwd.reshape(TC, P, 2 * N).transpose(1, 0, 2)
    m = t + N // 2
    inv = np.concatenate([np.cos(np.outer(theta, m)), -np.sin(np.outer(theta, m))], axis=0) / N
    inv = inv.reshape(4, P, N).transpose(1, 0, 2)
    bands = np.linspace(1e-4, 15, 16).astype(f)
    ang = (f(TWO_PI / N) * t.astype(f)[:, None] * bands[None]).astype(f)
    z = np.concatenate([np.linspace(0, 1, N).astype(f)[:, None], np.cos(ang), -np.sin(ang)], axis=1)
    zt = np.zeros((P, N), f)
    zt[:33] = z.T
    dist = np.abs(t - N // 2) / (N // 2)
    rates = np.abs(np.linspace(math.log(1e-2) / 1.5, math.log(1e-2) / 0.3, 512))
    decay = np.exp(-dist[:, None] * rates[None]).reshape(TC, P, 512).transpose(1, 0, 2)
    hyena = np.concatenate([fwd.reshape(P, -1), inv.reshape(P, -1), decay.reshape(P, -1), zt], axis=1)

    inv16 = (10000.0 ** (-np.arange(16, dtype=f) / f(16))).astype(f)
    feat = row % 64
    pos = np.where((feat < 32)[:, None], (t // 64)[None], (t % 64)[None]).astype(f)
    a = (pos * inv16[feat % 16][:, None]).astype(f)
    swap = np.zeros((P, P), f)
    for r in range(P):
        if r % 32 < 16:
            swap[r + 16, r] = -1.0
        else:
            swap[r - 16, r] = 1.0
    half = (row[:, None] // 64 == row[None] // 64).astype(f)
    axial = np.concatenate([np.cos(a), np.sin(a), swap, half], axis=1)

    mswap = np.zeros((P, 64), f)
    for r in range(64):
        if r < 32:
            mswap[r + 32, r] = -1.0
        else:
            mswap[r - 32, r] = 1.0
    causal = np.stack([np.where(t[None] <= (qc * P + row)[:, None], 0.0, NEG) for qc in range(TC)], axis=1)
    mla = np.concatenate([mswap, causal.reshape(P, -1)], axis=1)

    q_all, q_late = np.arange(N), np.arange(P, N)
    strict = np.concatenate([np.where(row[:, None] < q_all[None], 0.0, NEG),
                             np.where((row + P)[:, None] < q_late[None], 0.0, NEG)], axis=1)
    suffix = (row[:, None] >= row[None]).astype(f)
    stick = np.concatenate([strict, suffix], axis=1)

    gam = np.log(f(1.0) - f(2.0) ** (f(-5.0) - np.arange(4, dtype=f))).astype(f)
    ret = []
    for h in range(4):
        for keys, qs in ((row, q_all), (row + P, q_late)):
            diff = (qs[None] - keys[:, None]).astype(np.float64)
            ret.append(np.where(diff >= 0, np.exp(np.maximum(diff, 0) * gam[h]), 0.0) / 16.0)
    ret = np.concatenate(ret, axis=1)
    return {
        "k_base": base, "k_before": before.reshape(P, -1), "k_hyena": hyena, "k_axial": axial,
        "k_mla": mla, "k_stick": stick, "k_ret": ret,
    }


CONST_WIDTH = {"k_base": 162, "k_before": 512, "k_hyena": 3328, "k_axial": 768, "k_mla": 576,
               "k_stick": 512, "k_ret": 1536}
_PARAMS = [
    "x", "c", "ctx", "c_ctx", "w_ada", "b_ada", "g_mix", "g_ffn", "w_in_ab", "conv_a", "conv_b",
    "conv_b_bias", "ln_b_g", "ln_b_b", "w_out_ab", "w_in_cd", "g_q", "g_k", "lam_q1", "lam_k1",
    "lam_q2", "lam_k2", "g_subln", "conv_d", "hf_w1", "hf_b1", "hf_freq", "hf_w2", "hf_b2", "hf_w3",
    "hf_bias", "w_out_cd", "w_router", "w_gate", "w_up", "w_down", "c_2", "positions_2", "ada_w_2",
    "ada_b_2", "norm_g_2", "ffn_w1_2", "ffn_w2_2", "mla_w_in_2", "mla_q_norm_2", "mla_kv_norm_2",
    "mla_w_q_up_2", "mla_w_kv_up_2", "mla_w_out_2", "sb_w_in_2", "sb_w_out_2", "ret_w_in_2",
    "ret_gn_g_2", "ret_w_out_2",
]


class Mark:

    def __init__(self, sem, at, step=0):
        self.sem, self.at, self.step = sem, at, step

    def wait(self, eng, it=0):
        eng.wait_ge(self.sem, self.at + it * self.step if self.step else self.at)


class Fill:

    def __init__(self, bank, full, free, before, step):
        self.bank, self.before, self.step = bank, before, step
        self.full, self.free = Mark(full, before + 1, step), Mark(free, before + 1, step)

    def open(self, pe, it=0):
        if self.step:
            pe.wait_ge(self.free.sem, self.before + it * self.step)
        elif self.before:
            pe.wait_ge(self.free.sem, self.before)


class Unit:

    def __init__(self, slot, landed, before, step, width, src):
        self.slot, self.width, self.src = slot, width, src
        self.landed = Mark(landed, 16 * (before + 1), 16 * step)
        self.used = None


def block_program(nc, a, out, LAST=8):
    with ExitStack() as ctx:
        def sb(name, shape, dt=F32):
            return ctx.enter_context(nc.sbuf_tensor(name, shape, dt))

        def sem(name):
            return ctx.enter_context(nc.semaphore(name))

        ring = sb("ring", [P, RING, SLOT])
        hT = sb("hT", [P, KC, 2 * N])
        arena = sb("arena", [P, 22528])
        PS = ctx.enter_context(nc.psum_tensor("banks", [P, 8, 512], F32))
        base = sb("base", [P, CONST_WIDTH["k_base"]])
        ident, iota, invf = base[:, 0:P], base[:, P:P + CAP], base[:, P + CAP:P + CAP + 2]
        ones = sb("ones", [P, P])
        zeros_bf = sb("zeros_bf", [P, P], BF16)

        VEC = {}
        vec_rows = []

        def vec(name, view, rows, width=P, at=0):
            if name not in VEC:
                VEC[name] = (vec.n, rows)
                vec.n += rows
            vec_rows.append((VEC[name][0], view, rows, width, at))
        vec.n = 0
        r128 = lambda ap: ap.rearrange("a (k p) -> (a k) p", p=P)
        vec("c", r128(a["c"]), 8)
        vec("c_ctx", r128(a["c_ctx"]), 8)
        vec("c_2", r128(a["c_2"]), 8)
        vec("b_ada", r128(a["b_ada"]), 96)
        vec("ada_b_2", r128(a["ada_b_2"]), 192)
        vec("g_mix", r128(a["g_mix"]), 16)
        vec("g_ffn", r128(a["g_ffn"]), 16)
        vec("norm_g", a["norm_g_2"].rearrange("l n (k p) -> (l n k) p", p=P), 128)
        vec("conv_a", a["conv_a"].rearrange("a j (k p) -> (a j k) p", p=P), 12)
        vec("conv_b", a["conv_b"].rearrange("a j (k p) -> (a j k) p", p=P), 124)
        vec("conv_d", a["conv_d"].rearrange("a j (k p) -> (a j k) p", p=P), 36)
        for nm, n in (("conv_b_bias", 4), ("ln_b_g", 4), ("ln_b_b", 4), ("hf_bias", 4), ("g_subln", 1),
                      ("mla_q_norm_2", 4), ("mla_kv_norm_2", 2), ("ret_gn_g_2", 16)):
            vec(nm, r128(a[nm]), n)
        for nm in ("g_q", "g_k"):
            vec(nm, a[nm], 1, 64, 0)
            vec(nm, a[nm], 1, 64, 64)
        for nm in ("hf_b1", "hf_freq", "hf_b2", "lam_q1", "lam_k1", "lam_q2", "lam_k2"):
            vec(nm, a[nm], 1, 64)
        NV = vec.n
        NVR = -(-NV // P)
        V = sb("V", [P, NV])
        MOD = sb("MOD", [P, 2 * 96 + 4 * 48])
        AM = sb("AM", [P, 2 * 32 + 4 * 16])
        GP = sb("GP", [P, 4, 2, KC])
        cond2 = sb("cond2", [P, KC, 32])
        small = sb("small", [P, 24])
        stat8 = sb("stat8", [P, 64])

        def col(name, i=0):
            return V[:, VEC[name][0] + i:VEC[name][0] + i + 1]

        def cols(name, i, n):
            return V[:, VEC[name][0] + i:VEC[name][0] + i + n]

        def mod(layer, part, k, s=0):
            if layer < 2:
                i = layer * 96 + (part * KC + k) * 2 + s
            else:
                i = 192 + (layer - 2) * 48 + part * KC + k
            return MOD[:, i:i + 1]

        def gain(layer, which, k, s=0):
            if layer < 2:
                i = layer * 32 + which * 16 + k * 2 + s
            else:
                i = 64 + (layer - 2) * 16 + which * 8 + k
            return AM[:, i:i + 1]

        def region(at, shape, dt=None):
            n = int(np.prod(shape))
            v = arena[:, at:at + n]
            if len(shape) == 1:
                return v
            names = "abcdef"[:len(shape)]
            dims = {names[i]: shape[i] for i in range(1, len(shape))}
            return v.rearrange(f"p ({' '.join(names)}) -> p {' '.join(names)}", **dims)

        uT = region(0, [KC, 2 * N])
        W = 4096
        SQ = region(18432 + 2560, [2, 512])
        RS = region(18432 + 3584, [512])

        bank_full = [sem(f"bank_full{b}") for b in range(8)]
        bank_free = [sem(f"bank_free{b}") for b in range(8)]
        landed = [sem(f"landed{s}") for s in range(RING)]
        sems = {}

        def S(name):
            if name not in sems:
                sems[name] = sem(name)
            return sems[name]

        bank_uses = [0] * 8
        slot_uses = [0] * RING
        plan = {}
        stream = []

        def fills(name, banks, rounds=1):
            per = {b: banks.count(b) for b in set(banks)}
            seen = {b: 0 for b in per}
            got = []
            for b in banks:
                got.append(Fill(b, bank_full[b], bank_free[b], bank_uses[b] + seen[b],
                                per[b] if rounds > 1 else 0))
                seen[b] += 1
            for b in per:
                bank_uses[b] += per[b] * rounds
            plan[name] = got
            return got

        def load(slots, sources, rounds=1, looped=True):
            per = {s: slots.count(s) for s in set(slots)}
            seen = {s: 0 for s in per}
            got = []
            for s, (width, src) in zip(slots, sources):
                got.append(Unit(s, landed[s], slot_uses[s] + seen[s], per[s] if rounds > 1 else 0, width, src))
                seen[s] += 1
            for s in per:
                slot_uses[s] += per[s] * rounds
            stream.append((rounds, looped, got))
            return got

        cursor = [0]

        def turn(n):
            got = [(cursor[0] + i) % RING for i in range(n)]
            cursor[0] = (cursor[0] + n) % RING
            return got

        def col_units(w, n0, n1, width=512, k=KC):
            v = w.rearrange("(k p) n -> p k n", p=P)
            return [(k * width, (lambda it, j=j: v[:, :, j:j + width])) for j in range(n0, n1, width)]

        def wview(u, k):
            return ring[:, u.slot, 0:u.width].rearrange("p (k n) -> p k n", k=k)

        ada_w = [a["w_ada"][0], a["w_ada"][1]] + [a["ada_w_2"][i] for i in range(4)]
        ADA_ROUNDS = {0: 2, 1: 2, 2: 2}
        ada_units = {}
        fills("setup", ([0, 1, 2, 3] * 3)[:8 + -(-NVR // 4)])
        fills("lam", [0])
        adaP = {}
        for which, layers in (("first", (0, 1)), ("second", (2,))):
            rounds = 2 * len(layers)
            f_rows = fills(f"ada_{which}_rows", [0, 1] * 3, rounds)
            f_cols = fills(f"ada_{which}_cols", [2, 3] * 3, rounds)
            slots = turn(6)
            v = [ada_w[l].rearrange("(k p) n -> p k n", p=P) for l in layers]
            src = [(SLOT, (lambda it, j=j, v=v: v[it // 2][:, :, (it % 2) * 3072 + j * 512:(it % 2) * 3072 + (j + 1) * 512]))
                   for j in range(6)]
            us = load(slots, src, rounds, looped=False)
            for u, f in zip(us, f_rows):
                u.used = f.full
            adaP[which] = (us, f_rows, f_cols, rounds)

        def plan_norm(name):
            fills(name, [7])

        def plan_moe(l, ns):
            p = f"moe{l}_"
            plan_norm(p + "norm")
            fills(p + "logit", [0])
            fills(p + "affT", [1])
            fills(p + "utok", [2, 3, 4, 5] * ns)
            fills(p + "gather", [0, 1, 2, 3] * 2 * ns)
            fills(p + "selT", [4, 5] * ns)
            slots = turn(6)
            units = []
            for j in range(4):
                gsrc = [(SLOT, (lambda it, j=j, w=w, h=h: w.rearrange("e (k p) n -> p e k n", p=P)
                                [:, it * 4 + j, :, h * 512:(h + 1) * 512]))
                        for w in (a["w_gate"][l], a["w_up"][l]) for h in range(2)]
                dsrc = [(SLOT, (lambda it, j=j, r=r: a["w_down"][l].rearrange("e (r k p) n -> p e r k n", p=P, k=4)
                                [:, it * 4 + j, r])) for r in range(2)]
                units += gsrc + dsrc
            us = load([slots[i % 6] for i in range(24)], units, 4)
            fs = fills(p + "experts", [0, 1, 2, 3, 4, 5, 6, 7] * 2, 4)
            for j in range(4):
                g, u, t, d = fs[4 * j:4 * j + 4]
                for i, f in enumerate((g, g, u, u, d, d)):
                    us[6 * j + i].used = f.full
            plan[p + "units"] = us
            fills(p + "combine", [0, 1, 2, 3] * 2 * ns)

        def use_dense(name, units, per_unit, banks):
            fs = fills(name, banks)
            for i, u in enumerate(units):
                u.used = fs[per_unit * (i + 1) - 1].full
            plan[name + "_units"] = units

        if LAST >= 1:
            plan_norm("ab_norm")
            w_ab = a["w_in_ab"][0]
            AB_ORDER = (3, 4, 1, 2, 0)
            use_dense("ab_in", load(turn(5), [col_units(w_ab, j * 512, (j + 1) * 512)[0] for j in AB_ORDER]),
                      4, [0, 1, 2, 3] * 5)
            fills("ab_mean", [4])
            fills("ab_var", [5])
            use_dense("ab_out", load(turn(2), col_units(a["w_out_ab"][0], 0, D)), 4, [0, 1, 2, 3] * 2)
        if LAST >= 2:
            plan_moe(0, 2)

        if LAST >= 3:
            plan_norm("cd_norm")
            fills("hf_mlp", [0, 1])
            fills("hf_tok", [2, 3])
            fills("hf_freq", [0, 1, 2, 3])
            w_cd = a["w_in_cd"][0]
            hy_cols = (2048, 2560, 1536)
            use_dense("hy_in", load(turn(3), [col_units(w_cd, c, c + 512)[0] for c in hy_cols]), 4, [0, 1, 2, 3] * 3)
            fills("hy_utok", [4, 5])
            fills("hy_ufreq", [0, 1, 2, 3])
            fills("hy_out", [4, 5] * 2)
            use_dense("qk_in", load(turn(2), col_units(w_cd, 0, 1024)), 4, [0, 1, 2, 3] * 2)
            use_dense("v_in", load(turn(1), col_units(w_cd, 1024, 1536)), 4, [4, 5, 6, 7])
            fills("qk_ms", [0, 1, 2, 3] * 2)
            fills("qk_rot", [4, 5, 6, 7] * 2)
            fills("da_scores", [0, 1, 2, 3] * 4)
            fills("da_turn", [4, 5] * 4)
            fills("da_out", [6, 7] * 2)
            fills("da_sub", [4, 5] * 2)
            use_dense("cd_out", load(turn(2), col_units(a["w_out_cd"][0], 0, D)), 4, [0, 1, 2, 3] * 2)
        if LAST >= 4:
            plan_moe(1, 1)

        KINDS = ("mla", "stick", "ret", "mla")
        for i, kind in enumerate(KINDS[:max(0, LAST - 4)]):
            p = f"b{i}_"
            plan_norm(p + "norm")
            if kind == "mla":
                j = i // 3
                win = a["mla_w_in_2"][j].rearrange("(k p) n -> p k n", p=P)
                wq = a["mla_w_q_up_2"][j].rearrange("(k p) n -> p k n", p=P)
                wkv = a["mla_w_kv_up_2"][j].rearrange("(k p) n -> p k n", p=P)
                us = load(turn(3), [(KC * 448, lambda it, v=win: v), (2 * 1536, lambda it, v=wq: v),
                                    (2048, lambda it, v=wkv: v)])
                f = fills(p + "lat", [0, 1, 2, 3])
                us[0].used = f[-1].full
                fills(p + "ms", [4, 5])
                fills(p + "kper", [6])
                f = fills(p + "qup", [0, 1, 2, 3] * 4)
                us[1].used = f[-1].full
                fills(p + "qrot", [4, 5] * 2)
                f = fills(p + "kvup", [0, 1, 2, 3] * 3)
                us[2].used = f[-1].full
                plan[p + "units"] = us
                fills(p + "scores", [0, 1] * 8)
                fills(p + "turn", [2, 3] * 8)
                fills(p + "pv", [4, 5] * 4)
                use_dense(p + "out", load(turn(2), col_units(a["mla_w_out_2"][j], 0, D)), 4, [0, 1, 2, 3] * 2)
            elif kind == "stick":
                w = a["sb_w_in_2"][0]
                use_dense(p + "qk", load(turn(4), col_units(w, 0, 2048)), 4, [0, 1, 2, 3] * 4)
                use_dense(p + "v", load(turn(2), col_units(w, 2048, 3072)), 2, [4, 5] * 2)
                fills(p + "z", [0, 1] * 8)
                fills(p + "suf", [2, 3] * 8)
                fills(p + "pv", [4, 5] * 4)
                use_dense(p + "out", load(turn(2), col_units(a["sb_w_out_2"][0], 0, D)), 4, [0, 1, 2, 3] * 2)
            else:
                w = a["ret_w_in_2"][0]
                use_dense(p + "qk", load(turn(4), col_units(w, 0, 2048)), 4, [0, 1, 2, 3] * 4)
                use_dense(p + "v", load(turn(4), col_units(w, 2048, 4096)), 2, [4, 5] * 4)
                use_dense(p + "g", load(turn(4), col_units(w, 4096, 6144)), 4, [0, 1, 2, 3] * 4)
                fills(p + "s", [4, 5] * 2)
                fills(p + "pv", [0, 1, 2, 3] * 4)
                fills(p + "ms", [6, 7] * 2)
                use_dense(p + "out", load(turn(4), col_units(a["ret_w_out_2"][0], 0, D, 256, 16)), 2,
                          [0, 1, 2, 3] * 2)
            plan_norm(p + "post")
            plan_norm(p + "fnorm")
            more = i < 3
            c0 = cursor[0]
            s = [(c0 + q) % RING for q in range(RING)]
            w1 = a["ffn_w1_2"][i].rearrange("(k p) n -> p k n", p=P)
            w2 = a["ffn_w2_2"][i].rearrange("(g k p) n -> p g k n", p=P, k=4)
            f1 = lambda g: (SLOT, lambda it, v=w1, g=g: v[:, :, bass.ds(it * 1024 + g * 512, 512)])
            f2 = lambda g: (SLOT, lambda it, v=w2, g=g: v[:, it * 2 + g])
            items, slots = [f1(0), f1(1), f2(0), f2(1)], [s[0], s[2], s[1], s[3]]
            if more:
                wa = ada_w[i + 3].rearrange("(k p) n -> p k n", p=P)
                fa = lambda q: (SLOT, lambda it, v=wa, q=q: v[:, :, bass.ds(it * 1536 + q * 512, 512)])
                items = [f1(0), fa(0), f1(1), fa(1), f2(0), fa(2), f2(1)]
                slots = [s[0], s[4], s[2], s[5], s[1], s[4], s[3]]
            us = load(slots, items, 4)
            fu = fills(p + "up", [0, 1] * 4, 4)
            if more:
                fr = fills(p + "ada_rows", [2] * 3, 4)
                fc = fills(p + "ada_cols", [3] * 3, 4)
                w1u, w2u, au = [us[0], us[2]], [us[4], us[6]], [us[1], us[3], us[5]]
                for u, f in zip(au, fr):
                    u.used = f.full
                plan[p + "ada_units"] = au
            else:
                w1u, w2u = us[0:2], us[2:4]
            w1u[0].used, w1u[1].used = fu[3].full, fu[7].full
            for g in range(2):
                w2u[g].used = Mark(S("ffn_down_used"), 8 * i + g + 1, 2)
            plan[p + "w1"], plan[p + "w2"] = w1u, w2u
            fills(p + "down", [4, 5, 6, 7])
            plan_norm(p + "fpost")
        fills("final", [0, 1, 2, 3])

        aff_dram = [nc.dram_tensor(f"aff_scratch{l}", (2, E, N), F32, kind="Internal").ap() for l in range(2)]

        x_tok = region(W, [2, TC, D])
        v_rows = region(W + 4096, [NVR, P])
        cond1 = region(W + 8192, [KC, 32])
        ada_rows = region(W + 12288, [3, 512])
        ffn_h = region(W, [2, 4, N])
        y_T = region(W + 2048, [KC, N])
        out_tok = region(W, [TC, D])

        vec_copies = []
        for r0, view, rows, width, at in vec_rows:
            i = 0
            while i < rows:
                n = min(rows - i, P - (r0 + i) % P)
                ch_, r = (r0 + i) // P, (r0 + i) % P
                vec_copies.append((v_rows[r:r + n, ch_, at:at + width], view[i:i + n, :]))
                i += n
        vec_dmas = len(vec_copies)
        one_col = ones[:, 0:1]
        zero_row = zeros_bf[:, :].unsqueeze(1).to_broadcast([P, 4, P])

        def counters():
            return {"sq": 0, "rs": 0, "u": 0, "t": 0, "sq_hist": [], "used": 0, "n": {}}

        def stat_act(act, c, chunks, fill, width, rows=P):
            for i, (src, ready) in enumerate(chunks):
                if ready is not None:
                    ready.wait(act)
                k = c["sq"]
                if k >= 2:
                    c["sq_hist"][k - 2].wait(act)
                nc.scalar.activation(SQ[:, k % 2, 0:width], src, ACT.Square).then_inc(S("sq_ready"), 1)
                c["sq"] += 1
                if i < len(chunks) - 1:
                    c["used"] += 1
                    c["sq_hist"].append(Mark(S("sq_used"), c["used"]))
                else:
                    c["sq_hist"].append(fill.full)

        def stat_pe(pe, c, n, fill, width, lhs=None):
            fill.open(pe)
            for i in range(n):
                k = c["sq"]
                pe.wait_ge(S("sq_ready"), k + 1)
                mm = nc.tensor.matmul(PS[:, fill.bank, 0:width], (ones[:, :] if lhs is None else lhs),
                                      SQ[:, k % 2, 0:width], start=(i == 0), stop=(i == n - 1))
                mm.then_inc(S("sq_used") if i < n - 1 else fill.full.sem, 1)
                c["sq"] += 1

        def rsqrt_act(act, c, fill, width, count, eps_at=0, dst=None):
            dst = RS if dst is None else dst
            fill.full.wait(act)
            nc.scalar.activation(dst[:, 0:width], PS[:, fill.bank, 0:width], ACT.Ln, scale=1.0 / count,
                                 bias=small[:, 9 + eps_at:10 + eps_at]).then_inc(fill.free.sem, 1)
            fill.free.wait(act)
            nc.scalar.activation(dst[:, 0:width], dst[:, 0:width], ACT.Exp, scale=-0.5).then_inc(S("rs_ready"), 1)

        def rsqrt_wait(dve, c):
            c["rs"] += 1
            dve.wait_ge(S("rs_ready"), c["rs"])

        def scale_dve(dve, c, layer, which, ns):
            for k in range(KC):
                for s in range(ns):
                    t = slice(s * N, (s + 1) * N)
                    nc.vector.scalar_tensor_tensor(uT[:, k, t], hT[:, k, t], gain(layer, which, k, s), RS[:, t],
                                                   ALU.mult, ALU.mult).then_inc(S("u_scaled"), 1)

        def shift_act(act, c, layer, which, ns):
            for k in range(KC):
                for s in range(ns):
                    t = slice(s * N, (s + 1) * N)
                    c["u"] += 1
                    act.wait_ge(S("u_scaled"), c["u"])
                    nc.scalar.activation(uT[:, k, t], uT[:, k, t], ACT.Identity,
                                         bias=mod(layer, 3 * which, k, s)).then_inc(S("u_ready"), 1)

        def u_ready(pe, c, ns):
            c["u"] += KC * ns
            pe.wait_ge(S("u_ready"), c["u"])

        def norm_act(act, c, name, layer, which, ns, first=None):
            width = ns * N
            stat_act(act, c, [(hT[:, k, 0:width], first if k == 0 else None) for k in range(KC)],
                     plan[name][0], width)
            rsqrt_act(act, c, plan[name][0], width, D)
            shift_act(act, c, layer, which, ns)

        def norm_pe(pe, c, name, ns):
            stat_pe(pe, c, KC, plan[name][0], ns * N)
            u_ready(pe, c, ns)

        def norm_dve(dve, c, name, layer, which, ns):
            rsqrt_wait(dve, c)
            scale_dve(dve, c, layer, which, ns)

        def dense_pe(pe, name, rhs, width, per_unit, k=KC, ready=None):
            units, fs = plan[name + "_units"], plan[name]
            for i, u in enumerate(units):
                w = wview(u, k)
                u.landed.wait(pe)
                for m in range(per_unit):
                    f = fs[i * per_unit + m]
                    f.open(pe)
                    for q in range(k):
                        mm = nc.tensor.matmul(PS[:, f.bank, 0:width], w[:, q, m * P:(m + 1) * P], rhs(i, q),
                                              start=(q == 0), stop=(q == k - 1))
                    mm.then_inc(f.full.sem, 1)

        def token_pe(pe, name, tchunks):
            units, fs = plan[name + "_units"], plan[name]
            for i, u in enumerate(units):
                w = wview(u, KC)
                u.landed.wait(pe)
                for t in range(tchunks):
                    f = fs[i * tchunks + t]
                    f.open(pe)
                    for q in range(KC):
                        mm = nc.tensor.matmul(PS[:, f.bank, :], uT[:, q, t * P:(t + 1) * P], w[:, q, :],
                                              start=(q == 0), stop=(q == KC - 1))
                    mm.then_inc(f.full.sem, 1)

        def copy_act(act, f, dst, src):
            f.full.wait(act)
            nc.scalar.copy(dst, src).then_inc(f.free.sem, 1)

        class Chain:

            def __init__(self, eng, sem_):
                self.eng, self.sem, self.n = eng, sem_, 0

            def put(self, ins):
                ins.then_inc(self.sem, 1)
                self.n += 1
                return self.n

            def sync(self, back=0):
                if self.n - back > 0:
                    self.eng.wait_ge(self.sem, self.n - back)

            def do(self, ins):
                self.put(ins)
                self.sync()

        def residual_dve(ch, name, layer, part, ns, width=N, s_of=None):
            for m, f in enumerate(plan[name]):
                f.full.wait(ch.eng)
                for s in range(ns):
                    t = slice(s * N, (s + 1) * N)
                    ins = nc.vector.scalar_tensor_tensor(hT[:, m, t], PS[:, f.bank, t], mod(layer, part, m, s),
                                                         hT[:, m, t], ALU.mult, ALU.add)
                    if s == ns - 1:
                        ins.then_inc(f.free.sem, 1)

        block = ctx.enter_context(nc.Block())

        ab_z = region(W, [4, 512])
        ab_gin = region(W + 2048, [4, 512])
        ab_val = region(W + 4096, [4, 512])
        ab_gout = region(W + 6144, [4, 512])
        ab_gv = region(W + 8192, [4, 2, N + 2])
        ab_zin = region(W + 10256, [4, 2, N + 30])
        ab_sg = region(W + 12544, [2, 512])
        ab_mu = region(W + 13568, [512])
        v512 = lambda ap: ap.rearrange("p (s t) -> p s t", s=2)

        moe_utok = region(4096, [4, D])
        moe_xe = region(8192, [KC, E, 2, CAP])
        moe_aall = region(8192, [2, E, N])
        moe_y = region(0, [2, 4, D])
        moe_selT = region(16384, [2, 4, N])
        moe_sel = region(18432, [4, E, CAP])
        moe_selw = region(20480, [4, E, CAP])
        moe_before = region(16384, [2, N])
        moe_junk = region(16896, [2, N])
        moe_wr = region(17408, [KC, E])
        moe_affT = region(17536, [P])
        moe_e, moe_aff, moe_rank = (region(17664 + 64 * i, [4, E]) for i in range(3))
        moe_c1, moe_c2 = (region(17856 + 64 * i, [64]) for i in range(2))
        moe_mx, moe_sm = (region(17984 + 4 * i, [4]) for i in range(2))
        x_cur = region(18432, [2, KC, 2 * CAP])
        x_sil = region(19456, [2, 512])
        x_act = region(20480, [2, 512])
        x_actT = region(21504, [2, 4, P])

        hy_const = region(W, [3328])
        hy_fwd = hy_const[:, 0:1024].rearrange("p (t f) -> p t f", t=TC)
        hy_inv = hy_const[:, 1024:2048].rearrange("p (q t) -> p q t", q=4)
        hy_decay = hy_const[:, 2048:3072].rearrange("p (t c) -> p t c", t=TC)
        hy_zt = hy_const[:, 3072:3328]
        hf_w1, hf_w2, hf_w3 = region(W + 3328, [64]), region(W + 3392, [64]), region(W + 3456, [512])
        hf_x, hf_k = region(W + 3968, [N]), region(W + 4224, [N])
        hf_tok = region(W + 4736, [TC, 512])
        hf_F = region(W + 5760, [4, 512])
        hy_p = region(W + 7808, [12, N + 2])
        hy_z = region(W + 10904, [12, N])
        hy_utok = region(W + 13976, [TC, 512])
        hy_Y = region(W + 7808, [4, 512])
        hy_t = region(W + 9856, [2, 512])
        hy_y = region(W + 15200, [4, N])

        da_const = region(W, [768])
        da_cos, da_sin = da_const[:, 0:N], da_const[:, N:2 * N]
        da_swap, da_half = da_const[:, 512:640], da_const[:, 640:768]
        da_qk = region(W + 768, [8, 512])
        da_v = region(W + 4864, [4, 512])
        da_sq = region(W + 6912, [8, 512])
        da_rs = region(W + 11008, [8, 512])
        da_p = region(W + 6912, [2, 2, 512])
        da_aT = region(W + 8960, [2, 4, N])
        da_o = region(W + 11008, [4, N])
        da_a = region(W + 12032, [2, 512])
        da_rso = region(W + 13056, [4, N])

        yv = y_T
        rope_tab = region(W + 15872, [4, N])
        rope_x, rope_k = region(W + 4096, [N]), region(W + 4352, [N])
        pos_i = region(W + 4608, [N]).bitcast(I32)
        pos_f = region(W + 4864, [N])
        ml_const = region(W, [576])
        ml_swap = ml_const[:, 0:64]
        ml_causal = ml_const[:, 64:576].rearrange("p (q k) -> p q k", q=TC)
        ml_s = region(W + 576, [2, N])
        ml_pT = region(W + 1088, [2, 2, N])
        ml_qlat = region(W + 4096, [2, N])
        ml_kvlat = region(W + 4608, [N])
        ml_kpe, ml_kt = region(W + 4864, [N]), region(W + 5120, [N])
        ml_qn = region(W + 5376, [8, N])
        ml_qpe = region(W + 7424, [8, N])
        ml_qt = region(W + 9472, [8, N])
        ml_kn = region(W + 11520, [8, N])
        ml_v = region(W + 13568, [2, D])
        ml_o = region(W + 9472, [8, N])
        st_const = region(W, [512])
        st_mask, st_suffix = st_const[:, 0:384], st_const[:, 384:512]
        st_qk = region(W + 4096, [16, N])
        st_v = region(W + 8192, [2, D])
        st_t, st_sp = region(W + 10240, [4, 384]), region(W + 11776, [4, 384])
        st_o = region(W + 13312, [8, N])
        rt_decay = region(W, [4, 384])
        rt_g = region(W + 1536, [16, N])
        rt_qk = region(W + 5632, [16, N])
        rt_v = region(W + 9728, [2, 2048])
        rt_s = region(W + 13824, [4, 384])
        rt_rs = region(W + 13824, [4, N])
        rt_t = region(W + 15360, [2, N])
        rt_o = region(W + 5632, [16, N])
        n_mla = {0: 0, 3: 1}
        mla_scale = (128 + 64) ** -0.5

        @block.sync
        def _(sp):
            users = {}

            def send(u, it, waits):
                for w, at in waits:
                    w.wait(sp, at)
                shape = u.src(it)
                dst = ring[:, u.slot, 0:u.width]
                if len(shape.shape) == 3:
                    dst = dst.rearrange("p (k n) -> p k n", k=shape.shape[1])
                sp.dma_start(dst, shape).then_inc(u.landed.sem, 16)

            for rounds, looped, units in stream:
                for u in units:
                    w = users.get(u.slot)
                    send(u, 0, [w] if w else [])
                    users[u.slot] = (u.used, 0)
                if rounds > 1:
                    before = []
                    last = {}
                    for i, u in enumerate(units):
                        before.append(last.get(u.slot))
                        last[u.slot] = u

                    def later(it):
                        for u, b in zip(units, before):
                            send(u, it, [(b.used, it) if b is not None else (last[u.slot].used, it - 1)])

                    if looped:
                        with sp.Fori(1, rounds) as it:
                            later(it)
                    else:
                        for it in range(1, rounds):
                            later(it)
                    for s, u in last.items():
                        users[s] = (u.used, rounds - 1)
            sp.wait_ge(S("out_ready"), TC)
            for t in range(TC):
                sp.dma_start(out.rearrange("b (t p) d -> p (b t) d", p=P)[:, t, :], out_tok[:, t, :])\
                    .then_inc(S("out_sent"), 16)
            sp.wait_ge(S("out_sent"), 16 * TC)

        @block.tensor
        def _(pe):
            c = counters()

            def ada_rows_pe(u, f, cond, it):
                w = wview(u, KC)
                u.landed.wait(pe, it)
                f.open(pe, it)
                for k in range(KC):
                    g = 32 * (k % 4)
                    mm = nc.tensor.matmul(PS[g:g + 32, f.bank, :], cond[:, k, :], w[:, k, :],
                                          start=(k < 4), stop=(k >= 4), skip_group_check=True)
                mm.then_inc(f.full.sem, 1)

            def ada_cols_pe(rows, f, buf, it):
                rows.free.wait(pe, it)
                f.open(pe, it)
                for q in range(4):
                    mm = nc.tensor.transpose(PS[:, f.bank, q * P:(q + 1) * P], ada_rows[:, buf, q * P:(q + 1) * P],
                                             ident)
                mm.then_inc(f.full.sem, 1)

            pe.wait_ge(S("in_landed"), 48)
            fs = plan["setup"]
            i = 0
            for s in range(2):
                for t in range(TC):
                    for kq in range(2):
                        f = fs[i]
                        f.open(pe)
                        for q in range(4):
                            mm = nc.tensor.transpose(PS[:, f.bank, q * P:(q + 1) * P],
                                                     x_tok[:, s, t, (4 * kq + q) * P:(4 * kq + q + 1) * P], ident)
                        mm.then_inc(f.full.sem, 1)
                        i += 1
            pe.wait_ge(S("vec_landed"), 16 * vec_dmas)
            for j in range(0, NVR, 4):
                f = fs[i]
                f.open(pe)
                for q in range(min(4, NVR - j)):
                    mm = nc.tensor.transpose(PS[:, f.bank, q * P:(q + 1) * P], v_rows[:, j + q, :], ident)
                mm.then_inc(f.full.sem, 1)
                i += 1
            f = plan["lam"][0]
            pe.wait_ge(S("lam_prod"), 1)
            pe.wait_ge(S("cleared"), 6)
            f.open(pe)
            nc.tensor.matmul(PS[:, f.bank, 0:2], ones[:, :], small[:, 0:2], start=True, stop=True)\
                .then_inc(f.full.sem, 1)
            pe.wait_ge(S("cond_ready"), 3)
            for which, cond in (("first", cond1), ("second", cond2)):
                us, fr, fc, rounds = adaP[which]
                with pe.Fori(0, rounds) as it:
                    for j in range(6):
                        ada_rows_pe(us[j], fr[j], cond, it)
                        if j >= 1:
                            ada_cols_pe(fr[j - 1], fc[j - 1], (j - 1) % 3, it)
                    ada_cols_pe(fr[5], fc[5], 2, it)

            def moe_pe(l, ns):
                p = f"moe{l}_"
                norm_pe(pe, c, p + "norm", ns)
                pe.wait_ge(S("moe_const"), 32 * (l + 1))
                f = plan[p + "logit"][0]
                f.open(pe)
                for t in range(2 * ns):
                    for k in range(KC):
                        mm = nc.tensor.matmul(PS[:, f.bank, t * E:(t + 1) * E], uT[:, k, t * P:(t + 1) * P],
                                              moe_wr[:, k, :], start=(k == 0), stop=(k == KC - 1))
                mm.then_inc(f.full.sem, 1)
                for i, f in enumerate(plan[p + "utok"]):
                    t, kq = i // 2, i % 2
                    f.open(pe)
                    for q in range(4):
                        mm = nc.tensor.transpose(PS[:, f.bank, q * P:(q + 1) * P],
                                                 uT[:, 4 * kq + q, t * P:(t + 1) * P], ident)
                    mm.then_inc(f.full.sem, 1)
                f = plan[p + "affT"][0]
                pe.wait_ge(S("moe_aff"), l + 1)
                f.open(pe)
                nc.tensor.transpose(PS[0:2 * ns * E, f.bank, 0:P],
                                    moe_aff[:, 0:2 * ns, :].rearrange("p t e -> p (t e)"), ident)\
                    .then_inc(f.full.sem, 1)
                pe.wait_ge(S("moe_sel"), (4 if l else 0) + 2 * ns)
                for f in plan[p + "utok"][-4:]:
                    f.free.wait(pe)
                for s in range(ns):
                    for k in range(KC):
                        f = plan[p + "gather"][s * KC + k]
                        f.open(pe)
                        for t in range(TC):
                            mm = nc.tensor.matmul(PS[:, f.bank, :], moe_utok[:, TC * s + t, k * P:(k + 1) * P],
                                                  moe_sel[:, TC * s + t].rearrange("p e c -> p (e c)"),
                                                  start=(t == 0), stop=(t == TC - 1))
                        mm.then_inc(f.full.sem, 1)
                pe.wait_ge(S("moe_selw"), (4 if l else 0) + 2 * ns)
                for t, f in enumerate(plan[p + "selT"]):
                    f.open(pe)
                    w = moe_selw[:, t].rearrange("p e c -> p (e c)")
                    for q in range(4):
                        mm = nc.tensor.transpose(PS[:, f.bank, q * P:(q + 1) * P], w[:, q * P:(q + 1) * P], ident)
                    mm.then_inc(f.full.sem, 1)
                us, fs = plan[p + "units"], plan[p + "experts"]
                with pe.Fori(0, 4) as it:
                    for j in range(4):
                        b = j % 2
                        fg, fu, ft, fd = fs[4 * j:4 * j + 4]
                        un = us[6 * j:6 * j + 6]
                        pe.wait_ge(S("x_cur"), 16 * l + j + 1 + it * 4)
                        for f, h0 in ((fg, 0), (fu, 2)):
                            f.open(pe, it)
                            un[h0].landed.wait(pe, it)
                            un[h0 + 1].landed.wait(pe, it)
                            for k in range(KC):
                                for h in range(2):
                                    mm = nc.tensor.matmul(PS[64 * h:64 * h + 64, f.bank, :], x_cur[:, b, k, :],
                                                          wview(un[h0 + h], KC)[:, k, :], start=(k == 0),
                                                          stop=(k == KC - 1), skip_group_check=True)
                            mm.then_inc(f.full.sem, 1)
                        fu.free.wait(pe, it)
                        ft.open(pe, it)
                        for q in range(4):
                            mm = nc.tensor.transpose(PS[:, ft.bank, q * P:(q + 1) * P],
                                                     x_act[:, b, q * P:(q + 1) * P], ident)
                        mm.then_inc(ft.full.sem, 1)
                        fd.open(pe, it)
                        un[4].landed.wait(pe, it)
                        un[5].landed.wait(pe, it)
                        ft.free.wait(pe, it)
                        for fc in range(8):
                            for h in range(2):
                                mm = nc.tensor.matmul(
                                    PS[64 * h:64 * h + 64, fd.bank, :],
                                    x_actT[:, b, fc % 4, (fc // 4) * 64:(fc // 4) * 64 + 64],
                                    wview(un[4 + fc // 4], 4)[:, fc % 4, h * 512:(h + 1) * 512],
                                    start=(fc == 0), stop=(fc == 7), skip_group_check=True)
                        mm.then_inc(fd.full.sem, 1)
                for f in plan[p + "selT"]:
                    f.free.wait(pe)
                for j in range(4):
                    fs[4 * j + 3].free.wait(pe, 3)
                for i, f in enumerate(plan[p + "combine"]):
                    s, m = i // KC, i % KC
                    f.open(pe)
                    for q in range(4):
                        mm = nc.tensor.matmul(PS[:, f.bank, 0:N], moe_y[:, s, q, m * P:(m + 1) * P],
                                              moe_selT[:, s, q, :], start=(q == 0), stop=(q == 3))
                    mm.then_inc(f.full.sem, 1)

            if LAST >= 1:
                norm_pe(pe, c, "ab_norm", 2)
                dense_pe(pe, "ab_in", lambda i, q: uT[:, q, :], 512, 4)
                f = plan["ab_mean"][0]
                f.open(pe)
                for m in range(4):
                    pe.wait_ge(S("z_conv"), m + 1)
                    mm = nc.tensor.matmul(PS[:, f.bank, :], ones[:, :], ab_z[:, m, :], start=(m == 0), stop=(m == 3))
                mm.then_inc(f.full.sem, 1)
                stat_pe(pe, c, 4, plan["ab_var"][0], 512)
                pe.wait_ge(S("ya_ready"), 4)
                pe.wait_ge(S("yb_ready"), 4)
                dense_pe(pe, "ab_out", lambda i, q: ab_gin[:, q, :] if q < 4 else ab_z[:, q - 4, :], 512, 4)
            if LAST >= 2:
                moe_pe(0, 2)
            if LAST >= 3:
                pe.wait_ge(S("hy_const"), 64)
                for r in range(2):
                    f = plan["hf_mlp"][r]
                    f.open(pe)
                    if r == 0:
                        mm = nc.tensor.matmul(PS[0:64, f.bank, 0:N], hf_w1[0:33, :], hy_zt[0:33, :], start=True, stop=True)
                    else:
                        pe.wait_ge(S("hf_sin"), 1)
                        mm = nc.tensor.matmul(PS[0:64, f.bank, 0:N], hf_w2[0:64, :], hf_x[0:64, :], start=True, stop=True)
                    mm.then_inc(f.full.sem, 1)
                pe.wait_ge(S("hf_sin"), 2)
                for t in range(TC):
                    f = plan["hf_tok"][t]
                    f.open(pe)
                    nc.tensor.matmul(PS[:, f.bank, :], hf_x[0:64, t * P:(t + 1) * P], hf_w3[0:64, :],
                                     start=True, stop=True).then_inc(f.full.sem, 1)
                for f in plan["hf_tok"]:
                    f.free.wait(pe)

                def forward(fill_list, src):
                    for q, f in enumerate(fill_list):
                        f.open(pe)
                        for t in range(TC):
                            mm = nc.tensor.matmul(PS[:, f.bank, :], hy_fwd[:, t, q * P:(q + 1) * P], src[:, t, :],
                                                  start=(t == 0), stop=(t == TC - 1))
                        mm.then_inc(f.full.sem, 1)

                forward(plan["hf_freq"], hf_tok)
                norm_pe(pe, c, "cd_norm", 2)
                dense_pe(pe, "hy_in", lambda i, q: uT[:, q, 0:N], N, 4)
                pe.wait_ge(S("hy_u"), 4)
                for t, f in enumerate(plan["hy_utok"]):
                    f.open(pe)
                    for m in range(4):
                        mm = nc.tensor.transpose(PS[:, f.bank, m * P:(m + 1) * P], hy_z[:, m, t * P:(t + 1) * P], ident)
                    mm.then_inc(f.full.sem, 1)
                for f in plan["hy_utok"]:
                    f.free.wait(pe)
                forward(plan["hy_ufreq"], hy_utok)
                pe.wait_ge(S("hy_Y"), 4)
                for m, f in enumerate(plan["hy_out"]):
                    f.open(pe)
                    for q in range(4):
                        mm = nc.tensor.matmul(PS[:, f.bank, 0:N], hy_Y[:, q, m * P:(m + 1) * P], hy_inv[:, q, :],
                                              start=(q == 0), stop=(q == 3))
                    mm.then_inc(f.full.sem, 1)
                units, fs = plan["qk_in_units"], plan["qk_in"]
                for i, u in enumerate(units):
                    w, width = wview(u, KC), (N, 2 * N)[i]
                    u.landed.wait(pe)
                    for m in range(4):
                        f = fs[4 * i + m]
                        f.open(pe)
                        for q in range(KC):
                            mm = nc.tensor.matmul(PS[:, f.bank, 0:width], w[:, q, m * P:(m + 1) * P],
                                                  uT[:, q, 0:width], start=(q == 0), stop=(q == KC - 1))
                        mm.then_inc(f.full.sem, 1)
                token_pe(pe, "v_in", 4)
                pe.wait_ge(S("da_const"), 16)
                for i, f in enumerate(plan["qk_ms"]):
                    width = N if i < 4 else 2 * N
                    pe.wait_ge(S("qk_sq"), i + 1)
                    f.open(pe)
                    nc.tensor.matmul(PS[:, f.bank, 0:width], da_half, da_sq[:, i, 0:width], start=True, stop=True)\
                        .then_inc(f.full.sem, 1)
                for i, f in enumerate(plan["qk_rot"]):
                    pe.wait_ge(S("qk_n"), i + 1)
                    f.open(pe)
                    nc.tensor.matmul(PS[:, f.bank, 0:N], da_swap, da_qk[:, i, 0:N], start=True, stop=True)\
                        .then_inc(f.full.sem, 1)

                def scores(i):
                    h, qc = i // TC, i % TC
                    for j in range(2):
                        f = plan["da_scores"][2 * i + j]
                        f.open(pe)
                        r = slice(64 * j, 64 * j + 64)
                        nc.tensor.matmul(PS[:, f.bank, :], da_qk[r, h, qc * P:(qc + 1) * P], da_qk[r, 4 + h, :],
                                         start=True, stop=True).then_inc(f.full.sem, 1)

                def turn_probs(i):
                    f = plan["da_turn"][i]
                    pe.wait_ge(S("da_a"), i + 1)
                    f.open(pe)
                    for kc in range(4):
                        mm = nc.tensor.transpose(PS[:, f.bank, kc * P:(kc + 1) * P],
                                                 da_a[:, i % 2, kc * P:(kc + 1) * P], ident)
                    mm.then_inc(f.full.sem, 1)

                def out_head(h):
                    plan["da_turn"][2 * h].free.wait(pe)
                    plan["da_turn"][2 * h + 1].free.wait(pe)
                    f = plan["da_out"][h]
                    f.open(pe)
                    for kc in range(4):
                        mm = nc.tensor.matmul(PS[:, f.bank, 0:N], da_v[:, kc, h * P:(h + 1) * P],
                                              da_aT[:, h % 2, kc, :], start=(kc == 0), stop=(kc == 3))
                    mm.then_inc(f.full.sem, 1)

                pe.wait_ge(S("qk_rope"), 8)
                for f in plan["v_in"]:
                    f.free.wait(pe)
                scores(0)
                for i in range(8):
                    if i < 7:
                        scores(i + 1)
                    turn_probs(i)
                    if i % 2:
                        out_head(i // 2)
                for h in range(4):
                    stat_pe(pe, c, 1, plan["da_sub"][h], N)
                pe.wait_ge(S("da_o"), 4)
                pe.wait_ge(S("hy_y"), 4)
                dense_pe(pe, "cd_out", lambda i, q: da_o[:, q, :] if q < 4 else hy_y[:, q - 4, :], N, 4)
            if LAST >= 4:
                moe_pe(1, 1)

            def mla_pe(i):
                p, j = f"b{i}_", n_mla[i]
                us = plan[p + "units"]
                norm_pe(pe, c, p + "norm", 1)
                w = wview(us[0], KC)
                us[0].landed.wait(pe)
                for m, f in enumerate(plan[p + "lat"]):
                    rows = P if m < 3 else 64
                    f.open(pe)
                    for q in range(KC):
                        mm = nc.tensor.matmul(PS[0:rows, f.bank, 0:N], w[:, q, m * P:m * P + rows], uT[:, q, 0:N],
                                              start=(q == 0), stop=(q == KC - 1))
                    mm.then_inc(f.full.sem, 1)
                stat_pe(pe, c, 2, plan[p + "ms"][0], N)
                stat_pe(pe, c, 1, plan[p + "ms"][1], N)
                f = plan[p + "kper"][0]
                pe.wait_ge(S("ml_const"), 16 * (j + 1))
                plan[p + "lat"][3].free.wait(pe)
                f.open(pe)
                nc.tensor.matmul(PS[0:64, f.bank, 0:N], ml_swap[0:64, :], ml_kpe[0:64, :], start=True, stop=True)\
                    .then_inc(f.full.sem, 1)
                w = wview(us[1], 2)
                us[1].landed.wait(pe)
                plan[p + "lat"][0].free.wait(pe)
                plan[p + "lat"][1].free.wait(pe)
                for h in range(8):
                    for part, (o, rows) in enumerate(((0, P), (P, 64))):
                        f = plan[p + "qup"][2 * h + part]
                        f.open(pe)
                        for q in range(2):
                            mm = nc.tensor.matmul(PS[0:rows, f.bank, 0:N], w[:, q, h * 192 + o:h * 192 + o + rows],
                                                  ml_qlat[:, q, :], start=(q == 0), stop=(q == 1))
                        mm.then_inc(f.full.sem, 1)
                wkv = ring[:, us[2].slot, 0:2048].rearrange("p (h two e) -> p h two e", h=8, two=2)
                us[2].landed.wait(pe)
                plan[p + "lat"][2].free.wait(pe)
                for m, f in enumerate(plan[p + "kvup"]):
                    f.open(pe)
                    if m < 8:
                        mm = nc.tensor.matmul(PS[:, f.bank, 0:N], wkv[:, m, 0, :], ml_kvlat, start=True, stop=True)
                    else:
                        t, half = (m - 8) // 2, (m - 8) % 2
                        mm = nc.tensor.matmul(PS[:, f.bank, :], ml_kvlat[:, t * P:(t + 1) * P],
                                              wkv[:, 4 * half:4 * half + 4, 1, :], start=True, stop=True)
                    mm.then_inc(f.full.sem, 1)
                for r, f in enumerate(plan[p + "qrot"]):
                    plan[p + "qup"][4 * r + 1].free.wait(pe)
                    plan[p + "qup"][4 * r + 3].free.wait(pe)
                    f.open(pe)
                    nc.tensor.matmul(PS[0:64, f.bank, :], ml_swap[0:64, :],
                                     ml_qpe[0:64, 2 * r:2 * r + 2, :].rearrange("p h t -> p (h t)"),
                                     start=True, stop=True).then_inc(f.full.sem, 1)
                pe.wait_ge(S("ml_rope"), 5 * (j + 1))
                for f in plan[p + "kvup"][-4:] + plan[p + "qup"][-4:]:
                    f.free.wait(pe)

                def scores(i2):
                    h, qc = i2 // 2, i2 % 2
                    f = plan[p + "scores"][i2]
                    width = (qc + 1) * P
                    f.open(pe)
                    nc.tensor.matmul(PS[:, f.bank, 0:width], ml_qn[:, h, qc * P:(qc + 1) * P], ml_kn[:, h, 0:width],
                                     start=True, stop=False)
                    nc.tensor.matmul(PS[:, f.bank, 0:width], ml_qpe[0:64, h, qc * P:(qc + 1) * P],
                                     ml_kpe[0:64, 0:width], start=False, stop=True).then_inc(f.full.sem, 1)

                scores(0)
                for i2 in range(16):
                    h, qc = i2 // 2, i2 % 2
                    if i2 < 15:
                        scores(i2 + 1)
                    f = plan[p + "turn"][i2]
                    pe.wait_ge(S("ml_p"), 16 * j + i2 + 1)
                    f.open(pe)
                    for kc in range(qc + 1):
                        mm = nc.tensor.transpose(PS[:, f.bank, kc * P:(kc + 1) * P],
                                                 ml_s[:, i2 % 2, kc * P:(kc + 1) * P], ident)
                    mm.then_inc(f.full.sem, 1)
                    if qc == 1:
                        if h == 0:
                            pe.wait_ge(S("pT_zero"), j + 1)
                        plan[p + "turn"][i2 - 1].free.wait(pe)
                        plan[p + "turn"][i2].free.wait(pe)
                        f = plan[p + "pv"][h]
                        f.open(pe)
                        for kc in range(2):
                            mm = nc.tensor.matmul(PS[:, f.bank, 0:N], ml_v[:, kc, h * P:(h + 1) * P],
                                                  ml_pT[:, h % 2, kc, :], start=(kc == 0), stop=(kc == 1))
                        mm.then_inc(f.full.sem, 1)
                for f in plan[p + "pv"][-2:]:
                    f.free.wait(pe)
                dense_pe(pe, p + "out", lambda i, q: ml_o[:, q, :], N, 4)

            def stick_pe(i):
                p = f"b{i}_"
                norm_pe(pe, c, p + "norm", 1)
                dense_pe(pe, p + "qk", lambda i, q: uT[:, q, 0:N], N, 4)
                token_pe(pe, p + "v", TC)
                pe.wait_ge(S("st_const"), 16)
                for f in plan[p + "qk"][-4:] + plan[p + "v"][-2:]:
                    f.free.wait(pe)
                for s in range(16 + 3):
                    if s < 16:
                        h, r = s // 2, slice(64 * (s % 2), 64 * (s % 2) + 64)
                        f = plan[p + "z"][s]
                        f.open(pe)
                        nc.tensor.matmul(PS[:, f.bank, 0:N], st_qk[r, 8 + h, 0:P], st_qk[r, h, :], start=True, stop=True)
                        nc.tensor.matmul(PS[:, f.bank, N:384], st_qk[r, 8 + h, P:N], st_qk[r, h, P:N],
                                         start=True, stop=True).then_inc(f.full.sem, 1)
                    if 1 <= s <= 16:
                        k = s - 1
                        f = plan[p + "suf"][k]
                        pe.wait_ge(S("st_sp"), k + 1)
                        f.open(pe)
                        nc.tensor.matmul(PS[:, f.bank, 0:N], st_suffix, st_sp[:, k % 4, 0:N], start=True, stop=False)
                        nc.tensor.matmul(PS[:, f.bank, P:N], ones[:, :], st_sp[:, k % 4, N:384], start=False,
                                         stop=True)
                        nc.tensor.matmul(PS[:, f.bank, N:384], st_suffix, st_sp[:, k % 4, N:384], start=True,
                                         stop=True).then_inc(f.full.sem, 1)
                    if s >= 3:
                        k = s - 3
                        f = plan[p + "pv"][k // 2]
                        o = 64 * (k % 2)
                        pe.wait_ge(S("st_a"), k + 1)
                        if k % 2 == 0:
                            f.open(pe)
                        nc.tensor.matmul(PS[o:o + 64, f.bank, 0:N], st_v[:, 0, k * 64:k * 64 + 64],
                                         st_t[:, k % 4, 0:N], start=True, stop=False, skip_group_check=True)
                        nc.tensor.matmul(PS[o:o + 64, f.bank, P:N], st_v[:, 1, k * 64:k * 64 + 64],
                                         st_t[:, k % 4, N:384], start=False, stop=True, skip_group_check=True)\
                            .then_inc(f.full.sem if k % 2 else S("st_pv"), 1)
                for f in plan[p + "pv"][-2:]:
                    f.free.wait(pe)
                dense_pe(pe, p + "out", lambda i, q: st_o[:, q, :], N, 4)

            def ret_pe(i):
                p = f"b{i}_"
                norm_pe(pe, c, p + "norm", 1)
                dense_pe(pe, p + "qk", lambda i, q: uT[:, q, 0:N], N, 4)
                token_pe(pe, p + "v", TC)
                dense_pe(pe, p + "g", lambda i, q: uT[:, q, 0:N], N, 4)
                pe.wait_ge(S("rt_rope"), 8)
                for h in range(4):
                    f = plan[p + "s"][h]
                    f.open(pe)
                    for q in range(2):
                        nc.tensor.matmul(PS[:, f.bank, 0:N], rt_qk[:, 8 + 2 * h + q, 0:P], rt_qk[:, 2 * h + q, :],
                                         start=(q == 0), stop=(q == 1))
                    for q in range(2):
                        mm = nc.tensor.matmul(PS[:, f.bank, N:384], rt_qk[:, 8 + 2 * h + q, P:N],
                                              rt_qk[:, 2 * h + q, P:N], start=(q == 0), stop=(q == 1))
                    mm.then_inc(f.full.sem, 1)
                for f in plan[p + "v"][-2:]:
                    f.free.wait(pe)
                for h in range(4):
                    plan[p + "s"][h].free.wait(pe)
                    for vc in range(4):
                        f = plan[p + "pv"][4 * h + vc]
                        e = slice(h * 512 + vc * P, h * 512 + (vc + 1) * P)
                        f.open(pe)
                        nc.tensor.matmul(PS[:, f.bank, 0:N], rt_v[:, 0, e], rt_s[:, h, 0:N], start=True, stop=False)
                        nc.tensor.matmul(PS[:, f.bank, P:N], rt_v[:, 1, e], rt_s[:, h, N:384], start=False, stop=True)\
                            .then_inc(f.full.sem, 1)
                for h in range(4):
                    stat_pe(pe, c, 4, plan[p + "ms"][h], N)
                pe.wait_ge(S("rt_o"), 16)
                dense_pe(pe, p + "out", lambda i, q: rt_o[:, q, :], N, 2, k=16)

            def ffn_pe(i):
                p = f"b{i}_"
                norm_pe(pe, c, p + "fnorm", 1)
                down = plan[p + "down"]
                for f in down:
                    f.open(pe)
                    nc.tensor.matmul(PS[:, f.bank, :], zeros_bf[:, :], zero_row, start=True, stop=False,
                                     skip_group_check=True)
                fu, w1, w2 = plan[p + "up"], plan[p + "w1"], plan[p + "w2"]
                more = i < 3
                with pe.Fori(0, 4) as it:
                    def up(g):
                        w1[g].landed.wait(pe, it)
                        w = wview(w1[g], KC)
                        for m in range(4):
                            f = fu[4 * g + m]
                            f.open(pe, it)
                            for q in range(KC):
                                mm = nc.tensor.matmul(PS[:, f.bank, 0:N], w[:, q, m * P:(m + 1) * P], uT[:, q, 0:N],
                                                      start=(q == 0), stop=(q == KC - 1))
                            mm.then_inc(f.full.sem, 1)

                    def down_part(g):
                        w2[g].landed.wait(pe, it)
                        w = wview(w2[g], 4)
                        pe.wait_ge(S("ffn_squared"), 32 * i + 4 * g + 4 + it * 8)
                        for q in range(4):
                            for m in range(KC):
                                mm = nc.tensor.matmul(PS[:, down[m // 2].bank, (m % 2) * N:(m % 2) * N + N],
                                                      w[:, q, m * P:(m + 1) * P], ffn_h[:, g, q, :],
                                                      start=False, stop=False, skip_group_check=True)
                        mm.then_inc(S("ffn_down_used"), 1)

                    def rows(q):
                        if more:
                            ada_rows_pe(plan[p + "ada_units"][q], plan[p + "ada_rows"][q], cond2, it)

                    def turn_rows(q):
                        if more:
                            ada_cols_pe(plan[p + "ada_rows"][q], plan[p + "ada_cols"][q], q, it)

                    up(0)
                    rows(0)
                    up(1)
                    turn_rows(0)
                    rows(1)
                    down_part(0)
                    turn_rows(1)
                    rows(2)
                    down_part(1)
                    turn_rows(2)
                for f in down:
                    nc.tensor.matmul(PS[:, f.bank, :], zeros_bf[:, :], zero_row, start=False, stop=True,
                                     skip_group_check=True).then_inc(f.full.sem, 1)

            for i, kind in enumerate(KINDS[:max(0, LAST - 4)]):
                {"mla": mla_pe, "stick": stick_pe, "ret": ret_pe}[kind](i)
                stat_pe(pe, c, KC, plan[f"b{i}_post"][0], N)
                ffn_pe(i)
                stat_pe(pe, c, KC, plan[f"b{i}_fpost"][0], N)
            pe.wait_ge(S("h_final"), 1)
            for i, f in enumerate(plan["final"]):
                t, kq = i // 2, i % 2
                f.open(pe)
                for q in range(4):
                    mm = nc.tensor.transpose(PS[:, f.bank, q * P:(q + 1) * P], hT[:, 4 * kq + q, t * P:(t + 1) * P],
                                             ident)
                mm.then_inc(f.full.sem, 1)

        @block.scalar
        def _(act):
            c = counters()
            act.dma_start(base[:, :], a["k_base"]).then_inc(S("in_landed"), 16)
            act.dma_start(x_tok[:, 0], a["x"].rearrange("b (t p) d -> p (b t) d", p=P)).then_inc(S("in_landed"), 16)
            act.dma_start(x_tok[:, 1], a["ctx"].rearrange("b (t p) d -> p (b t) d", p=P)).then_inc(S("in_landed"), 16)
            act.wait_ge(S("rows_zero"), 1)
            for dst, src in vec_copies:
                act.dma_start(dst, src).then_inc(S("vec_landed"), 16)
            last = plan["setup"][8:]
            for f in last:
                f.free.wait(act)
            act.wait_ge(S("cleared"), 6)
            for dst, nm in ((cond1[:, :, 0], "c"), (cond1[:, :, 1], "c_ctx"), (cond2[:, :, 0], "c_2")):
                nc.scalar.activation(dst, cols(nm, 0, KC), ACT.Silu).then_inc(S("cond_ready"), 1)
            f = plan["lam"][0]
            f.full.wait(act)
            nc.scalar.activation(small[:, 2:4], PS[:, f.bank, 0:2], ACT.Exp).then_inc(f.free.sem, 1)

            def rows_act(f, buf, it):
                f.full.wait(act, it)
                nc.scalar.copy(ada_rows[:, buf, :], PS[:, f.bank, :]).then_inc(f.free.sem, 1)

            for which in ("first", "second"):
                us, fr, fc, rounds = adaP[which]
                with act.Fori(0, rounds) as it:
                    for j in range(6):
                        rows_act(fr[j], j % 3, it)

            def moe_act(l, ns, ready):
                p = f"moe{l}_"
                norm_act(act, c, p + "norm", l, 1, ns, first=ready)
                act.dma_start(moe_before.rearrange("p t n -> p (t n)"), a["k_before"]).then_inc(S("moe_const"), 16)
                act.dma_start(moe_wr, a["w_router"][l].rearrange("(k p) e -> p k e", p=P)).then_inc(S("moe_const"), 16)
                f = plan[p + "logit"][0]
                f.free.wait(act)
                nc.scalar.activation(moe_e[:, 0:2 * ns, :], moe_e[:, 0:2 * ns, :], ACT.Exp).then_inc(S("moe_exp"), 1)
                for i, f in enumerate(plan[p + "utok"]):
                    t, kq = i // 2, i % 2
                    copy_act(act, f, moe_utok[:, t, kq * 512:(kq + 1) * 512], PS[:, f.bank, :])
                f = plan[p + "affT"][0]
                rows = 2 * ns * E
                f.full.wait(act)
                nc.scalar.copy(moe_affT[0:rows, :], PS[0:rows, f.bank, 0:P]).then_inc(f.free.sem, 1)
                f.free.wait(act)
                for t in range(2 * ns):
                    act.dma_start(aff_dram[l][t // 2, :, (t % 2) * P:(t % 2 + 1) * P], moe_affT[t * E:(t + 1) * E, :])\
                        .then_inc(S("aff_out"), 16)
                act.wait_ge(S("aff_out"), 16 * ((4 if l else 0) + 2 * ns))
                for s in range(ns):
                    src = aff_dram[l][s].rearrange("e t -> (e t)").unsqueeze(0).to_broadcast([P, E * N])
                    act.dma_start(moe_aall[:, s].rearrange("p e t -> p (e t)"), src).then_inc(S(f"aff_in{s}"), 16)
                for i, f in enumerate(plan[p + "gather"]):
                    s, k = i // KC, i % KC
                    if i % 2:
                        f.full.wait(act)
                        nc.scalar.copy(moe_xe[:, k, :, s, :], PS[:, f.bank, :].rearrange("p (e c) -> p e c", e=E))\
                            .then_inc(f.free.sem, 1)
                fs = plan[p + "experts"]
                with act.Fori(0, 4) as it:
                    for j in range(4):
                        fg, fu, ft, fd = fs[4 * j:4 * j + 4]
                        fg.full.wait(act, it)
                        nc.scalar.activation(x_sil[:, j % 2, :], PS[:, fg.bank, :], ACT.Silu).then_inc(fg.free.sem, 1)
                        fd.full.wait(act, it)
                        for s in range(ns):
                            for h in range(2):
                                r = 64 * h + 32 * s
                                ins = nc.scalar.copy(
                                    moe_y[32 * j:32 * j + 32, s, bass.ds(it, 1), h * 512:(h + 1) * 512].rearrange("p o n -> p (o n)"),
                                    PS[r:r + 32, fd.bank, :])
                        ins.then_inc(fd.free.sem, 1)

            if LAST >= 1:
                act.wait_ge(S("mod_ready"), 1)
                norm_act(act, c, "ab_norm", 0, 0, 2)
                fs = plan["ab_in"]
                for m in range(4):
                    copy_act(act, fs[m], ab_z[:, m, :], PS[:, fs[m].bank, :])
                for m in range(4):
                    f = fs[4 + m]
                    f.full.wait(act)
                    if m >= 2:
                        act.wait_ge(S("z_in"), m - 1)
                    nc.scalar.activation(ab_sg[:, m % 2, :], PS[:, f.bank, :], ACT.Sigmoid).then_inc(f.free.sem, 1)
                for g, dst in enumerate((ab_gin, ab_val, ab_gout)):
                    for m in range(4):
                        f = fs[8 + 4 * g + m]
                        copy_act(act, f, dst[:, m, :], PS[:, f.bank, :])
                stat_act(act, c, [(ab_z[:, m, :], Mark(S("z_centred"), m + 1)) for m in range(4)],
                         plan["ab_var"][0], 512)
                rsqrt_act(act, c, plan["ab_var"][0], 512, 512)
                for m in range(4):
                    act.wait_ge(S("z_normed"), m + 1)
                    nc.scalar.activation(ab_z[:, m, :], ab_z[:, m, :], ACT.Silu, bias=col("ln_b_b", m),
                                         scale=col("ln_b_g", m)).then_inc(S("yb_ready"), 1)
            if LAST >= 2:
                moe_act(0, 2, plan["ab_out"][-1].free)
            if LAST >= 3:
                plan["moe0_combine"][-1].free.wait(act)
                act.dma_start(hy_const, a["k_hyena"]).then_inc(S("hy_const"), 16)
                act.dma_start(hf_w1[0:33, :], a["hf_w1"][0]).then_inc(S("hy_const"), 16)
                act.dma_start(hf_w2[0:64, :], a["hf_w2"][0]).then_inc(S("hy_const"), 16)
                act.dma_start(hf_w3[0:64, :], a["hf_w3"][0]).then_inc(S("hy_const"), 16)
                for r in range(2):
                    act.wait_ge(S("hf_arg"), r + 1)
                    nc.scalar.activation(hf_x[0:64, :], hf_x[0:64, :], ACT.Sin).then_inc(S("hf_sin"), 1)
                for q, f in enumerate(plan["hf_freq"]):
                    copy_act(act, f, hf_F[:, q, :], PS[:, f.bank, :])
                norm_act(act, c, "cd_norm", 1, 0, 2)
                act.wait_ge(S("hp_pad"), 1)
                for i, f in enumerate(plan["hy_in"]):
                    copy_act(act, f, hy_p[:, i, 1:N + 1], PS[:, f.bank, 0:N])
                for t, f in enumerate(plan["hy_utok"]):
                    copy_act(act, f, hy_utok[:, t, :], PS[:, f.bank, :])
                plan["hy_out"][-1].full.wait(act)
                act.dma_start(da_const, a["k_axial"]).then_inc(S("da_const"), 16)
                act.wait_ge(S("hy_y"), 4)
                for i, f in enumerate(plan["qk_in"]):
                    width = N if i < 4 else 2 * N
                    f.full.wait(act)
                    nc.scalar.activation(da_sq[:, i, 0:width], PS[:, f.bank, 0:width], ACT.Square)\
                        .then_inc(S("qk_sq"), 1)
                    nc.scalar.copy(da_qk[:, i, 0:width], PS[:, f.bank, 0:width]).then_inc(f.free.sem, 1)
                for t, f in enumerate(plan["v_in"]):
                    copy_act(act, f, da_v[:, t, :], PS[:, f.bank, :])
                for i, f in enumerate(plan["qk_ms"]):
                    rsqrt_act(act, c, f, N if i < 4 else 2 * N, 64, dst=da_rs[:, i, :])

                def exps(i):
                    for j in range(2):
                        f = plan["da_scores"][2 * i + j]
                        act.wait_ge(S("da_nb"), 2 * i + j + 1)
                        if i >= 2:
                            act.wait_ge(S("da_a"), i - 1)
                        k = 2 * i + j
                        nc.scalar.activation(da_p[:, i % 2, j, :], PS[:, f.bank, :], ACT.Exp, scale=0.125,
                                             bias=stat8[:, 16 + k:17 + k], accum_out=stat8[:, 32 + k:33 + k])\
                            .then_inc(f.free.sem, 1)

                def turn_act(i):
                    f = plan["da_turn"][i]
                    h, qc = i // 2, i % 2
                    f.full.wait(act)
                    if h >= 2 and qc == 0:
                        plan["da_out"][h - 2].full.wait(act)
                    nc.scalar.copy(da_aT[:, h % 2, :, qc * P:(qc + 1) * P],
                                   PS[:, f.bank, :].rearrange("p (k q) -> p k q", k=4)).then_inc(f.free.sem, 1)

                exps(0)
                for i in range(8):
                    if i < 7:
                        exps(i + 1)
                    turn_act(i)
                    if i % 2:
                        f = plan["da_out"][i // 2]
                        copy_act(act, f, da_o[:, i // 2, :], PS[:, f.bank, 0:N])
                for h in range(4):
                    stat_act(act, c, [(da_o[:, h, :], plan["da_out"][h].free)], plan["da_sub"][h], N)
                    rsqrt_act(act, c, plan["da_sub"][h], N, P, eps_at=1, dst=da_rso[:, h, :])
            if LAST >= 4:
                moe_act(1, 1, plan["cd_out"][-1].free)

            def mla_act(i, ready):
                p, j = f"b{i}_", n_mla[i]
                lat = plan[p + "lat"]
                norm_act(act, c, p + "norm", i + 2, 0, 1, first=ready)
                act.dma_start(ml_const, a["k_mla"]).then_inc(S("ml_const"), 16)
                stat_act(act, c, [(PS[:, lat[m].bank, 0:N], lat[m].full) for m in range(2)], plan[p + "ms"][0], N)
                stat_act(act, c, [(PS[:, lat[2].bank, 0:N], lat[2].full)], plan[p + "ms"][1], N)
                rsqrt_act(act, c, plan[p + "ms"][0], N, 256, dst=RS[:, 0:N])
                rsqrt_act(act, c, plan[p + "ms"][1], N, 128, dst=RS[:, N:2 * N])
                copy_act(act, lat[3], ml_kpe[0:64, :], PS[0:64, lat[3].bank, 0:N])
                for h in range(8):
                    f = plan[p + "qup"][2 * h]
                    copy_act(act, f, ml_qn[:, h, :], PS[:, f.bank, 0:N])
                    f = plan[p + "qup"][2 * h + 1]
                    copy_act(act, f, ml_qpe[0:64, h, :], PS[0:64, f.bank, 0:N])
                for m, f in enumerate(plan[p + "kvup"]):
                    if m < 8:
                        copy_act(act, f, ml_kn[:, m, :], PS[:, f.bank, 0:N])
                    else:
                        t, half = (m - 8) // 2, (m - 8) % 2
                        copy_act(act, f, ml_v[:, t, half * 512:(half + 1) * 512], PS[:, f.bank, :])

                def exps(i2):
                    width = (i2 % 2 + 1) * P
                    act.wait_ge(S("ml_nb"), 16 * j + i2 + 1)
                    nc.scalar.activation(ml_s[:, i2 % 2, 0:width], ml_s[:, i2 % 2, 0:width], ACT.Exp,
                                         bias=stat8[:, 16 + i2:17 + i2], accum_out=stat8[:, 32 + i2:33 + i2])\
                        .then_inc(S("ml_exp"), 1)

                act.wait_ge(S("pT_zero"), j + 1)
                exps(0)
                for i2 in range(16):
                    h, qc = i2 // 2, i2 % 2
                    if i2 < 15:
                        exps(i2 + 1)
                    f = plan[p + "turn"][i2]
                    if h >= 2 and qc == 0:
                        plan[p + "pv"][h - 2].full.wait(act)
                    copy_act(act, f, ml_pT[:, h % 2, 0:qc + 1, qc * P:(qc + 1) * P],
                             PS[:, f.bank, 0:(qc + 1) * P].rearrange("p (k q) -> p k q", k=qc + 1))
                    if qc == 1:
                        f = plan[p + "pv"][h]
                        copy_act(act, f, ml_o[:, h, :], PS[:, f.bank, 0:N])

            def stick_act(i, ready):
                p = f"b{i}_"
                norm_act(act, c, p + "norm", i + 2, 0, 1, first=ready)
                act.dma_start(st_const, a["k_stick"]).then_inc(S("st_const"), 16)
                for m, f in enumerate(plan[p + "qk"]):
                    copy_act(act, f, st_qk[:, m, :], PS[:, f.bank, 0:N])
                for m, f in enumerate(plan[p + "v"]):
                    copy_act(act, f, st_v[:, m % 2, (m // 2) * 512:(m // 2 + 1) * 512], PS[:, f.bank, :])
                for s in range(16 + 3):
                    if s < 16:
                        act.wait_ge(S("st_abs"), s + 1)
                        nc.scalar.activation(st_sp[:, s % 4, :], st_sp[:, s % 4, :], ACT.Exp, scale=-1.0)\
                            .then_inc(S("st_e"), 1)
                        act.wait_ge(S("st_e"), s + 1)
                        nc.scalar.activation(st_sp[:, s % 4, :], st_sp[:, s % 4, :], ACT.Ln, bias=one_col)\
                            .then_inc(S("st_l"), 1)
                    if 2 <= s <= 17:
                        k = s - 2
                        act.wait_ge(S("st_arg"), k + 1)
                        nc.scalar.activation(st_t[:, k % 4, :], st_t[:, k % 4, :], ACT.Exp).then_inc(S("st_a"), 1)
                    if s >= 4 and s % 2 == 0:
                        f = plan[p + "pv"][(s - 4) // 2]
                        copy_act(act, f, st_o[:, (s - 4) // 2, :], PS[:, f.bank, 0:N])

            def ret_act(i, ready):
                p = f"b{i}_"
                norm_act(act, c, p + "norm", i + 2, 0, 1, first=ready)
                act.dma_start(rt_decay.rearrange("p h n -> p (h n)"), a["k_ret"]).then_inc(S("rt_const"), 16)
                for m, f in enumerate(plan[p + "qk"]):
                    copy_act(act, f, rt_qk[:, m, :], PS[:, f.bank, 0:N])
                for m, f in enumerate(plan[p + "v"]):
                    copy_act(act, f, rt_v[:, m % 2, (m // 2) * 512:(m // 2 + 1) * 512], PS[:, f.bank, :])
                for m, f in enumerate(plan[p + "g"]):
                    f.full.wait(act)
                    nc.scalar.activation(rt_g[:, m, :], PS[:, f.bank, 0:N], ACT.Silu).then_inc(f.free.sem, 1)
                for m, f in enumerate(plan[p + "pv"]):
                    copy_act(act, f, rt_o[:, m, :], PS[:, f.bank, 0:N])
                for h in range(4):
                    stat_act(act, c, [(rt_o[:, 4 * h + q, :], plan[p + "pv"][4 * h + q].free) for q in range(4)],
                             plan[p + "ms"][h], N)
                    rsqrt_act(act, c, plan[p + "ms"][h], N, 512, dst=rt_rs[:, h, :])

            def post_act(name_out, name, per):
                for m, f in enumerate(plan[name_out]):
                    w = per * N
                    copy_act(act, f, y_T[:, per * m:per * (m + 1), :].rearrange("p k t -> p (k t)"), PS[:, f.bank, 0:w])
                stat_act(act, c, [(y_T[:, k, :], plan[name_out][k // per].free) for k in range(KC)],
                         plan[name][0], N)
                rsqrt_act(act, c, plan[name][0], N, D)

            nh = 0
            ready = plan["moe1_combine"][-1].free if LAST >= 5 else None
            if LAST >= 5:
                ready.wait(act)
                act.dma_start(pos_i, a["positions_2"].to_broadcast([P, N])).then_inc(S("pos"), 16)
                for r in range(4):
                    act.wait_ge(S("tab_arg"), r + 1)
                    nc.scalar.activation(rope_tab[:, r, :], rope_tab[:, r, :], ACT.Sin).then_inc(S("tab"), 1)
                act.wait_ge(S("tab_arg"), 4)
            for i, kind in enumerate(KINDS[:max(0, LAST - 4)]):
                p = f"b{i}_"
                {"mla": mla_act, "stick": stick_act, "ret": ret_act}[kind](i, ready)
                post_act(p + "out", p + "post", 1)
                nh += 1
                norm_act(act, c, p + "fnorm", i + 2, 1, 1, first=Mark(S("h_done"), nh))
                with act.Fori(0, 4) as it:
                    for g in range(2):
                        for m in range(4):
                            f = plan[p + "up"][4 * g + m]
                            f.full.wait(act, it)
                            nc.scalar.activation(ffn_h[:, g, m, :], PS[:, f.bank, 0:N], ACT.Relu)\
                                .then_inc(f.free.sem, 1)
                            if i < 3 and (g, m) == (1, 0):
                                rows_act(plan[p + "ada_rows"][0], 0, it)
                    if i < 3:
                        rows_act(plan[p + "ada_rows"][1], 1, it)
                        rows_act(plan[p + "ada_rows"][2], 2, it)
                post_act(p + "down", p + "fpost", 2)
                nh += 1
                ready = Mark(S("h_done"), nh)
                if i < 3:
                    act.wait_ge(S("mod_ready"), i + 2)

        @block.vector
        def _(dve):
            c = counters()
            ch = Chain(dve, S("dve_seq"))
            V_ = nc.vector
            TT, TS, STT = V_.tensor_tensor, V_.tensor_scalar, V_.scalar_tensor_tensor
            V_.memset(v_rows, 0.0).then_inc(S("rows_zero"), 1)
            fs = plan["setup"]
            i = 0
            for s in range(2):
                for t in range(TC):
                    for kq in range(2):
                        f = fs[i]
                        f.full.wait(dve)
                        V_.tensor_copy(hT[:, 4 * kq:4 * kq + 4, s * N + t * P:s * N + (t + 1) * P],
                                       PS[:, f.bank, :].rearrange("p (k t) -> p k t", k=4)).then_inc(f.free.sem, 1)
                        i += 1
            for j in range(0, NVR, 4):
                f = fs[i]
                n = min(4 * P, NV - j * P)
                f.full.wait(dve)
                V_.tensor_copy(V[:, j * P:j * P + n], PS[:, f.bank, 0:n]).then_inc(f.free.sem, 1)
                i += 1
            for f in fs[8:]:
                f.free.wait(dve)
            TT(small[:, 0:1], col("lam_q1"), col("lam_k1"), ALU.mult).then_inc(S("lam_a"), 1)
            dve.wait_ge(S("lam_a"), 1)
            TT(small[:, 1:2], col("lam_q2"), col("lam_k2"), ALU.mult).then_inc(S("lam_prod"), 1)
            plan["lam"][0].free.wait(dve)
            ch.do(TT(small[:, 4:5], small[:, 3:4], small[:, 2:3], ALU.subtract))
            ch.do(TS(small[:, 5:6], small[:, 4:5], -LAM_INIT, None, ALU.add))
            ch.do(TS(small[:, 6:7], col("g_subln"), 1.0 - LAM_INIT, None, ALU.mult))

            def cols_dve(f, at, step, n, it):
                f.full.wait(dve, it)
                src = PS[:, f.bank, :].rearrange("p (q j r) -> p q r j", q=4, j=4)[:, :, 0:n, :]
                dst = MOD[:, bass.ds(it * step + at, 4 * n)].rearrange("p (q r) -> p q r", q=4)
                V_.tensor_reduce(dst, src, AX.X, ALU.add).then_inc(f.free.sem, 1)

            def gains_first():
                m = MOD[:, 0:192].rearrange("p (i s) -> p i s", s=2)
                ch.do(TT(m, m, cols("b_ada", 0, 96).unsqueeze(2).to_broadcast([P, 96, 2]), ALU.add))
                for l in range(2):
                    for which, nm in ((0, "g_mix"), (1, "g_ffn")):
                        at = l * 96 + (3 * which + 1) * 16
                        g = cols(nm, l * KC, KC).unsqueeze(2).to_broadcast([P, KC, 2])
                        o = l * 32 + which * 16
                        ch.put(STT(AM[:, o:o + 16].rearrange("p (k s) -> p k s", s=2),
                                   MOD[:, at:at + 16].rearrange("p (k s) -> p k s", s=2), 1.0, g, ALU.add, ALU.mult))
                ch.sync()

            def gains_second(i):
                at = 192 + i * 48
                ch.do(TT(MOD[:, at:at + 48], MOD[:, at:at + 48], cols("ada_b_2", i * 48, 48), ALU.add))
                for which in range(2):
                    o = 64 + i * 16 + which * 8
                    sc = at + (3 * which + 1) * 8
                    ch.put(STT(AM[:, o:o + 8], MOD[:, sc:sc + 8], 1.0, cols("norm_g", (i * 4 + 2 * which) * 8, 8),
                               ALU.add, ALU.mult))
                    ch.put(TT(GP[:, i, which, :], MOD[:, sc + 8:sc + 16], cols("norm_g", (i * 4 + 2 * which + 1) * 8, 8),
                              ALU.mult))
                ch.sync()
                ch.sync()

            for which, at, n in (("first", 0, 2), ("second", 192, 1)):
                us, fr, fc, rounds = adaP[which]
                with dve.Fori(0, rounds) as it:
                    for j in range(6):
                        cols_dve(fc[j], at + j * 4 * n, 24 * n, n, it)
                for f in fc[-2:]:
                    f.free.wait(dve, rounds - 1)
            gains_first()
            gains_second(0)
            TS(small[:, 7:8], small[:, 5:6], 1.0, None, ALU.mult).then_inc(S("mod_ready"), 1)

            def trig(x, k, rows, quarter):
                ch.do(TS(k, x, 1.0 / TWO_PI, 0.25 if quarter else 0.0, ALU.mult, ALU.add))
                ch.do(TS(k, k, ROUND, None, ALU.add))
                ch.do(TS(k, k, -ROUND, None, ALU.add))
                for part in (PI_A, PI_B, PI_C):
                    ch.do(STT(x, k, -part, x, ALU.mult, ALU.add))
                if quarter:
                    ch.do(TS(x, x, math.pi / 2, None, ALU.add))
                return TS(x, x, PI_SAFE, -PI_SAFE, ALU.min, ALU.max)

            def moe_dve(l, ns):
                p = f"moe{l}_"
                nt = 2 * ns
                norm_dve(dve, c, p + "norm", l, 1, ns)
                f = plan[p + "logit"][0]
                f.full.wait(dve)
                lg = PS[:, f.bank, 0:nt * E].rearrange("p (t e) -> p t e", t=nt)
                bc = lambda v: v[:, 0:nt].unsqueeze(2).to_broadcast([P, nt, E])
                ch.do(V_.tensor_reduce(moe_mx[:, 0:nt], lg, AX.X, ALU.max))
                TT(moe_e[:, 0:nt, :], lg, bc(moe_mx), ALU.subtract).then_inc(f.free.sem, 1)
                dve.wait_ge(S("moe_exp"), l + 1)
                ch.do(V_.tensor_reduce(moe_sm[:, 0:nt], moe_e[:, 0:nt, :], AX.X, ALU.add))
                ch.do(V_.reciprocal(moe_sm[:, 0:nt], moe_sm[:, 0:nt]))
                TT(moe_aff[:, 0:nt, :], moe_e[:, 0:nt, :], bc(moe_sm), ALU.mult).then_inc(S("moe_aff"), 1)
                dve.wait_ge(S("moe_aff"), l + 1)
                dve.wait_ge(S("moe_const"), 32 * (l + 1))
                for t in range(nt):
                    s = t // 2
                    if t % 2 == 0:
                        dve.wait_ge(S(f"aff_in{s}"), 16 * (l + 1))
                    for e in range(E):
                        i = t * E + e
                        ch.sync(back=1)
                        ch.put(STT(moe_junk[:, 0, :], moe_aall[:, s, e, :], moe_aff[:, t, e:e + 1], moe_before[:, t % 2, :],
                                   ALU.is_equal, ALU.mult, accum_out=moe_c1[:, i:i + 1]))
                        ch.sync(back=1)
                        ch.put(TS(moe_junk[:, 1, :], moe_aall[:, s, e, :], moe_aff[:, t, e:e + 1], 0.0,
                                  ALU.is_gt, ALU.add, accum_out=moe_c2[:, i:i + 1]))
                ch.sync()
                rank = moe_rank.rearrange("p t e -> p (t e)")
                ch.do(TT(rank[:, 0:nt * E], moe_c1[:, 0:nt * E], moe_c2[:, 0:nt * E], ALU.add))
                for t in range(nt):
                    TT(moe_sel[:, t], iota.unsqueeze(1).to_broadcast([P, E, CAP]),
                       moe_rank[:, t].unsqueeze(2).to_broadcast([P, E, CAP]), ALU.is_equal).then_inc(S("moe_sel"), 1)
                dve.wait_ge(S("moe_sel"), (4 if l else 0) + nt)
                for t in range(nt):
                    TT(moe_selw[:, t], moe_sel[:, t], moe_aff[:, t].unsqueeze(2).to_broadcast([P, E, CAP]), ALU.mult)\
                        .then_inc(S("moe_selw"), 1)
                for i, f in enumerate(plan[p + "gather"]):
                    s, k = i // KC, i % KC
                    if i % 2 == 0:
                        f.full.wait(dve)
                        V_.tensor_copy(moe_xe[:, k, :, s, :], PS[:, f.bank, :].rearrange("p (e c) -> p e c", e=E))\
                            .then_inc(f.free.sem, 1)
                for t, f in enumerate(plan[p + "selT"]):
                    f.full.wait(dve)
                    V_.tensor_copy(moe_selT[:, t // 2, :, (t % 2) * P:(t % 2 + 1) * P],
                                   PS[:, f.bank, :].rearrange("p (q t) -> p q t", q=4)).then_inc(f.free.sem, 1)
                fs = plan[p + "experts"]
                with dve.Fori(0, 4) as it:
                    for j in range(4):
                        fg, fu, ft, fd = fs[4 * j:4 * j + 4]
                        fu.full.wait(dve, it)
                        fg.free.wait(dve, it)
                        TT(x_act[:, j % 2, :], x_sil[:, j % 2, :], PS[:, fu.bank, :], ALU.mult).then_inc(fu.free.sem, 1)
                        ft.full.wait(dve, it)
                        V_.tensor_copy(x_actT[:, j % 2].rearrange("p q t -> p (q t)"), PS[:, ft.bank, :])\
                            .then_inc(ft.free.sem, 1)
                for i, f in enumerate(plan[p + "combine"]):
                    s, m = i // KC, i % KC
                    t = slice(s * N, (s + 1) * N)
                    f.full.wait(dve)
                    STT(hT[:, m, t], PS[:, f.bank, 0:N], mod(l, 5, m, s), hT[:, m, t], ALU.mult, ALU.add)\
                        .then_inc(f.free.sem, 1)
                for f in plan[p + "combine"][-4:]:
                    f.free.wait(dve)

            if LAST >= 1:
                norm_dve(dve, c, "ab_norm", 0, 0, 2)
                dve.wait_ge(S("ab_pads"), 2)
                fs = plan["ab_in"]
                for m in range(4):
                    fs[m].free.wait(dve)
                    fs[4 + m].free.wait(dve)
                    TT(ab_zin[:, m, :, 15:15 + N], v512(ab_z[:, m, :]), v512(ab_sg[:, m % 2, :]), ALU.mult)\
                        .then_inc(S("z_in"), 1)
                for j in range(31):
                    for m in range(4):
                        src, w = ab_zin[:, m, :, j:j + N], col("conv_b", 4 * j + m)
                        dst = v512(ab_z[:, m, :])
                        if j == 0:
                            dve.wait_ge(S("z_in"), 4)
                            ch.put(TS(dst, src, w, col("conv_b_bias", m), ALU.mult, ALU.add))
                        else:
                            ch.sync(back=3)
                            ins = STT(dst, src, w, dst, ALU.mult, ALU.add)
                            if j < 30:
                                ch.put(ins)
                            else:
                                ins.then_inc(S("z_conv"), 1)
                                if m < 3:
                                    dve.wait_ge(S("dve_seq"), ch.n)
                for j in range(3):
                    for m in range(4):
                        if j == 0:
                            dve.wait_ge(S("ab_gv"), m + 1)
                            ch.put(TS(v512(ab_gin[:, m, :]), ab_gv[:, m, :, 0:N], col("conv_a", m), None, ALU.mult))
                        else:
                            ch.sync(back=3)
                            ch.put(STT(v512(ab_gin[:, m, :]), ab_gv[:, m, :, j:j + N], col("conv_a", 4 * j + m),
                                       v512(ab_gin[:, m, :]), ALU.mult, ALU.add))
                for m in range(4):
                    fs[16 + m].free.wait(dve)
                    ch.sync()
                    TT(ab_gin[:, m, :], ab_gin[:, m, :], ab_gout[:, m, :], ALU.mult).then_inc(S("ya_ready"), 1)
                f = plan["ab_mean"][0]
                f.full.wait(dve)
                TS(ab_mu, PS[:, f.bank, :], 1.0 / 512, None, ALU.mult).then_inc(f.free.sem, 1)
                f.free.wait(dve)
                dve.wait_ge(S("z_conv"), 4)
                for m in range(4):
                    TT(ab_z[:, m, :], ab_z[:, m, :], ab_mu, ALU.subtract).then_inc(S("z_centred"), 1)
                rsqrt_wait(dve, c)
                dve.wait_ge(S("z_centred"), 4)
                for m in range(4):
                    TT(ab_z[:, m, :], ab_z[:, m, :], RS[:, 0:512], ALU.mult).then_inc(S("z_normed"), 1)
                residual_dve(ch, "ab_out", 0, 2, 2)
                for f in plan["ab_out"][-4:]:
                    f.free.wait(dve)
            if LAST >= 2:
                moe_dve(0, 2)
            if LAST >= 3:
                for r in range(2):
                    f = plan["hf_mlp"][r]
                    f.full.wait(dve)
                    TS(hf_x[0:64, :], PS[0:64, f.bank, 0:N], col(("hf_b1", "hf_b2")[r])[0:64], col("hf_freq")[0:64],
                       ALU.add, ALU.mult).then_inc(f.free.sem, 1)
                    f.free.wait(dve)
                    trig(hf_x[0:64, :], hf_k[0:64, :], 64, False).then_inc(S("hf_arg"), 1)
                for t, f in enumerate(plan["hf_tok"]):
                    f.full.wait(dve)
                    TT(hf_tok[:, t, :], PS[:, f.bank, :], hy_decay[:, t, :], ALU.mult).then_inc(f.free.sem, 1)
                norm_dve(dve, c, "cd_norm", 1, 0, 2)
                orig = [4, 5, 6, 7, 8, 9, 10, 11, 0, 1, 2, 3]
                for g in range(3):
                    for j in range(3):
                        for m in range(4):
                            i = 4 * g + m
                            w = col("conv_d", j * 12 + orig[i])
                            if j == 0:
                                plan["hy_in"][i].free.wait(dve)
                                ch.put(TS(hy_z[:, i, :], hy_p[:, i, 0:N], w, None, ALU.mult))
                            else:
                                ch.sync(back=3)
                                ch.put(STT(hy_z[:, i, :], hy_p[:, i, j:j + N], w, hy_z[:, i, :], ALU.mult, ALU.add))
                    if g == 1:
                        ch.sync()
                        for m in range(4):
                            TT(hy_z[:, m, :], hy_z[:, m, :], hy_z[:, 4 + m, :], ALU.mult).then_inc(S("hy_u"), 1)
                fr = plan["hy_ufreq"]
                for fc in range(2):
                    re, im = PS[:, fr[fc].bank, :], PS[:, fr[2 + fc].bank, :]
                    fr[2 + fc].full.wait(dve)
                    plan["hf_freq"][2 + fc].free.wait(dve)
                    ch.sync()
                    dve.wait_ge(S("hy_u"), 4)
                    if fc:
                        dve.wait_ge(S("hy_Y"), 2)
                    ch.put(TT(hy_t[:, 0, :], re, hf_F[:, fc, :], ALU.mult))
                    ch.do(TT(hy_t[:, 1, :], im, hf_F[:, 2 + fc, :], ALU.mult))
                    TT(hy_Y[:, fc, :], hy_t[:, 0, :], hy_t[:, 1, :], ALU.subtract).then_inc(S("hy_Y"), 1)
                    dve.wait_ge(S("hy_Y"), 2 * fc + 1)
                    TT(hy_t[:, 0, :], re, hf_F[:, 2 + fc, :], ALU.mult).then_inc(fr[fc].free.sem, 1)
                    TT(hy_t[:, 1, :], im, hf_F[:, fc, :], ALU.mult).then_inc(fr[2 + fc].free.sem, 1)
                    fr[fc].free.wait(dve)
                    fr[2 + fc].free.wait(dve)
                    TT(hy_Y[:, 2 + fc, :], hy_t[:, 0, :], hy_t[:, 1, :], ALU.add).then_inc(S("hy_Y"), 1)
                for m, f in enumerate(plan["hy_out"]):
                    f.full.wait(dve)
                    STT(hy_y[:, m, :], hy_z[:, m, :], col("hf_bias", m), PS[:, f.bank, 0:N], ALU.mult, ALU.add)\
                        .then_inc(f.free.sem, 1)
                for m, f in enumerate(plan["hy_out"]):
                    f.free.wait(dve)
                    TT(hy_y[:, m, :], hy_y[:, m, :], hy_z[:, 8 + m, :], ALU.mult).then_inc(S("hy_y"), 1)
                for i in range(8):
                    width = N if i < 4 else 2 * N
                    rsqrt_wait(dve, c)
                    plan["qk_in"][i].free.wait(dve)
                    STT(da_qk[:, i, 0:width], da_qk[:, i, 0:width], col("g_q" if i < 4 else "g_k"), da_rs[:, i, 0:width],
                        ALU.mult, ALU.mult).then_inc(S("qk_n"), 1)
                for i, f in enumerate(plan["qk_rot"]):
                    f.full.wait(dve)
                    TT(da_sq[:, i, 0:N], PS[:, f.bank, 0:N], da_sin, ALU.mult).then_inc(f.free.sem, 1)
                    ch.do(TT(da_qk[:, i, 0:N], da_qk[:, i, 0:N], da_cos, ALU.mult))
                    f.free.wait(dve)
                    TT(da_qk[:, i, 0:N], da_qk[:, i, 0:N], da_sq[:, i, 0:N], ALU.add).then_inc(S("qk_rope"), 1)

                def da_max(i):
                    for j in range(2):
                        k = 2 * i + j
                        f = plan["da_scores"][k]
                        f.full.wait(dve)
                        ch.do(V_.tensor_reduce(stat8[:, k:k + 1], PS[:, f.bank, :], AX.X, ALU.max))
                        TS(stat8[:, 16 + k:17 + k], stat8[:, k:k + 1], -0.125, None, ALU.mult).then_inc(S("da_nb"), 1)

                dve.wait_ge(S("qk_rope"), 8)
                da_max(0)
                for i in range(8):
                    if i < 7:
                        da_max(i + 1)
                    f0, f1 = plan["da_scores"][2 * i:2 * i + 2]
                    f0.free.wait(dve)
                    f1.free.wait(dve)
                    r = stat8[:, 48 + 2 * i:50 + 2 * i]
                    ch.do(V_.reciprocal(r, stat8[:, 32 + 2 * i:34 + 2 * i]))
                    ch.put(TT(r[:, 1:2], r[:, 1:2], small[:, 5:6], ALU.mult))
                    if i >= 2:
                        plan["da_turn"][i - 2].full.wait(dve)
                    ch.do(TS(da_a[:, i % 2, :], da_p[:, i % 2, 0, :], r[:, 0:1], None, ALU.mult))
                    STT(da_a[:, i % 2, :], da_p[:, i % 2, 1, :], r[:, 1:2], da_a[:, i % 2, :], ALU.mult, ALU.add)\
                        .then_inc(S("da_a"), 1)
                for h in range(4):
                    rsqrt_wait(dve, c)
                    STT(da_o[:, h, :], da_o[:, h, :], small[:, 6:7], da_rso[:, h, :], ALU.mult, ALU.mult)\
                        .then_inc(S("da_o"), 1)
                residual_dve(ch, "cd_out", 1, 2, 1)
                for f in plan["cd_out"][-4:]:
                    f.free.wait(dve)
            if LAST >= 4:
                moe_dve(1, 1)

            def mla_dve(i):
                p, j = f"b{i}_", n_mla[i]
                lat = plan[p + "lat"]
                norm_dve(dve, c, p + "norm", i + 2, 0, 1)
                rsqrt_wait(dve, c)
                for m in range(2):
                    STT(ml_qlat[:, m, :], PS[:, lat[m].bank, 0:N], col("mla_q_norm_2", 2 * j + m), RS[:, 0:N],
                        ALU.mult, ALU.mult).then_inc(lat[m].free.sem, 1)
                rsqrt_wait(dve, c)
                STT(ml_kvlat, PS[:, lat[2].bank, 0:N], col("mla_kv_norm_2", j), RS[:, N:2 * N], ALU.mult, ALU.mult)\
                    .then_inc(lat[2].free.sem, 1)
                f = plan[p + "kper"][0]
                cos, sin = rope_tab[0:64, 0, :], rope_tab[0:64, 1, :]
                f.full.wait(dve)
                dve.wait_ge(S("tab"), 4)
                TT(ml_kt[0:64, :], PS[0:64, f.bank, 0:N], sin, ALU.mult).then_inc(f.free.sem, 1)
                lat[3].free.wait(dve)
                ch.do(TT(ml_kpe[0:64, :], ml_kpe[0:64, :], cos, ALU.mult))
                f.free.wait(dve)
                TT(ml_kpe[0:64, :], ml_kpe[0:64, :], ml_kt[0:64, :], ALU.add).then_inc(S("ml_rope"), 1)
                for r, f in enumerate(plan[p + "qrot"]):
                    pair = ml_qpe[0:64, 2 * r:2 * r + 2, :]
                    tmp = ml_qt[0:64, 2 * r:2 * r + 2, :]
                    f.full.wait(dve)
                    TT(tmp, PS[0:64, f.bank, :].rearrange("p (h t) -> p h t", h=2),
                       sin.unsqueeze(1).to_broadcast([64, 2, N]), ALU.mult).then_inc(f.free.sem, 1)
                    ch.do(TT(pair, pair, cos.unsqueeze(1).to_broadcast([64, 2, N]), ALU.mult))
                    f.free.wait(dve)
                    TT(pair, pair, tmp, ALU.add).then_inc(S("ml_rope"), 1)

                def soft_a(i2):
                    qc = i2 % 2
                    width = (qc + 1) * P
                    f = plan[p + "scores"][i2]
                    f.full.wait(dve)
                    if i2 >= 2:
                        plan[p + "turn"][i2 - 2].full.wait(dve)
                    s = ml_s[:, i2 % 2, 0:width]
                    STT(s, PS[:, f.bank, 0:width], mla_scale, ml_causal[:, qc, 0:width], ALU.mult, ALU.add)\
                        .then_inc(f.free.sem, 1)
                    f.free.wait(dve)
                    ch.do(V_.tensor_reduce(stat8[:, i2:i2 + 1], s, AX.X, ALU.max))
                    TS(stat8[:, 16 + i2:17 + i2], stat8[:, i2:i2 + 1], -1.0, None, ALU.mult).then_inc(S("ml_nb"), 1)

                def soft_b(i2):
                    width = (i2 % 2 + 1) * P
                    dve.wait_ge(S("ml_exp"), 16 * j + i2 + 1)
                    ch.do(V_.reciprocal(stat8[:, 48 + i2:49 + i2], stat8[:, 32 + i2:33 + i2]))
                    s = ml_s[:, i2 % 2, 0:width]
                    TS(s, s, stat8[:, 48 + i2:49 + i2], None, ALU.mult).then_inc(S("ml_p"), 1)

                soft_a(0)
                for i2 in range(16):
                    if i2 < 15:
                        soft_a(i2 + 1)
                    soft_b(i2)

            def stick_dve(i):
                p = f"b{i}_"
                norm_dve(dve, c, p + "norm", i + 2, 0, 1)
                dve.wait_ge(S("st_const"), 16)
                for s in range(16 + 3):
                    if s < 16:
                        f = plan[p + "z"][s]
                        f.full.wait(dve)
                        if s >= 4:
                            k = s - 4
                            if k % 2:
                                plan[p + "pv"][k // 2].full.wait(dve)
                            else:
                                dve.wait_ge(S("st_pv"), k // 2 + 1)
                            plan[p + "suf"][k].full.wait(dve)
                        STT(st_t[:, s % 4, :], PS[:, f.bank, 0:384], 0.125, st_mask, ALU.mult, ALU.add)\
                            .then_inc(f.free.sem, 1)
                        f.free.wait(dve)
                        STT(st_sp[:, s % 4, :], st_t[:, s % 4, :], -1.0, st_t[:, s % 4, :], ALU.mult, ALU.max)\
                            .then_inc(S("st_abs"), 1)
                    if 1 <= s <= 16:
                        k = s - 1
                        dve.wait_ge(S("st_l"), k + 1)
                        STT(st_sp[:, k % 4, :], st_t[:, k % 4, :], 0.0, st_sp[:, k % 4, :], ALU.max, ALU.add)\
                            .then_inc(S("st_sp"), 1)
                    if 2 <= s <= 17:
                        k = s - 2
                        f = plan[p + "suf"][k]
                        f.full.wait(dve)
                        TT(st_t[:, k % 4, :], st_t[:, k % 4, :], PS[:, f.bank, 0:384], ALU.subtract)\
                            .then_inc(f.free.sem, 1)
                        f.free.wait(dve)
                        TS(st_t[:, k % 4, :], st_t[:, k % 4, :], 0.0, None, ALU.min).then_inc(S("st_arg"), 1)

            def ret_dve(i):
                p = f"b{i}_"
                norm_dve(dve, c, p + "norm", i + 2, 0, 1)
                cos, sin = rope_tab[:, 2, :], rope_tab[:, 3, :]
                qk = plan[p + "qk"]
                for r in range(8):
                    x1, x2 = rt_qk[:, 2 * r, :], rt_qk[:, 2 * r + 1, :]
                    qk[2 * r].free.wait(dve)
                    qk[2 * r + 1].free.wait(dve)
                    if r:
                        dve.wait_ge(S("rt_rope"), r)
                    ch.put(TT(rt_t[:, 0, :], x1, sin, ALU.mult))
                    ch.put(TT(rt_t[:, 1, :], x2, sin, ALU.mult))
                    ch.put(TT(x1, x1, cos, ALU.mult))
                    ch.put(TT(x2, x2, cos, ALU.mult))
                    ch.sync()
                    ch.put(TT(x1, x1, rt_t[:, 1, :], ALU.subtract))
                    TT(x2, x2, rt_t[:, 0, :], ALU.add).then_inc(S("rt_rope"), 1)
                    ch.sync()
                dve.wait_ge(S("rt_const"), 16)
                for h, f in enumerate(plan[p + "s"]):
                    f.full.wait(dve)
                    TT(rt_s[:, h, :], PS[:, f.bank, 0:384], rt_decay[:, h, :], ALU.mult).then_inc(f.free.sem, 1)
                for h in range(4):
                    rsqrt_wait(dve, c)
                    for q in range(4):
                        m = 4 * h + q
                        ch.do(STT(rt_o[:, m, :], rt_o[:, m, :], col("ret_gn_g_2", m), rt_rs[:, h, :], ALU.mult, ALU.mult))
                        plan[p + "g"][m].free.wait(dve)
                        TT(rt_o[:, m, :], rt_o[:, m, :], rt_g[:, m, :], ALU.mult).then_inc(S("rt_o"), 1)

            def post_dve(i, name, which):
                rsqrt_wait(dve, c)
                for m in range(KC):
                    ch.put(STT(y_T[:, m, :], y_T[:, m, :], GP[:, i, which, m:m + 1], RS[:, 0:N], ALU.mult, ALU.mult))
                for m in range(KC):
                    ch.sync(back=KC - 1 if m == 0 else 0)
                    ins = TT(hT[:, m, 0:N], hT[:, m, 0:N], y_T[:, m, :], ALU.add)
                    if m < KC - 1:
                        ch.put(ins)
                    else:
                        ins.then_inc(S("h_done"), 1)

            if LAST >= 5:
                plan["moe1_combine"][-1].free.wait(dve)
                dve.wait_ge(S("pos"), 16)
                ch.do(V_.tensor_copy(pos_f, pos_i))
                for r in range(4):
                    ch.do(TS(rope_tab[:, r, :], pos_f, invf[:, r // 2:r // 2 + 1], None, ALU.mult))
                    trig(rope_tab[:, r, :], rope_k, P, r % 2 == 0).then_inc(S("tab_arg"), 1)
                    dve.wait_ge(S("tab_arg"), r + 1)
            nh = 0
            for i, kind in enumerate(KINDS[:max(0, LAST - 4)]):
                p = f"b{i}_"
                {"mla": mla_dve, "stick": stick_dve, "ret": ret_dve}[kind](i)
                post_dve(i, p + "post", 0)
                nh += 1
                dve.wait_ge(S("h_done"), nh)
                norm_dve(dve, c, p + "fnorm", i + 2, 1, 1)
                fu = plan[p + "up"]
                with dve.Fori(0, 4) as it:
                    for g in range(2):
                        for m in range(4):
                            f = fu[4 * g + m]
                            f.free.wait(dve, it)
                            TT(ffn_h[:, g, m, :], ffn_h[:, g, m, :], ffn_h[:, g, m, :], ALU.mult)\
                                .then_inc(S("ffn_squared"), 1)
                        if g == 1 and i < 3:
                            for q in range(3):
                                cols_dve(plan[p + "ada_cols"][q], 192 + (i + 1) * 48 + 4 * q, 12, 1, it)
                if i < 3:
                    plan[p + "ada_cols"][-1].free.wait(dve, 3)
                    gains_second(i + 1)
                    TS(small[:, 7:8], small[:, 5:6], 1.0, None, ALU.mult).then_inc(S("mod_ready"), 1)
                post_dve(i, p + "fpost", 1)
                nh += 1
                dve.wait_ge(S("h_done"), nh)
            TS(small[:, 8:9], small[:, 5:6], 1.0, None, ALU.mult).then_inc(S("h_final"), 1)
            for i, f in enumerate(plan["final"]):
                t, kq = i // 2, i % 2
                f.full.wait(dve)
                ins = V_.tensor_copy(out_tok[:, t, kq * 512:(kq + 1) * 512], PS[:, f.bank, :])
                if kq == 1:
                    ins.then_inc(S("out_ready"), 1)
                else:
                    ins.then_inc(f.free.sem, 1)

        @block.gpsimd
        def _(pool):
            c = counters()
            nc.gpsimd.memset(ones[:, :], 1.0).then_inc(S("cleared"), 1)
            nc.gpsimd.memset(zeros_bf[:, :], 0.0).then_inc(S("cleared"), 1)
            nc.gpsimd.memset(cond1, 0.0).then_inc(S("cleared"), 1)
            nc.gpsimd.memset(cond2[:, :, :], 0.0).then_inc(S("cleared"), 1)
            nc.gpsimd.memset(small[:, 9:10], EPS).then_inc(S("cleared"), 1)
            nc.gpsimd.memset(small[:, 10:11], SUBLN_EPS).then_inc(S("cleared"), 1)

            def moe_pool(l, ns):
                p = f"moe{l}_"
                fs = plan[p + "experts"]
                for f in plan[p + "gather"][-4:]:
                    f.free.wait(pool)
                if ns == 1:
                    nc.gpsimd.memset(x_cur[:, :, :, CAP:2 * CAP], 0.0).then_inc(S("x_zero"), 1)
                    pool.wait_ge(S("x_zero"), 1)
                with pool.Fori(0, 4) as it:
                    for j in range(4):
                        fs[4 * ((j + 2) % 4) + 1].full.wait(pool, it if j >= 2 else it - 1)
                        nc.gpsimd.tensor_copy(
                            x_cur[:, j % 2, :, 0:CAP * ns].rearrange("p k (s c) -> p k s c", s=ns),
                            moe_xe[:, :, bass.ds(it * 4 + j, 1), 0:ns, :].rearrange("p k o s c -> p k (o s) c"))\
                            .then_inc(S("x_cur"), 1)

            if LAST >= 1:
                pool.wait_ge(S("mod_ready"), 1)
                nc.gpsimd.memset(ab_gv, 0.0).then_inc(S("ab_pads"), 1)
                nc.gpsimd.memset(ab_zin, 0.0).then_inc(S("ab_pads"), 1)
                fs = plan["ab_in"]
                pool.wait_ge(S("ab_pads"), 2)
                for m in range(4):
                    fs[8 + m].free.wait(pool)
                    fs[12 + m].free.wait(pool)
                    nc.gpsimd.tensor_tensor(ab_gv[:, m, :, 1:N + 1], v512(ab_gin[:, m, :]), v512(ab_val[:, m, :]),
                                            ALU.mult).then_inc(S("ab_gv"), 1)
            if LAST >= 2:
                moe_pool(0, 2)
            if LAST >= 3:
                plan["moe0_combine"][-1].free.wait(pool)
                nc.gpsimd.memset(hy_p, 0.0).then_inc(S("hp_pad"), 1)
            if LAST >= 4:
                moe_pool(1, 1)
            for i, kind in enumerate(KINDS[:max(0, LAST - 4)]):
                p = f"b{i}_"
                if kind == "mla":
                    if i == 0:
                        plan["moe1_combine"][-1].free.wait(pool)
                    else:
                        pool.wait_ge(S("h_done"), 2 * i)
                    nc.gpsimd.memset(ml_pT, 0.0).then_inc(S("pT_zero"), 1)


def kernel(**inputs):
    import numpy as _np
    import concourse.bacc as _bacc
    from concourse import mybir as _mybir
    from concourse.bass_utils import run_bass_kernel_spmd as _run

    nc = _bacc.Bacc("TRN2", target_bir_lowering=False, num_devices=1)
    arrays, aps = {}, {}
    given = {name: _np.ascontiguousarray(inputs[name]) for name in _PARAMS}
    given["c_ctx"] = given["c_ctx"].reshape(1, D)
    for name, v in {**given, **shape_constants()}.items():
        if name.startswith("k_"):
            v = _np.ascontiguousarray(v, _np.float32)
        arrays[f"in_{name}"] = v
        aps[name] = nc.dram_tensor(f"in_{name}", v.shape, _mybir.dt.from_np(v.dtype), kind="ExternalInput").ap()
    out = nc.dram_tensor("out", (1, N, D), _mybir.dt.float32, kind="ExternalOutput").ap()
    block_program(nc, aps, out)
    r = _run(nc, [arrays], core_ids=[0])
    return r.results[0]["out"]
```

```python
import math
from contextlib import ExitStack

import numpy as np

import concourse.bass as bass
from concourse import mybir

F32 = mybir.dt.float32
BF16 = mybir.dt.bfloat16
F32R = mybir.dt.float32r
I32 = mybir.dt.int32
ALU = mybir.AluOpType
ACT = mybir.ActivationFunctionType
AX = mybir.AxisListType

P = 128
D = 1024
KC = D // P
N = 256
TC = N // P
E = 16
CAP = 32
RING = 6
SLOT = 4096
FF = 4096
EPS = 1e-6
SUBLN_EPS = 1e-5
LAM_INIT = 0.8 - 0.6 * math.exp(-0.3)
NEG = -1e30
TWO_PI = 2.0 * math.pi
ROUND = 12582912.0
PI_A = 6.28125
PI_B = float(np.float32(np.float64(TWO_PI) - PI_A).view(np.uint32) & np.uint32(0xFFFFF000))
PI_B = float(np.array([int(PI_B)], np.uint32).view(np.float32)[0])
PI_C = float(np.float32(np.float64(TWO_PI) - PI_A - PI_B))
PI_SAFE = 3.1415925


def shape_constants():
    f = np.float32
    ident = np.eye(P, dtype=f)
    iota = np.tile(np.arange(1, CAP + 1, dtype=f), (P, 1))
    row = np.arange(P)
    inv_mla = (10000.0 ** (-np.arange(0, 64, 2, dtype=f) / f(64))).astype(f)
    inv_ret = (10000.0 ** (-np.arange(0, 256, 2, dtype=f) / f(256))).astype(f)
    invf = np.stack([inv_mla[row % 32], inv_ret[row]], axis=1)
    base = np.concatenate([ident, iota, invf], axis=1)

    t = np.arange(N)
    theta = TWO_PI * (np.arange(N) + 0.5) / (2 * N)
    fwd = np.concatenate([np.cos(np.outer(t, theta)), -np.sin(np.outer(t, theta))], axis=1)
    fwd = fwd.reshape(TC, P, 2 * N).transpose(1, 0, 2)
    m = t + N // 2
    inv = np.concatenate([np.cos(np.outer(theta, m)), -np.sin(np.outer(theta, m))], axis=0) / N
    inv = inv.reshape(4, P, N).transpose(1, 0, 2)
    bands = np.linspace(1e-4, 15, 16).astype(f)
    ang = (f(TWO_PI / N) * t.astype(f)[:, None] * bands[None]).astype(f)
    z = np.concatenate([np.linspace(0, 1, N).astype(f)[:, None], np.cos(ang), -np.sin(ang)], axis=1)
    zt = np.zeros((P, N), f)
    zt[:33] = z.T
    dist = np.abs(t - N // 2) / (N // 2)
    rates = np.abs(np.linspace(math.log(1e-2) / 1.5, math.log(1e-2) / 0.3, 512))
    decay = np.exp(-dist[:, None] * rates[None]).reshape(TC, P, 512).transpose(1, 0, 2)
    hyena = np.concatenate([fwd.reshape(P, -1), inv.reshape(P, -1), decay.reshape(P, -1), zt], axis=1)

    inv16 = (10000.0 ** (-np.arange(16, dtype=f) / f(16))).astype(f)
    feat = row % 64
    pos = np.where((feat < 32)[:, None], (t // 64)[None], (t % 64)[None]).astype(f)
    a = (pos * inv16[feat % 16][:, None]).astype(f)
    swap = np.zeros((P, P), f)
    for r in range(P):
        if r % 32 < 16:
            swap[r + 16, r] = -1.0
        else:
            swap[r - 16, r] = 1.0
    half = (row[:, None] // 64 == row[None] // 64).astype(f)
    axial = np.concatenate([np.cos(a), np.sin(a), swap, half], axis=1)

    mswap = np.zeros((P, 64), f)
    for r in range(64):
        if r < 32:
            mswap[r + 32, r] = -1.0
        else:
            mswap[r - 32, r] = 1.0
    causal = np.stack([np.where(t[None] <= (qc * P + row)[:, None], 0.0, NEG) for qc in range(TC)], axis=1)
    mla = np.concatenate([mswap, causal.reshape(P, -1)], axis=1)

    q_all, q_late = np.arange(N), np.arange(P, N)
    strict = np.concatenate([np.where(row[:, None] < q_all[None], 0.0, NEG),
                             np.where((row + P)[:, None] < q_late[None], 0.0, NEG)], axis=1)
    suffix = (row[:, None] >= row[None]).astype(f)
    stick = np.concatenate([strict, suffix], axis=1)

    gam = np.log(f(1.0) - f(2.0) ** (f(-5.0) - np.arange(4, dtype=f))).astype(f)
    ret = []
    for h in range(4):
        for keys, qs in ((row, q_all), (row + P, q_late)):
            diff = (qs[None] - keys[:, None]).astype(np.float64)
            ret.append(np.where(diff >= 0, np.exp(np.maximum(diff, 0) * gam[h]), 0.0) / 16.0)
    ret = np.concatenate(ret, axis=1)
    return {
        "k_base": base, "k_hyena": hyena, "k_axial": axial,
        "k_mla": mla, "k_stick": stick, "k_ret": ret,
    }


CONST_WIDTH = {"k_base": 162, "k_hyena": 3328, "k_axial": 768, "k_mla": 576,
               "k_stick": 512, "k_ret": 1536}
_PARAMS = [
    "x", "c", "ctx", "c_ctx", "w_ada", "b_ada", "g_mix", "g_ffn", "w_in_ab", "conv_a", "conv_b",
    "conv_b_bias", "ln_b_g", "ln_b_b", "w_out_ab", "w_in_cd", "g_q", "g_k", "lam_q1", "lam_k1",
    "lam_q2", "lam_k2", "g_subln", "conv_d", "hf_w1", "hf_b1", "hf_freq", "hf_w2", "hf_b2", "hf_w3",
    "hf_bias", "w_out_cd", "w_router", "w_gate", "w_up", "w_down", "c_2", "positions_2", "ada_w_2",
    "ada_b_2", "norm_g_2", "ffn_w1_2", "ffn_w2_2", "mla_w_in_2", "mla_q_norm_2", "mla_kv_norm_2",
    "mla_w_q_up_2", "mla_w_kv_up_2", "mla_w_out_2", "sb_w_in_2", "sb_w_out_2", "ret_w_in_2",
    "ret_gn_g_2", "ret_w_out_2",
]


class Mark:

    def __init__(self, sem, at, step=0):
        self.sem, self.at, self.step = sem, at, step

    def wait(self, eng, it=0):
        eng.wait_ge(self.sem, self.at + it * self.step if self.step else self.at)


class Fill:

    def __init__(self, bank, full, free, before, step):
        self.bank, self.before, self.step = bank, before, step
        self.full, self.free = Mark(full, before + 1, step), Mark(free, before + 1, step)

    def open(self, pe, it=0):
        if self.step:
            pe.wait_ge(self.free.sem, self.before + it * self.step)
        elif self.before:
            pe.wait_ge(self.free.sem, self.before)


class Unit:

    def __init__(self, slot, landed, before, step, width, src):
        self.slot, self.width, self.src = slot, width, src
        self.landed = Mark(landed, 16 * (before + 1), 16 * step)
        self.used = None


class Quarter:

    def __init__(self, unit, kind, n):
        self.unit, self.kind, self.n, self.fills, self.used = unit, kind, n, [], None

    def part(self, store):
        v = store[:, self.unit.slot, 0:SLOT]
        if self.kind == "rows":
            return v.rearrange("p (k n) -> p k n", k=KC)[:, :, self.n * P:(self.n + 1) * P]
        if self.kind == "deep":
            k = 8 * (self.n % 2)
            return v.rearrange("p (k n) -> p k n", k=16)[:, k:k + 8, (self.n // 2) * P:(self.n // 2 + 1) * P]
        return v.rearrange("p (q k n) -> p q k n", q=4, k=KC)[:, self.n]


def block_program(nc, a, out, LAST=8):
    with ExitStack() as ctx:
        def sb(name, shape, dt=F32):
            return ctx.enter_context(nc.sbuf_tensor(name, shape, dt))

        def sem(name):
            return ctx.enter_context(nc.semaphore(name))

        ring_at = -(-nc.sbuf_base // 32) * 32
        ring = sb("ring", [P, RING, SLOT])
        arena_at = ring_at + 4 * RING * SLOT
        arena = sb("arena", [P, 22528])
        hT = sb("hT", [P, KC, 2 * N])
        PS = ctx.enter_context(nc.psum_tensor("banks", [P, 8, 512], F32))
        base = sb("base", [P, CONST_WIDTH["k_base"]])
        ident, iota, invf = base[:, 0:P], base[:, P:P + CAP], base[:, P + CAP:P + CAP + 2]
        ones = sb("ones", [P, P])
        zeros_bf = sb("zeros_bf", [P, P], BF16)

        VEC = {}
        vec_rows = []

        def vec(name, view, rows, width=P, at=0):
            if name not in VEC:
                VEC[name] = (vec.n, rows)
                vec.n += rows
            vec_rows.append((VEC[name][0], view, rows, width, at))
        vec.n = 0
        r128 = lambda ap: ap.rearrange("a (k p) -> (a k) p", p=P)
        vec("b_ada", r128(a["b_ada"]), 96)
        vec("ada_b_2", r128(a["ada_b_2"]), 192)
        vec("g_mix", r128(a["g_mix"]), 16)
        vec("g_ffn", r128(a["g_ffn"]), 16)
        vec("norm_g", a["norm_g_2"].rearrange("l n (k p) -> (l n k) p", p=P), 128)
        vec("conv_a", a["conv_a"].rearrange("a j (k p) -> (a j k) p", p=P), 12)
        vec("conv_b", a["conv_b"].rearrange("a j (k p) -> (a j k) p", p=P), 124)
        vec("conv_d", a["conv_d"].rearrange("a j (k p) -> (a j k) p", p=P), 36)
        for nm, n in (("conv_b_bias", 4), ("ln_b_g", 4), ("ln_b_b", 4), ("hf_bias", 4), ("g_subln", 1),
                      ("mla_q_norm_2", 4), ("mla_kv_norm_2", 2), ("ret_gn_g_2", 16)):
            vec(nm, r128(a[nm]), n)
        for nm in ("g_q", "g_k"):
            vec(nm, a[nm], 1, 64, 0)
            vec(nm, a[nm], 1, 64, 64)
        for nm in ("hf_b1", "hf_freq", "hf_b2", "lam_q1", "lam_k1", "lam_q2", "lam_k2"):
            vec(nm, a[nm], 1, 64)
        NV = vec.n
        NVR = -(-NV // P)
        V = sb("V", [P, NV])
        MOD = sb("MOD", [P, 2 * 96 + 4 * 48])
        AM = sb("AM", [P, 2 * 32 + 4 * 16])
        GP = sb("GP", [P, 4, 2, KC])
        c_raw = sb("c_raw", [P, 3, KC])
        cond = sb("cond", [P, KC, 32])
        small = sb("small", [P, 24])
        stat8 = sb("stat8", [P, 64])

        def col(name, i=0):
            return V[:, VEC[name][0] + i:VEC[name][0] + i + 1]

        def cols(name, i, n):
            return V[:, VEC[name][0] + i:VEC[name][0] + i + n]

        def mod(layer, part, k, s=0):
            if layer < 2:
                i = layer * 96 + (part * KC + k) * 2 + s
            else:
                i = 192 + (layer - 2) * 48 + part * KC + k
            return MOD[:, i:i + 1]

        def gain(layer, which, k, s=0):
            if layer < 2:
                i = layer * 32 + which * 16 + k * 2 + s
            else:
                i = 64 + (layer - 2) * 16 + which * 8 + k
            return AM[:, i:i + 1]

        def region(at, shape, dt=None):
            n = int(np.prod(shape))
            v = arena[:, at:at + n]
            if len(shape) == 1:
                return v
            names = "abcdef"[:len(shape)]
            dims = {names[i]: shape[i] for i in range(1, len(shape))}
            return v.rearrange(f"p ({' '.join(names)}) -> p {' '.join(names)}", **dims)

        def region_r(name, at, shape):
            return nc.alloc_sbuf_tensor_at(name, [P] + shape, F32R, offset=arena_at + 4 * at)

        ring_lo = nc.alloc_sbuf_tensor_at("ring_lo", [P, RING, SLOT], F32R, offset=ring_at)

        uT = region(0, [KC, 2 * N])
        W = 4096
        SQ = region(18432 + 2560, [2, 512])
        RS = region(18432 + 3584, [512])

        uT_r = region_r("uT_r", 0, [KC, 2 * N])
        x_lo, x_hi = uT_r[:, :, 0:N], uT_r[:, :, N:2 * N]
        hT_r = nc.alloc_sbuf_tensor_at("hT_r", [P, KC, 2 * N], F32R, offset=arena_at + 4 * 22528)
        half_slots = [hT_r[:, 4 * i:4 * i + 4, N:2 * N] for i in range(2)]
        mla_slots = [region_r(f"mla_w{i}", W + 5376 + 1024 * i, [KC, P]) for i in range(4)]
        st_in_slots = [region_r(f"st_in_w{i}", W + 10240 + 1024 * i, [KC, P]) for i in range(4)]
        st_out_slots = [region_r(f"st_out_w{i}", W + 4096 + 1024 * i, [KC, P]) for i in range(4)]
        rt_in_slots = [region_r("rt_in_w", W + 13824, [KC, P])] + half_slots
        rt_out_slots = [region_r("rt_out_w", W + 14848, [KC, P])] + half_slots

        bank_full = [sem(f"bank_full{b}") for b in range(8)]
        bank_free = [sem(f"bank_free{b}") for b in range(8)]
        landed = [sem(f"landed{s}") for s in range(RING)]
        sems = {}

        def S(name):
            if name not in sems:
                sems[name] = sem(name)
            return sems[name]

        bank_uses = [0] * 8
        slot_uses = [0] * RING
        plan = {}
        stream = []

        def fills(name, banks, rounds=1):
            per = {b: banks.count(b) for b in set(banks)}
            seen = {b: 0 for b in per}
            got = []
            for b in banks:
                got.append(Fill(b, bank_full[b], bank_free[b], bank_uses[b] + seen[b],
                                per[b] if rounds > 1 else 0))
                seen[b] += 1
            for b in per:
                bank_uses[b] += per[b] * rounds
            plan[name] = got
            return got

        def load(slots, sources, rounds=1, looped=True):
            per = {s: slots.count(s) for s in set(slots)}
            seen = {s: 0 for s in per}
            got = []
            for s, (width, src) in zip(slots, sources):
                got.append(Unit(s, landed[s], slot_uses[s] + seen[s], per[s] if rounds > 1 else 0, width, src))
                seen[s] += 1
            for s in per:
                slot_uses[s] += per[s] * rounds
            stream.append((rounds, looped, got))
            return got

        cursor = [0]

        def turn(n):
            got = [(cursor[0] + i) % RING for i in range(n)]
            cursor[0] = (cursor[0] + n) % RING
            return got

        def col_units(w, n0, n1, width=512, k=KC):
            v = w.rearrange("(k p) n -> p k n", p=P)
            return [(k * width, (lambda it, j=j: v[:, :, j:j + width])) for j in range(n0, n1, width)]

        def wview(u, k):
            return ring[:, u.slot, 0:u.width].rearrange("p (k n) -> p k n", k=k)

        ada_w = [a["w_ada"][0], a["w_ada"][1]] + [a["ada_w_2"][i] for i in range(4)]

        def plan_ada(name, layer, half, banks):
            f_rows = fills(f"ada_{name}_rows", banks[0:2] * 3)
            f_cols = fills(f"ada_{name}_cols", banks[2:4] * 3)
            v = ada_w[layer].rearrange("(p k) n -> p k n", p=P)
            src = [(SLOT, (lambda it, j=j: v[:, :, half * 3072 + j * 512:half * 3072 + (j + 1) * 512]))
                   for j in range(6)]
            us = load(turn(6), src)
            for u, f in zip(us, f_rows):
                u.used = f.full
            plan[f"ada_{name}"] = us

        plan_ada("l0a", 0, 0, [0, 1, 2, 3])
        fills("setup", ([0, 1, 2, 3] * 3)[:8 + -(-NVR // 4)])
        fills("lam", [0])
        plan_ada("l0b", 0, 1, [0, 1, 2, 3])
        BETWEEN = (("l1a", 1, 0), ("l1b", 1, 1), ("b0a", 2, 0), ("b0b", 2, 1))

        def plan_norm(name):
            fills(name, [7])

        def plan_moe(l, ns):
            p = f"moe{l}_"
            plan_norm(p + "norm")
            fills(p + "logit", [0])
            fills(p + "affT", [1])
            fills(p + "slots", [1])
            fills(p + "utok", [2, 3, 4, 5] * ns)
            fills(p + "gather", [0, 1, 2, 3] * 2 * ns)
            fills(p + "selT", [4, 5] * ns)
            slots = turn(6)
            units = []
            for j in range(4):
                gsrc = [(SLOT, (lambda it, j=j, w=w, h=h: w.rearrange("e (k p) n -> p e k n", p=P)
                                [:, it * 4 + j, :, h * 512:(h + 1) * 512]))
                        for w in (a["w_gate"][l], a["w_up"][l]) for h in range(2)]
                dsrc = [(SLOT, (lambda it, j=j, r=r: a["w_down"][l].rearrange("e (r k p) n -> p e r k n", p=P, k=4)
                                [:, it * 4 + j, r])) for r in range(2)]
                units += gsrc + dsrc
            us = load([slots[i % 6] for i in range(24)], units, 4)
            fs = fills(p + "experts", [0, 1, 2, 3, 4, 5, 6, 7] * 2, 4)
            for j in range(4):
                g, u, t, d = fs[4 * j:4 * j + 4]
                for i, f in enumerate((g, g, u, u, d, d)):
                    us[6 * j + i].used = f.full
            plan[p + "units"] = us
            fills(p + "combine", [0, 1, 2, 3] * 2 * ns)

        def use_dense(name, units, per_unit, banks):
            fs = fills(name, banks)
            for i, u in enumerate(units):
                u.used = fs[per_unit * (i + 1) - 1].full
            plan[name + "_units"] = units

        splits = {"n": 0, "used": 0}

        def use_split(name, units, kind, banks, slots, chain=None):
            per_fill = {"rows": 1, "deep": 2, "tokens": 4}[kind]
            fs = fills(name, banks)
            quarters = []
            before = list(plan[chain + "_quarters"]) if chain else []
            for i, u in enumerate(units):
                for n in range(4):
                    q = Quarter(u, kind, n)
                    splits["n"] += 1
                    q.at = splits["n"]
                    if (n + 1) % per_fill:
                        splits["used"] += 1
                        q.used = Mark(S("dense_used"), splits["used"])
                    elif kind == "tokens":
                        q.fills = fs[2 * i:2 * i + 2]
                        q.used = q.fills[1].full
                    else:
                        q.fills = [fs[(4 * i + n) // per_fill]]
                        q.used = q.fills[0].full
                    q.at_fill = 2 * i if kind == "tokens" else (4 * i + n) // per_fill
                    q.before = before[-len(slots)] if len(before) >= len(slots) else None
                    q.turn = (before[-1].turn + 1) % len(slots) if before else 0
                    q.slot = slots[q.turn]
                    before.append(q)
                    quarters.append(q)
                u.used = q.used
            plan[name + "_quarters"] = quarters

        if LAST >= 1:
            plan_norm("ab_norm")
            w_ab = a["w_in_ab"][0]
            AB_ORDER = (3, 4, 1, 2, 0)
            ab_units = []
            for n, j in enumerate(AB_ORDER):
                ab_units += load(turn(1), col_units(w_ab, j * 512, (j + 1) * 512))
                if n < 4:
                    plan_ada(*BETWEEN[n], [4, 5, 6, 7])
            use_dense("ab_in", ab_units, 4, [0, 1, 2, 3] * 5)
            fills("ab_mean", [4])
            fills("ab_var", [5])
            use_dense("ab_out", load(turn(2), col_units(a["w_out_ab"][0], 0, D)), 4, [0, 1, 2, 3] * 2)
        if LAST >= 2:
            plan_moe(0, 2)

        if LAST >= 3:
            plan_norm("cd_norm")
            fills("hf_mlp", [0, 1])
            fills("hf_tok", [2, 3])
            fills("hf_freq", [0, 1, 2, 3])
            w_cd = a["w_in_cd"][0]
            hy_cols = (2048, 2560, 1536)
            use_dense("hy_in", load(turn(3), [col_units(w_cd, c, c + 512)[0] for c in hy_cols]), 4, [0, 1, 2, 3] * 3)
            fills("hy_utok", [4, 5])
            fills("hy_ufreq", [0, 1, 2, 3])
            fills("hy_out", [4, 5] * 2)
            use_dense("qk_in", load(turn(2), col_units(w_cd, 0, 1024)), 4, [0, 1, 2, 3] * 2)
            use_dense("v_in", load(turn(1), col_units(w_cd, 1024, 1536)), 4, [4, 5, 6, 7])
            fills("qk_ms", [0, 1, 2, 3] * 2)
            fills("qk_rot", [4, 5, 6, 7] * 2)
            fills("da_scores", [0, 1, 2, 3] * 4)
            fills("da_turn", [4, 5] * 4)
            fills("da_out", [6, 7] * 2)
            fills("da_sub", [4, 5] * 2)
            use_dense("cd_out", load(turn(2), col_units(a["w_out_cd"][0], 0, D)), 4, [0, 1, 2, 3] * 2)
        if LAST >= 4:
            plan_moe(1, 1)

        KINDS = ("mla", "stick", "ret", "mla")
        for i, kind in enumerate(KINDS[:max(0, LAST - 4)]):
            p = f"b{i}_"
            plan_norm(p + "norm")
            if kind == "mla":
                j = i // 3
                win = a["mla_w_in_2"][j].rearrange("(k p) n -> p k n", p=P)
                wq = a["mla_w_q_up_2"][j].rearrange("(k p) n -> p k n", p=P)
                wkv = a["mla_w_kv_up_2"][j].rearrange("(k p) n -> p k n", p=P)
                us = load(turn(3), [(KC * 448, lambda it, v=win: v), (2 * 1536, lambda it, v=wq: v),
                                    (2048, lambda it, v=wkv: v)])
                f = fills(p + "lat", [0, 1, 2, 3])
                us[0].used = f[-1].full
                fills(p + "ms", [4, 5])
                fills(p + "kper", [6])
                f = fills(p + "qup", [0, 1, 2, 3] * 4)
                us[1].used = f[-1].full
                fills(p + "qrot", [4, 5] * 2)
                f = fills(p + "kvup", [0, 1, 2, 3] * 3)
                us[2].used = f[-1].full
                plan[p + "units"] = us
                fills(p + "scores", [0, 1, 6, 7] * 4)
                fills(p + "turn", [2, 3] * 8)
                fills(p + "pv", [4, 5] * 4)
                use_split(p + "out", load(turn(2), col_units(a["mla_w_out_2"][j], 0, D)), "rows", [0, 1, 2, 3] * 2,
                          mla_slots)
            elif kind == "stick":
                w = a["sb_w_in_2"][0]
                use_split(p + "qk", load(turn(4), col_units(w, 0, 2048)), "rows", [0, 1, 2, 3] * 4, st_in_slots)
                use_split(p + "v", load(turn(2), col_units(w, 2048, 3072)), "tokens", [4, 5] * 2, st_in_slots, p + "qk")
                fills(p + "z", [0, 1] * 8)
                fills(p + "suf", [2, 3] * 8)
                fills(p + "pv", [4, 5] * 4)
                use_split(p + "out", load(turn(2), col_units(a["sb_w_out_2"][0], 0, D)), "rows", [0, 1, 2, 3] * 2,
                          st_out_slots)
            else:
                w = a["ret_w_in_2"][0]
                use_split(p + "qk", load(turn(4), col_units(w, 0, 2048)), "rows", [0, 1, 2, 3] * 4, rt_in_slots)
                use_split(p + "v", load(turn(4), col_units(w, 2048, 4096)), "tokens", [4, 5] * 4, rt_in_slots, p + "qk")
                use_split(p + "g", load(turn(4), col_units(w, 4096, 6144)), "rows", [0, 1, 2, 3] * 4, rt_in_slots, p + "v")
                fills(p + "s", [4, 5] * 2)
                fills(p + "pv", [0, 1, 2, 3] * 4)
                fills(p + "ms", [6, 7] * 2)
                use_split(p + "out", load(turn(4), col_units(a["ret_w_out_2"][0], 0, D, 256, 16)), "deep",
                          [0, 1, 2, 3] * 2, rt_out_slots)
            plan_norm(p + "post")
            plan_norm(p + "fnorm")
            more = i < 3
            c0 = cursor[0]
            s = [(c0 + q) % RING for q in range(RING)]
            w1 = a["ffn_w1_2"][i].rearrange("(k p) n -> p k n", p=P)
            w2 = a["ffn_w2_2"][i].rearrange("(g k p) n -> p g k n", p=P, k=4)
            f1 = lambda g: (SLOT, lambda it, v=w1, g=g: v[:, :, bass.ds(it * 1024 + g * 512, 512)])
            f2 = lambda g: (SLOT, lambda it, v=w2, g=g: v[:, it * 2 + g])
            items, slots = [f1(0), f1(1), f2(0), f2(1)], [s[0], s[2], s[1], s[3]]
            if more:
                wa = ada_w[i + 3].rearrange("(p k) n -> p k n", p=P)
                fa = lambda q: (SLOT, lambda it, v=wa, q=q: v[:, :, bass.ds(it * 1536 + q * 512, 512)])
                items = [f1(0), fa(0), f1(1), fa(1), f2(0), fa(2), f2(1)]
                slots = [s[0], s[4], s[2], s[5], s[1], s[4], s[3]]
            us = load(slots, items, 4)
            fu = fills(p + "up", [0, 1] * 4, 4)
            if more:
                fr = fills(p + "ada_rows", [2] * 3, 4)
                fc = fills(p + "ada_cols", [3] * 3, 4)
                w1u, w2u, au = [us[0], us[2]], [us[4], us[6]], [us[1], us[3], us[5]]
                for u, f in zip(au, fr):
                    u.used = f.full
                plan[p + "ada_units"] = au
            else:
                w1u, w2u = us[0:2], us[2:4]
            w1u[0].used, w1u[1].used = fu[3].full, fu[7].full
            for g in range(2):
                w2u[g].used = Mark(S("ffn_down_used"), 36 * i + 4 + 4 * (g + 1), 8)
            plan[p + "w1"], plan[p + "w2"] = w1u, w2u
            fills(p + "down", [4, 5, 6, 7])
            plan_norm(p + "fpost")
        fills("final", [0, 1, 2, 3])

        x_tok = region(W, [2, TC, D])
        v_rows = region(W + 4096, [NVR, P])
        ada_rows = region(18432, [3, 512])
        ffn_h = region(W, [2, 4, N])
        ffn_h_lo = region_r("ffn_h_lo", W, [2, 4, N])
        ffn_h_hi = region_r("ffn_h_hi", 16384, [2, 4, N])
        w_hi = region_r("w_hi", 8192, [4, KC, P])
        u_hi, u_lo = (region_r(f"u_{part}", 12288 + 2048 * i, [KC, N]) for i, part in enumerate(("hi", "lo")))
        y_T = region(W + 2048, [KC, N])
        out_tok = region(W, [TC, D])

        vec_copies = []
        for r0, view, rows, width, at in vec_rows:
            i = 0
            while i < rows:
                n = min(rows - i, P - (r0 + i) % P)
                ch_, r = (r0 + i) // P, (r0 + i) % P
                vec_copies.append((v_rows[r:r + n, ch_, at:at + width], view[i:i + n, :]))
                i += n
        vec_dmas = len(vec_copies)
        one_col = ones[:, 0:1]
        zero_row = zeros_bf[:, :].unsqueeze(1).to_broadcast([P, 4, P])

        def counters():
            return {"sq": 0, "rs": 0, "u": 0, "t": 0, "sq_hist": [], "used": 0, "split": 0}

        def stat_act(act, c, chunks, fill, width, rows=P):
            for i, (src, ready) in enumerate(chunks):
                if ready is not None:
                    ready.wait(act)
                k = c["sq"]
                if k >= 2:
                    c["sq_hist"][k - 2].wait(act)
                nc.scalar.activation(SQ[:, k % 2, 0:width], src, ACT.Square).then_inc(S("sq_ready"), 1)
                c["sq"] += 1
                if i < len(chunks) - 1:
                    c["used"] += 1
                    c["sq_hist"].append(Mark(S("sq_used"), c["used"]))
                else:
                    c["sq_hist"].append(fill.full)

        def stat_pe(pe, c, n, fill, width, lhs=None):
            fill.open(pe)
            for i in range(n):
                k = c["sq"]
                pe.wait_ge(S("sq_ready"), k + 1)
                mm = nc.tensor.matmul(PS[:, fill.bank, 0:width], (ones[:, :] if lhs is None else lhs),
                                      SQ[:, k % 2, 0:width], start=(i == 0), stop=(i == n - 1))
                mm.then_inc(S("sq_used") if i < n - 1 else fill.full.sem, 1)
                c["sq"] += 1

        def rsqrt_act(act, c, fill, width, count, eps_at=0, dst=None):
            dst = RS if dst is None else dst
            fill.full.wait(act)
            nc.scalar.activation(dst[:, 0:width], PS[:, fill.bank, 0:width], ACT.Ln, scale=1.0 / count,
                                 bias=small[:, 9 + eps_at:10 + eps_at]).then_inc(fill.free.sem, 1)
            fill.free.wait(act)
            nc.scalar.activation(dst[:, 0:width], dst[:, 0:width], ACT.Exp, scale=-0.5).then_inc(S("rs_ready"), 1)

        def log_exp_tables():
            nc.scalar.preload_act_table_set("natural_log_exp_and_others")

        def rsqrt_wait(dve, c):
            c["rs"] += 1
            dve.wait_ge(S("rs_ready"), c["rs"])

        def scale_dve(dve, c, layer, which, ns):
            for k in range(KC):
                for s in range(ns):
                    t = slice(s * N, (s + 1) * N)
                    nc.vector.scalar_tensor_tensor(uT[:, k, t], hT[:, k, t], gain(layer, which, k, s), RS[:, t],
                                                   ALU.mult, ALU.mult).then_inc(S("u_scaled"), 1)

        def shift_act(act, c, layer, which, ns, split=False):
            for k in range(KC):
                for s in range(ns):
                    t = slice(s * N, (s + 1) * N)
                    c["u"] += 1
                    act.wait_ge(S("u_scaled"), c["u"])
                    if split:
                        nc.scalar.activation((u_hi if split == "ffn" else x_hi)[:, k, :], uT[:, k, t], ACT.Identity, bias=mod(layer, 3 * which, k, s))
                    nc.scalar.activation(uT[:, k, t], uT[:, k, t], ACT.Identity,
                                         bias=mod(layer, 3 * which, k, s)).then_inc(S("u_ready"), 1)

        def h_chunks(n):
            return [Mark(S("h_done"), KC * (n - 1) + k + 1) for k in range(KC)]

        def u_ready(pe, c, ns):
            c["u"] += KC * ns
            pe.wait_ge(S("u_ready"), c["u"])

        def norm_act(act, c, name, layer, which, ns, first=None, split=False):
            width = ns * N
            marks = first if isinstance(first, list) else [first] + [None] * (KC - 1)
            stat_act(act, c, [(hT[:, k, 0:width], marks[k]) for k in range(KC)],
                     plan[name][0], width)
            rsqrt_act(act, c, plan[name][0], width, D)
            shift_act(act, c, layer, which, ns, split)

        def norm_pe(pe, c, name, ns, split=False):
            stat_pe(pe, c, KC, plan[name][0], ns * N)
            if split:
                c["u"] += KC
                c["split"] += 1
            else:
                u_ready(pe, c, ns)

        def norm_dve(dve, c, name, layer, which, ns, split=False):
            rsqrt_wait(dve, c)
            if not split:
                scale_dve(dve, c, layer, which, ns)
                c["u"] += KC * ns
                return
            hi, lo = (u_hi, u_lo) if split == "ffn" else (x_hi, x_lo)
            for k in range(KC + 2):
                if k < KC:
                    nc.vector.scalar_tensor_tensor(uT[:, k, 0:N], hT[:, k, 0:N], gain(layer, which, k), RS[:, 0:N],
                                                   ALU.mult, ALU.mult).then_inc(S("u_scaled"), 1)
                if k >= 2:
                    c["u"] += 1
                    dve.wait_ge(S("u_ready"), c["u"])
                    nc.vector.tensor_tensor(lo[:, k - 2, :], uT[:, k - 2, 0:N], hi[:, k - 2, :].bitcast(F32),
                                            ALU.subtract).then_inc(S("u_split"), 1)

        def dense_pe(pe, name, rhs, width, per_unit, k=KC, between=None):
            units, fs = plan[name + "_units"], plan[name]
            for i, u in enumerate(units):
                w = wview(u, k)
                u.landed.wait(pe)
                for m in range(per_unit):
                    f = fs[i * per_unit + m]
                    f.open(pe)
                    for q in range(k):
                        mm = nc.tensor.matmul(PS[:, f.bank, 0:width], w[:, q, m * P:(m + 1) * P], rhs(i, q),
                                              start=(q == 0), stop=(q == k - 1))
                    mm.then_inc(f.full.sem, 1)
                if between is not None:
                    between(i)

        def token_pe(pe, name, tchunks):
            units, fs = plan[name + "_units"], plan[name]
            for i, u in enumerate(units):
                w = wview(u, KC)
                u.landed.wait(pe)
                for t in range(tchunks):
                    f = fs[i * tchunks + t]
                    f.open(pe)
                    for q in range(KC):
                        mm = nc.tensor.matmul(PS[:, f.bank, :], uT[:, q, t * P:(t + 1) * P], w[:, q, :],
                                              start=(q == 0), stop=(q == KC - 1))
                    mm.then_inc(f.full.sem, 1)

        def quarter(p, n):
            u = plan[p + ("w1" if n < 8 else "w2")][n // 4 % 2]
            both = []
            for store in (ring, ring_lo):
                v = store[:, u.slot, 0:u.width]
                if n < 8:
                    both.append(v.rearrange("p (k n) -> p k n", k=KC)[:, :, (n % 4) * P:(n % 4 + 1) * P])
                else:
                    both.append(v.rearrange("p (q k n) -> p q k n", q=4, k=KC)[:, n % 4])
            return u, both[0], both[1]

        def slot_free(eng, i, n, it):
            if 4 <= n < 12:
                plan[f"b{i}_up"][n - 4].full.wait(eng, it)
            else:
                eng.wait_ge(S("ffn_down_used"), 36 * i + (n + 1 if n < 4 else n - 7) + it * 8)

        def like(slot, v):
            return v if slot.shape[1] == KC else v.rearrange("p (k two) n -> p k two n", two=2)

        def whole(slot):
            return slot[:, :, :] if slot.shape[1] == KC else slot.rearrange("p k (two n) -> p k two n", two=2)

        def chunk(slot, k, n=1):
            if slot.shape[1] == KC:
                return slot[:, k, :] if n == 1 else slot[:, k:k + n, :]
            c0 = (k % 2) * P
            return slot[:, k // 2, c0:c0 + P] if n == 1 else slot[:, k // 2, :] if n == 2 else slot[:, k // 2:k // 2 + n // 2, :]

        def split_act(act, names, evacuate):
            qs = [q for name in names for q in plan[name + "_quarters"]]
            fs = [(name, m, f) for name in names for m, f in enumerate(plan[name])]
            done = [0]

            def close(q):
                for _ in q.fills:
                    evacuate(*fs[done[0]])
                    done[0] += 1

            ahead = {id(q.before): q for q in qs if q.before is not None}
            for q in qs:
                if q.before is not None:
                    q.before.used.wait(act)
                q.unit.landed.wait(act)
                nc.scalar.copy(whole(q.slot), like(q.slot, q.part(ring))).then_inc(S("dense_hi"), 1)
                if q.before is not None:
                    close(q.before)
            for q in qs:
                if id(q) not in ahead:
                    close(q)

        def split_dve(dve, names, closed=None):
            qs = [q for name in names for q in plan[name + "_quarters"]]
            fs = [(name, m, f) for name in names for m, f in enumerate(plan[name])]
            done = [0]

            def close(q):
                for _ in q.fills:
                    if closed:
                        closed(*fs[done[0]])
                    done[0] += 1

            ahead = {id(q.before): q for q in qs if q.before is not None}
            for q in qs:
                dve.wait_ge(S("dense_hi"), q.at)
                nc.vector.tensor_tensor(like(q.slot, q.part(ring_lo)), like(q.slot, q.part(ring)),
                                        whole(q.slot).bitcast(F32), ALU.subtract).then_inc(S("dense_lo"), 1)
                if q.before is not None:
                    close(q.before)
            for q in qs:
                if id(q) not in ahead:
                    close(q)

        def split_pe(pe, name, hi=None, lo=None, chunks=None):
            hi = hi or (lambda q: x_hi[:, q, :])
            lo = lo or (lambda q: x_lo[:, q, :])
            for q in plan[name + "_quarters"]:
                w_lo = q.part(ring_lo)
                pe.wait_ge(S("dense_lo"), q.at)
                if q.kind == "tokens":
                    for t in range(TC):
                        f = plan[name][q.at_fill + t]
                        if q.n == 0:
                            f.open(pe)
                        for k in range(2):
                            kk = 2 * q.n + k
                            ts = slice(t * P, (t + 1) * P)
                            low = w_lo[:, 4 * k:4 * k + 4, :]
                            for step, (x, w) in enumerate(((hi(kk), chunk(q.slot, 4 * k, 4)), (hi(kk), low),
                                                           (lo(kk), chunk(q.slot, 4 * k, 4)))):
                                mm = nc.tensor.matmul(PS[:, f.bank, :], x[:, ts], w, start=(kk == 0 and step == 0),
                                                      stop=(kk == KC - 1 and step == 2))
                        if q.n == 3:
                            mm.then_inc(f.full.sem, 1)
                    if q.n < 3:
                        mm.then_inc(q.used.sem, 1)
                    continue
                f = plan[name][q.at_fill]
                part = q.n % 2 if q.kind == "deep" else 0
                last = q.kind == "rows" or part == 1
                if part == 0:
                    f.open(pe)
                for k in range(KC):
                    kk = 8 * part + k
                    if chunks is not None and q is plan[name + "_quarters"][0]:
                        pe.wait_ge(S("u_split"), chunks + k + 1)
                    for step, (w, x) in enumerate(((chunk(q.slot, k), hi(kk)), (chunk(q.slot, k), lo(kk)),
                                                   (w_lo[:, k, :], hi(kk)))):
                        mm = nc.tensor.matmul(PS[:, f.bank, 0:N], w, x, start=(kk == 0 and step == 0),
                                              stop=(last and k == KC - 1 and step == 2))
                mm.then_inc(q.used.sem, 1)

        def copy_act(act, f, dst, src):
            f.full.wait(act)
            nc.scalar.copy(dst, src).then_inc(f.free.sem, 1)

        class Chain:

            def __init__(self, eng, sem_):
                self.eng, self.sem, self.n = eng, sem_, 0

            def put(self, ins):
                ins.then_inc(self.sem, 1)
                self.n += 1
                return self.n

            def sync(self, back=0):
                if self.n - back > 0:
                    self.eng.wait_ge(self.sem, self.n - back)

            def do(self, ins):
                self.put(ins)
                self.sync()

        def residual_dve(ch, name, layer, part, ns, width=N, s_of=None):
            for m, f in enumerate(plan[name]):
                f.full.wait(ch.eng)
                for s in range(ns):
                    t = slice(s * N, (s + 1) * N)
                    ins = nc.vector.scalar_tensor_tensor(hT[:, m, t], PS[:, f.bank, t], mod(layer, part, m, s),
                                                         hT[:, m, t], ALU.mult, ALU.add)
                    if s == ns - 1:
                        ins.then_inc(f.free.sem, 1)

        block = ctx.enter_context(nc.Block())

        ab_z = region(W, [4, 512])
        ab_gin = region(W + 2048, [4, 512])
        ab_val = region(W + 4096, [4, 512])
        ab_gout = region(W + 6144, [4, 512])
        ab_gv = region(W + 8192, [4, 2, N + 2])
        ab_zin = region(W + 10256, [4, 2, N + 30])
        ab_sg = region(W + 12544, [2, 512])
        ab_mu = region(W + 13568, [512])
        v512 = lambda ap: ap.rearrange("p (s t) -> p s t", s=2)

        moe_utok = region(4096, [4, D])
        moe_xe = region(8192, [KC, E, 2, CAP])
        moe_y = region(0, [2, 4, D])
        moe_selT = region(16384, [2, 4, N])
        moe_sel = region(18432, [4, E, CAP])
        moe_selw = region(20480, [4, E, CAP])
        moe_left = region(16384, [2, N])
        moe_take, moe_slot = region(16896, [N]), region(17152, [N])
        moe_wr = region(17408, [KC, E])
        moe_e, moe_aff = (region(17664 + 64 * i, [4, E]) for i in range(2))
        moe_top = region(17856, [8])
        moe_byc = region(17888, [64])
        moe_mx, moe_sm = (region(17984 + 4 * i, [4]) for i in range(2))
        x_cur = region(18432, [2, KC, 2 * CAP])
        x_sil = region(19456, [2, 512])
        x_act = region(20480, [2, 512])
        x_actT = region(21504, [2, 4, P])

        hy_const = region(W, [3328])
        hy_fwd = hy_const[:, 0:1024].rearrange("p (t f) -> p t f", t=TC)
        hy_inv = hy_const[:, 1024:2048].rearrange("p (q t) -> p q t", q=4)
        hy_decay = hy_const[:, 2048:3072].rearrange("p (t c) -> p t c", t=TC)
        hy_zt = hy_const[:, 3072:3328]
        hf_w1, hf_w2, hf_w3 = region(W + 3328, [64]), region(W + 3392, [64]), region(W + 3456, [512])
        hf_x, hf_k = region(W + 3968, [N]), region(W + 4224, [N])
        hf_tok = region(W + 4736, [TC, 512])
        hf_F = region(W + 5760, [4, 512])
        hy_p = region(W + 7808, [12, N + 2])
        hy_z = region(W + 10904, [12, N])
        hy_utok = region(W + 13976, [TC, 512])
        hy_Y = region(W + 7808, [4, 512])
        hy_t = region(W + 9856, [2, 512])
        hy_y = region(W + 15200, [4, N])

        da_const = region(W, [768])
        da_cos, da_sin = da_const[:, 0:N], da_const[:, N:2 * N]
        da_swap, da_half = da_const[:, 512:640], da_const[:, 640:768]
        da_qk = region(W + 768, [8, 512])
        da_v = region(W + 4864, [4, 512])
        da_sq = region(W + 6912, [8, 512])
        da_rs = region(W + 11008, [8, 512])
        da_p = region(W + 6912, [2, 2, 512])
        da_aT = region(W + 8960, [2, 4, N])
        da_o = region(W + 11008, [4, N])
        da_a = region(W + 12032, [2, 512])
        da_rso = region(W + 13056, [4, N])

        yv = y_T
        rope_tab = region(W + 15872, [4, N])
        rope_x, rope_k = region(W + 4096, [N]), region(W + 4352, [N])
        pos_i = region(W + 4608, [N]).bitcast(I32)
        pos_f = region(W + 4864, [N])
        ml_const = region(W, [576])
        ml_swap = ml_const[:, 0:64]
        ml_causal = ml_const[:, 64:576].rearrange("p (q k) -> p q k", q=TC)
        ml_s = region(W + 576, [4, N])
        ml_pT = region(W + 1600, [2, 2, N])
        ml_qlat = region(W + 4096, [2, N])
        ml_kvlat = region(W + 4608, [N])
        ml_kpe, ml_kt = region(W + 4864, [N]), region(W + 5120, [N])
        ml_qn = region(W + 5376, [8, N])
        ml_qpe = region(W + 7424, [8, N])
        ml_qt = region(W + 9472, [8, N])
        ml_kn = region(W + 11520, [8, N])
        ml_v = region(W + 13568, [2, D])
        ml_o = region(W + 9472, [8, N])
        ml_o_lo = region_r("ml_o_lo", W + 9472, [8, N])
        st_const = region(W, [512])
        st_mask, st_suffix = st_const[:, 0:384], st_const[:, 384:512]
        st_qk = region(W + 4096, [16, N])
        st_v = region(W + 8192, [2, D])
        st_t, st_sp = region(W + 10240, [4, 384]), region(W + 11776, [4, 384])
        st_o = region(W + 13312, [8, N])
        st_o_lo = region_r("st_o_lo", W + 13312, [8, N])
        rt_decay = region(W, [4, 384])
        rt_g = region(W + 1536, [16, N])
        rt_qk = region(W + 5632, [16, N])
        rt_v = region(W + 9728, [2, 2048])
        rt_s = region(W + 13824, [4, 384])
        rt_rs = region(W + 13824, [4, N])
        rt_t = region(W + 15360, [2, N])
        rt_o = region(W + 5632, [16, N])
        rt_o_lo = region_r("rt_o_lo", W + 5632, [16, N])
        rt_o_hi = region_r("rt_o_hi", W + 9728, [16, N])
        n_mla = {0: 0, 3: 1}
        mla_scale = (128 + 64) ** -0.5

        @block.sync
        def _(sp):
            users = {}

            def send(u, it, waits):
                for w, at in waits:
                    w.wait(sp, at)
                shape = u.src(it)
                dst = ring[:, u.slot, 0:u.width]
                if len(shape.shape) == 3:
                    dst = dst.rearrange("p (k n) -> p k n", k=shape.shape[1])
                sp.dma_start(dst, shape).then_inc(u.landed.sem, 16)

            for rounds, looped, units in stream:
                for u in units:
                    w = users.get(u.slot)
                    send(u, 0, [w] if w else [])
                    users[u.slot] = (u.used, 0)
                if rounds > 1:
                    before = []
                    last = {}
                    for i, u in enumerate(units):
                        before.append(last.get(u.slot))
                        last[u.slot] = u

                    def later(it):
                        for u, b in zip(units, before):
                            send(u, it, [(b.used, it) if b is not None else (last[u.slot].used, it - 1)])

                    if looped:
                        with sp.Fori(1, rounds) as it:
                            later(it)
                    else:
                        for it in range(1, rounds):
                            later(it)
                    for s, u in last.items():
                        users[s] = (u.used, rounds - 1)
            sp.wait_ge(S("out_ready"), TC)
            for t in range(TC):
                sp.dma_start(out.rearrange("b (t p) d -> p (b t) d", p=P)[:, t, :], out_tok[:, t, :])\
                    .then_inc(S("out_sent"), 16)
            sp.wait_ge(S("out_sent"), 16 * TC)

        @block.tensor
        def _(pe):
            c = counters()

            def ada_rows_pe(u, f, it=0):
                w = wview(u, KC)
                u.landed.wait(pe, it)
                f.open(pe, it)
                for k in range(KC):
                    g = 32 * (k % 4)
                    mm = nc.tensor.matmul(PS[g:g + 32, f.bank, :], cond[:, k, :], w[:, k, :],
                                          start=(k < 4), stop=(k >= 4), skip_group_check=True)
                mm.then_inc(f.full.sem, 1)

            def ada_cols_pe(rows, f, buf, it=0):
                rows.free.wait(pe, it)
                f.open(pe, it)
                for q in range(4):
                    mm = nc.tensor.transpose(PS[:, f.bank, q * P:(q + 1) * P], ada_rows[:, buf, q * P:(q + 1) * P],
                                             ident)
                mm.then_inc(f.full.sem, 1)

            pe.wait_ge(S("cond_ready"), 3)
            pe.wait_ge(S("in_landed"), 16)

            def ada_pe(name, it=0):
                us, fr, fc = plan[f"ada_{name}"], plan[f"ada_{name}_rows"], plan[f"ada_{name}_cols"]
                for j in range(6):
                    ada_rows_pe(us[j], fr[j], it)
                    if j >= 1:
                        ada_cols_pe(fr[j - 1], fc[j - 1], (j - 1) % 3, it)
                ada_cols_pe(fr[5], fc[5], 2, it)

            ada_pe("l0a")
            pe.wait_ge(S("x_landed"), 32)
            fs = plan["setup"]
            i = 0
            for s in range(2):
                for t in range(TC):
                    for kq in range(2):
                        f = fs[i]
                        f.open(pe)
                        for q in range(4):
                            mm = nc.tensor.transpose(PS[:, f.bank, q * P:(q + 1) * P],
                                                     x_tok[:, s, t, (4 * kq + q) * P:(4 * kq + q + 1) * P], ident)
                        mm.then_inc(f.full.sem, 1)
                        i += 1
            pe.wait_ge(S("vec_landed"), 16 * vec_dmas)
            for j in range(0, NVR, 4):
                f = fs[i]
                f.open(pe)
                for q in range(min(4, NVR - j)):
                    mm = nc.tensor.transpose(PS[:, f.bank, q * P:(q + 1) * P], v_rows[:, j + q, :], ident)
                mm.then_inc(f.full.sem, 1)
                i += 1
            f = plan["lam"][0]
            pe.wait_ge(S("lam_prod"), 1)
            pe.wait_ge(S("cleared"), 5)
            f.open(pe)
            nc.tensor.matmul(PS[:, f.bank, 0:2], ones[:, :], small[:, 0:2], start=True, stop=True)\
                .then_inc(f.full.sem, 1)

            ada_pe("l0b")

            def moe_pe(l, ns):
                p = f"moe{l}_"
                norm_pe(pe, c, p + "norm", ns)
                pe.wait_ge(S("moe_const"), 16 * (l + 1))
                f = plan[p + "logit"][0]
                f.open(pe)
                for t in range(2 * ns):
                    for k in range(KC):
                        mm = nc.tensor.matmul(PS[:, f.bank, t * E:(t + 1) * E], uT[:, k, t * P:(t + 1) * P],
                                              moe_wr[:, k, :], start=(k == 0), stop=(k == KC - 1))
                mm.then_inc(f.full.sem, 1)
                for i, f in enumerate(plan[p + "utok"]):
                    t, kq = i // 2, i % 2
                    f.open(pe)
                    for q in range(4):
                        mm = nc.tensor.transpose(PS[:, f.bank, q * P:(q + 1) * P],
                                                 uT[:, 4 * kq + q, t * P:(t + 1) * P], ident)
                    mm.then_inc(f.full.sem, 1)
                rows = ns * E
                f = plan[p + "affT"][0]
                pe.wait_ge(S("moe_aff"), l + 1)
                f.open(pe)
                for t in range(TC):
                    mm = nc.tensor.transpose(PS[0:rows, f.bank, t * P:(t + 1) * P], moe_byc[:, t * rows:(t + 1) * rows], ident)
                mm.then_inc(f.full.sem, 1)
                f = plan[p + "slots"][0]
                pe.wait_ge(S("moe_slot"), l + 1)
                f.open(pe)
                for t in range(TC):
                    mm = nc.tensor.transpose(PS[:, f.bank, t * rows:(t + 1) * rows],
                                             moe_slot[0:rows, t * P:(t + 1) * P], ident[0:rows, 0:rows])
                mm.then_inc(f.full.sem, 1)
                pe.wait_ge(S("moe_sel"), (4 if l else 0) + 2 * ns)
                for f in plan[p + "utok"][-4:]:
                    f.free.wait(pe)
                for s in range(ns):
                    for k in range(KC):
                        f = plan[p + "gather"][s * KC + k]
                        f.open(pe)
                        for t in range(TC):
                            mm = nc.tensor.matmul(PS[:, f.bank, :], moe_utok[:, TC * s + t, k * P:(k + 1) * P],
                                                  moe_sel[:, TC * s + t].rearrange("p e c -> p (e c)"),
                                                  start=(t == 0), stop=(t == TC - 1))
                        mm.then_inc(f.full.sem, 1)
                pe.wait_ge(S("moe_selw"), (4 if l else 0) + 2 * ns)
                for t, f in enumerate(plan[p + "selT"]):
                    f.open(pe)
                    w = moe_selw[:, t].rearrange("p e c -> p (e c)")
                    for q in range(4):
                        mm = nc.tensor.transpose(PS[:, f.bank, q * P:(q + 1) * P], w[:, q * P:(q + 1) * P], ident)
                    mm.then_inc(f.full.sem, 1)
                us, fs = plan[p + "units"], plan[p + "experts"]
                with pe.Fori(0, 4) as it:
                    for j in range(4):
                        b = j % 2
                        fg, fu, ft, fd = fs[4 * j:4 * j + 4]
                        un = us[6 * j:6 * j + 6]
                        pe.wait_ge(S("x_cur"), 16 * l + j + 1 + it * 4)
                        for f, h0 in ((fg, 0), (fu, 2)):
                            f.open(pe, it)
                            un[h0].landed.wait(pe, it)
                            un[h0 + 1].landed.wait(pe, it)
                            for k in range(KC):
                                for h in range(2):
                                    mm = nc.tensor.matmul(PS[64 * h:64 * h + 64, f.bank, :], x_cur[:, b, k, :],
                                                          wview(un[h0 + h], KC)[:, k, :], start=(k == 0),
                                                          stop=(k == KC - 1), skip_group_check=True)
                            mm.then_inc(f.full.sem, 1)
                        fu.free.wait(pe, it)
                        ft.open(pe, it)
                        for q in range(4):
                            mm = nc.tensor.transpose(PS[:, ft.bank, q * P:(q + 1) * P],
                                                     x_act[:, b, q * P:(q + 1) * P], ident)
                        mm.then_inc(ft.full.sem, 1)
                        fd.open(pe, it)
                        un[4].landed.wait(pe, it)
                        un[5].landed.wait(pe, it)
                        ft.free.wait(pe, it)
                        for fc in range(8):
                            for h in range(2):
                                mm = nc.tensor.matmul(
                                    PS[64 * h:64 * h + 64, fd.bank, :],
                                    x_actT[:, b, fc % 4, (fc // 4) * 64:(fc // 4) * 64 + 64],
                                    wview(un[4 + fc // 4], 4)[:, fc % 4, h * 512:(h + 1) * 512],
                                    start=(fc == 0), stop=(fc == 7), skip_group_check=True)
                        mm.then_inc(fd.full.sem, 1)
                for f in plan[p + "selT"]:
                    f.free.wait(pe)
                for j in range(4):
                    fs[4 * j + 3].free.wait(pe, 3)
                for i, f in enumerate(plan[p + "combine"]):
                    s, m = i // KC, i % KC
                    f.open(pe)
                    for q in range(4):
                        mm = nc.tensor.matmul(PS[:, f.bank, 0:N], moe_y[:, s, q, m * P:(m + 1) * P],
                                              moe_selT[:, s, q, :], start=(q == 0), stop=(q == 3))
                    mm.then_inc(f.full.sem, 1)

            if LAST >= 1:
                norm_pe(pe, c, "ab_norm", 2)
                dense_pe(pe, "ab_in", lambda i, q: uT[:, q, :], 512, 4,
                         between=lambda i: ada_pe(BETWEEN[i][0]) if i < 4 else None)
                f = plan["ab_mean"][0]
                f.open(pe)
                for m in range(4):
                    pe.wait_ge(S("z_conv"), m + 1)
                    mm = nc.tensor.matmul(PS[:, f.bank, :], ones[:, :], ab_z[:, m, :], start=(m == 0), stop=(m == 3))
                mm.then_inc(f.full.sem, 1)
                stat_pe(pe, c, 4, plan["ab_var"][0], 512)
                pe.wait_ge(S("ya_ready"), 4)
                pe.wait_ge(S("yb_ready"), 4)
                dense_pe(pe, "ab_out", lambda i, q: ab_gin[:, q, :] if q < 4 else ab_z[:, q - 4, :], 512, 4)
            if LAST >= 2:
                moe_pe(0, 2)
            if LAST >= 3:
                pe.wait_ge(S("hy_const"), 64)
                for r in range(2):
                    f = plan["hf_mlp"][r]
                    f.open(pe)
                    if r == 0:
                        mm = nc.tensor.matmul(PS[0:64, f.bank, 0:N], hf_w1[0:33, :], hy_zt[0:33, :], start=True, stop=True)
                    else:
                        pe.wait_ge(S("hf_sin"), 1)
                        mm = nc.tensor.matmul(PS[0:64, f.bank, 0:N], hf_w2[0:64, :], hf_x[0:64, :], start=True, stop=True)
                    mm.then_inc(f.full.sem, 1)
                pe.wait_ge(S("hf_sin"), 2)
                for t in range(TC):
                    f = plan["hf_tok"][t]
                    f.open(pe)
                    nc.tensor.matmul(PS[:, f.bank, :], hf_x[0:64, t * P:(t + 1) * P], hf_w3[0:64, :],
                                     start=True, stop=True).then_inc(f.full.sem, 1)
                for f in plan["hf_tok"]:
                    f.free.wait(pe)

                def forward(fill_list, src):
                    for q, f in enumerate(fill_list):
                        f.open(pe)
                        for t in range(TC):
                            mm = nc.tensor.matmul(PS[:, f.bank, :], hy_fwd[:, t, q * P:(q + 1) * P], src[:, t, :],
                                                  start=(t == 0), stop=(t == TC - 1))
                        mm.then_inc(f.full.sem, 1)

                forward(plan["hf_freq"], hf_tok)
                norm_pe(pe, c, "cd_norm", 2)
                dense_pe(pe, "hy_in", lambda i, q: uT[:, q, 0:N], N, 4)
                pe.wait_ge(S("hy_u"), 4)
                for t, f in enumerate(plan["hy_utok"]):
                    f.open(pe)
                    for m in range(4):
                        mm = nc.tensor.transpose(PS[:, f.bank, m * P:(m + 1) * P], hy_z[:, m, t * P:(t + 1) * P], ident)
                    mm.then_inc(f.full.sem, 1)
                for f in plan["hy_utok"]:
                    f.free.wait(pe)
                forward(plan["hy_ufreq"], hy_utok)
                pe.wait_ge(S("hy_Y"), 4)
                for m, f in enumerate(plan["hy_out"]):
                    f.open(pe)
                    for q in range(4):
                        mm = nc.tensor.matmul(PS[:, f.bank, 0:N], hy_Y[:, q, m * P:(m + 1) * P], hy_inv[:, q, :],
                                              start=(q == 0), stop=(q == 3))
                    mm.then_inc(f.full.sem, 1)
                units, fs = plan["qk_in_units"], plan["qk_in"]
                for i, u in enumerate(units):
                    w, width = wview(u, KC), (N, 2 * N)[i]
                    u.landed.wait(pe)
                    for m in range(4):
                        f = fs[4 * i + m]
                        f.open(pe)
                        for q in range(KC):
                            mm = nc.tensor.matmul(PS[:, f.bank, 0:width], w[:, q, m * P:(m + 1) * P],
                                                  uT[:, q, 0:width], start=(q == 0), stop=(q == KC - 1))
                        mm.then_inc(f.full.sem, 1)
                token_pe(pe, "v_in", 4)
                pe.wait_ge(S("da_const"), 16)
                for i, f in enumerate(plan["qk_ms"]):
                    width = N if i < 4 else 2 * N
                    pe.wait_ge(S("qk_sq"), i + 1)
                    f.open(pe)
                    nc.tensor.matmul(PS[:, f.bank, 0:width], da_half, da_sq[:, i, 0:width], start=True, stop=True)\
                        .then_inc(f.full.sem, 1)
                for i, f in enumerate(plan["qk_rot"]):
                    pe.wait_ge(S("qk_n"), i + 1)
                    f.open(pe)
                    nc.tensor.matmul(PS[:, f.bank, 0:N], da_swap, da_qk[:, i, 0:N], start=True, stop=True)\
                        .then_inc(f.full.sem, 1)

                def scores(i):
                    h, qc = i // TC, i % TC
                    for j in range(2):
                        f = plan["da_scores"][2 * i + j]
                        f.open(pe)
                        r = slice(64 * j, 64 * j + 64)
                        nc.tensor.matmul(PS[:, f.bank, :], da_qk[r, h, qc * P:(qc + 1) * P], da_qk[r, 4 + h, :],
                                         start=True, stop=True).then_inc(f.full.sem, 1)

                def turn_probs(i):
                    f = plan["da_turn"][i]
                    pe.wait_ge(S("da_a"), i + 1)
                    f.open(pe)
                    for kc in range(4):
                        mm = nc.tensor.transpose(PS[:, f.bank, kc * P:(kc + 1) * P],
                                                 da_a[:, i % 2, kc * P:(kc + 1) * P], ident)
                    mm.then_inc(f.full.sem, 1)

                def out_head(h):
                    plan["da_turn"][2 * h].free.wait(pe)
                    plan["da_turn"][2 * h + 1].free.wait(pe)
                    f = plan["da_out"][h]
                    f.open(pe)
                    for kc in range(4):
                        mm = nc.tensor.matmul(PS[:, f.bank, 0:N], da_v[:, kc, h * P:(h + 1) * P],
                                              da_aT[:, h % 2, kc, :], start=(kc == 0), stop=(kc == 3))
                    mm.then_inc(f.full.sem, 1)

                pe.wait_ge(S("qk_rope"), 8)
                for f in plan["v_in"]:
                    f.free.wait(pe)
                scores(0)
                for i in range(8):
                    if i < 7:
                        scores(i + 1)
                    turn_probs(i)
                    if i % 2:
                        out_head(i // 2)
                for h in range(4):
                    stat_pe(pe, c, 1, plan["da_sub"][h], N)
                pe.wait_ge(S("da_o"), 4)
                pe.wait_ge(S("hy_y"), 4)
                dense_pe(pe, "cd_out", lambda i, q: da_o[:, q, :] if q < 4 else hy_y[:, q - 4, :], N, 4)
            if LAST >= 4:
                moe_pe(1, 1)

            def mla_pe(i):
                p, j = f"b{i}_", n_mla[i]
                us = plan[p + "units"]
                norm_pe(pe, c, p + "norm", 1)
                w = wview(us[0], KC)
                us[0].landed.wait(pe)
                for m, f in enumerate(plan[p + "lat"]):
                    rows = P if m < 3 else 64
                    f.open(pe)
                    for q in range(KC):
                        mm = nc.tensor.matmul(PS[0:rows, f.bank, 0:N], w[:, q, m * P:m * P + rows], uT[:, q, 0:N],
                                              start=(q == 0), stop=(q == KC - 1))
                    mm.then_inc(f.full.sem, 1)
                stat_pe(pe, c, 2, plan[p + "ms"][0], N)
                stat_pe(pe, c, 1, plan[p + "ms"][1], N)
                f = plan[p + "kper"][0]
                pe.wait_ge(S("ml_const"), 16 * (j + 1))
                plan[p + "lat"][3].free.wait(pe)
                f.open(pe)
                nc.tensor.matmul(PS[0:64, f.bank, 0:N], ml_swap[0:64, :], ml_kpe[0:64, :], start=True, stop=True)\
                    .then_inc(f.full.sem, 1)
                w = wview(us[1], 2)
                us[1].landed.wait(pe)
                plan[p + "lat"][0].free.wait(pe)
                plan[p + "lat"][1].free.wait(pe)
                for h in range(8):
                    for part, (o, rows) in enumerate(((0, P), (P, 64))):
                        f = plan[p + "qup"][2 * h + part]
                        f.open(pe)
                        for q in range(2):
                            mm = nc.tensor.matmul(PS[0:rows, f.bank, 0:N], w[:, q, h * 192 + o:h * 192 + o + rows],
                                                  ml_qlat[:, q, :], start=(q == 0), stop=(q == 1))
                        mm.then_inc(f.full.sem, 1)
                wkv = ring[:, us[2].slot, 0:2048].rearrange("p (h two e) -> p h two e", h=8, two=2)
                us[2].landed.wait(pe)
                plan[p + "lat"][2].free.wait(pe)
                for m, f in enumerate(plan[p + "kvup"]):
                    f.open(pe)
                    if m < 8:
                        mm = nc.tensor.matmul(PS[:, f.bank, 0:N], wkv[:, m, 0, :], ml_kvlat, start=True, stop=True)
                    else:
                        t, half = (m - 8) // 2, (m - 8) % 2
                        mm = nc.tensor.matmul(PS[:, f.bank, :], ml_kvlat[:, t * P:(t + 1) * P],
                                              wkv[:, 4 * half:4 * half + 4, 1, :], start=True, stop=True)
                    mm.then_inc(f.full.sem, 1)
                for r, f in enumerate(plan[p + "qrot"]):
                    plan[p + "qup"][4 * r + 1].free.wait(pe)
                    plan[p + "qup"][4 * r + 3].free.wait(pe)
                    f.open(pe)
                    nc.tensor.matmul(PS[0:64, f.bank, :], ml_swap[0:64, :],
                                     ml_qpe[0:64, 2 * r:2 * r + 2, :].rearrange("p h t -> p (h t)"),
                                     start=True, stop=True).then_inc(f.full.sem, 1)
                pe.wait_ge(S("ml_rope"), 5 * (j + 1))
                for f in plan[p + "kvup"][-4:] + plan[p + "qup"][-4:]:
                    f.free.wait(pe)

                def scores(i2):
                    h, qc = i2 // 2, i2 % 2
                    f = plan[p + "scores"][i2]
                    width = (qc + 1) * P
                    f.open(pe)
                    nc.tensor.matmul(PS[:, f.bank, 0:width], ml_qn[:, h, qc * P:(qc + 1) * P], ml_kn[:, h, 0:width],
                                     start=True, stop=False)
                    nc.tensor.matmul(PS[:, f.bank, 0:width], ml_qpe[0:64, h, qc * P:(qc + 1) * P],
                                     ml_kpe[0:64, 0:width], start=False, stop=True).then_inc(f.full.sem, 1)

                for s in range(16 + 5):
                    if s < 16:
                        scores(s)
                    if 3 <= s < 19:
                        i2 = s - 3
                        f = plan[p + "turn"][i2]
                        pe.wait_ge(S("ml_p"), 16 * j + i2 + 1)
                        f.open(pe)
                        for kc in range(i2 % 2 + 1):
                            mm = nc.tensor.transpose(PS[:, f.bank, kc * P:(kc + 1) * P],
                                                     ml_s[:, i2 % 4, kc * P:(kc + 1) * P], ident)
                        mm.then_inc(f.full.sem, 1)
                    if s >= 5 and s % 2 == 1 and s < 20:
                        i2, h = s - 4, (s - 4) // 2
                        if h == 0:
                            pe.wait_ge(S("pT_zero"), j + 1)
                        plan[p + "turn"][i2 - 1].free.wait(pe)
                        plan[p + "turn"][i2].free.wait(pe)
                        f = plan[p + "pv"][h]
                        f.open(pe)
                        for kc in range(2):
                            mm = nc.tensor.matmul(PS[:, f.bank, 0:N], ml_v[:, kc, h * P:(h + 1) * P],
                                                  ml_pT[:, h % 2, kc, :], start=(kc == 0), stop=(kc == 1))
                        mm.then_inc(f.full.sem, 1)
                for f in plan[p + "pv"][-2:]:
                    f.free.wait(pe)
                pe.wait_ge(S("x_lo"), 8 * (1 if j == 0 else 3))
                split_pe(pe, p + "out", lo=lambda q: ml_o_lo[:, q, :])

            def stick_pe(i):
                p = f"b{i}_"
                norm_pe(pe, c, p + "norm", 1, split=True)
                split_pe(pe, p + "qk", chunks=KC * (c["split"] - 1))
                split_pe(pe, p + "v")
                pe.wait_ge(S("st_const"), 16)
                for f in plan[p + "qk"][-4:] + plan[p + "v"][-2:]:
                    f.free.wait(pe)
                for s in range(16 + 3):
                    if s < 16:
                        h, r = s // 2, slice(64 * (s % 2), 64 * (s % 2) + 64)
                        f = plan[p + "z"][s]
                        f.open(pe)
                        nc.tensor.matmul(PS[:, f.bank, 0:N], st_qk[r, 8 + h, 0:P], st_qk[r, h, :], start=True, stop=True)
                        nc.tensor.matmul(PS[:, f.bank, N:384], st_qk[r, 8 + h, P:N], st_qk[r, h, P:N],
                                         start=True, stop=True).then_inc(f.full.sem, 1)
                    if 1 <= s <= 16:
                        k = s - 1
                        f = plan[p + "suf"][k]
                        pe.wait_ge(S("st_sp"), k + 1)
                        f.open(pe)
                        nc.tensor.matmul(PS[:, f.bank, 0:N], st_suffix, st_sp[:, k % 4, 0:N], start=True, stop=False)
                        nc.tensor.matmul(PS[:, f.bank, P:N], ones[:, :], st_sp[:, k % 4, N:384], start=False,
                                         stop=True)
                        nc.tensor.matmul(PS[:, f.bank, N:384], st_suffix, st_sp[:, k % 4, N:384], start=True,
                                         stop=True).then_inc(f.full.sem, 1)
                    if s >= 3:
                        k = s - 3
                        f = plan[p + "pv"][k // 2]
                        o = 64 * (k % 2)
                        pe.wait_ge(S("st_a"), k + 1)
                        if k % 2 == 0:
                            f.open(pe)
                        nc.tensor.matmul(PS[o:o + 64, f.bank, 0:N], st_v[:, 0, k * 64:k * 64 + 64],
                                         st_t[:, k % 4, 0:N], start=True, stop=False, skip_group_check=True)
                        nc.tensor.matmul(PS[o:o + 64, f.bank, P:N], st_v[:, 1, k * 64:k * 64 + 64],
                                         st_t[:, k % 4, N:384], start=False, stop=True, skip_group_check=True)\
                            .then_inc(f.full.sem if k % 2 else S("st_pv"), 1)
                for f in plan[p + "pv"][-2:]:
                    f.free.wait(pe)
                pe.wait_ge(S("x_lo"), 8 * 2)
                split_pe(pe, p + "out", lo=lambda q: st_o_lo[:, q, :])

            def ret_pe(i):
                p = f"b{i}_"
                norm_pe(pe, c, p + "norm", 1, split=True)
                split_pe(pe, p + "qk", chunks=KC * (c["split"] - 1))
                split_pe(pe, p + "v")
                split_pe(pe, p + "g")
                pe.wait_ge(S("rt_rope"), 8)
                for h in range(4):
                    f = plan[p + "s"][h]
                    f.open(pe)
                    for q in range(2):
                        nc.tensor.matmul(PS[:, f.bank, 0:N], rt_qk[:, 8 + 2 * h + q, 0:P], rt_qk[:, 2 * h + q, :],
                                         start=(q == 0), stop=(q == 1))
                    for q in range(2):
                        mm = nc.tensor.matmul(PS[:, f.bank, N:384], rt_qk[:, 8 + 2 * h + q, P:N],
                                              rt_qk[:, 2 * h + q, P:N], start=(q == 0), stop=(q == 1))
                    mm.then_inc(f.full.sem, 1)
                for f in plan[p + "v"][-2:]:
                    f.free.wait(pe)
                for h in range(4):
                    plan[p + "s"][h].free.wait(pe)
                    for vc in range(4):
                        f = plan[p + "pv"][4 * h + vc]
                        e = slice(h * 512 + vc * P, h * 512 + (vc + 1) * P)
                        f.open(pe)
                        nc.tensor.matmul(PS[:, f.bank, 0:N], rt_v[:, 0, e], rt_s[:, h, 0:N], start=True, stop=False)
                        nc.tensor.matmul(PS[:, f.bank, P:N], rt_v[:, 1, e], rt_s[:, h, N:384], start=False, stop=True)\
                            .then_inc(f.full.sem, 1)
                for h in range(4):
                    stat_pe(pe, c, 4, plan[p + "ms"][h], N)
                pe.wait_ge(S("rt_o_lo"), 16)
                split_pe(pe, p + "out", hi=lambda q: rt_o_hi[:, q, :], lo=lambda q: rt_o_lo[:, q, :])

            def ffn_pe(i):
                p = f"b{i}_"
                norm_pe(pe, c, p + "fnorm", 1, split=True)
                down = plan[p + "down"]
                for f in down:
                    f.open(pe)
                    nc.tensor.matmul(PS[:, f.bank, :], zeros_bf[:, :], zero_row, start=True, stop=False,
                                     skip_group_check=True).then_inc(S("ffn_down_used"), 1)
                fu = plan[p + "up"]
                more = i < 3
                with pe.Fori(0, 4) as it:
                    for n in range(16):
                        pe.wait_ge(S("ffn_w_lo"), 64 * i + n + 1 + it * 16)
                        hi, lo = w_hi[:, n % 4], quarter(p, n)[2]
                        if n < 8:
                            f = fu[n]
                            f.open(pe, it)
                            for q in range(KC):
                                if n == 0:
                                    pe.wait_ge(S("u_split"), KC * (c["split"] - 1) + q + 1)
                                for w, x in ((hi, u_hi), (hi, u_lo), (lo, u_hi)):
                                    mm = nc.tensor.matmul(PS[:, f.bank, 0:N], w[:, q, :], x[:, q, :],
                                                          start=(q == 0 and x is u_hi and w is hi),
                                                          stop=(q == KC - 1 and w is lo))
                            mm.then_inc(f.full.sem, 1)
                        else:
                            g, q = n // 4 - 2, n % 4
                            h_hi, h_lo = ffn_h_hi[:, g, q, :], ffn_h_lo[:, g, q, :]
                            pe.wait_ge(S("ffn_h_lo"), 32 * i + n - 7 + it * 8)
                            for m in range(KC):
                                for w, x in ((hi, h_hi), (hi, h_lo), (lo, h_hi)):
                                    mm = nc.tensor.matmul(PS[:, down[m // 2].bank, (m % 2) * N:(m % 2) * N + N],
                                                          w[:, m, :], x, start=False, stop=False,
                                                          skip_group_check=True)
                            mm.then_inc(S("ffn_down_used"), 1)
                        if more:
                            if n in (5, 7, 11):
                                q = (5, 7, 11).index(n)
                                ada_cols_pe(plan[p + "ada_rows"][q], plan[p + "ada_cols"][q], q, it)
                            if n in (3, 5, 9):
                                q = (3, 5, 9).index(n)
                                ada_rows_pe(plan[p + "ada_units"][q], plan[p + "ada_rows"][q], it)
                for f in down:
                    nc.tensor.matmul(PS[:, f.bank, :], zeros_bf[:, :], zero_row, start=False, stop=True,
                                     skip_group_check=True).then_inc(f.full.sem, 1)

            for i, kind in enumerate(KINDS[:max(0, LAST - 4)]):
                {"mla": mla_pe, "stick": stick_pe, "ret": ret_pe}[kind](i)
                stat_pe(pe, c, KC, plan[f"b{i}_post"][0], N)
                ffn_pe(i)
                stat_pe(pe, c, KC, plan[f"b{i}_fpost"][0], N)
            pe.wait_ge(S("h_final"), 1)
            for i, f in enumerate(plan["final"]):
                t, kq = i // 2, i % 2
                f.open(pe)
                for q in range(4):
                    mm = nc.tensor.transpose(PS[:, f.bank, q * P:(q + 1) * P], hT[:, 4 * kq + q, t * P:(t + 1) * P],
                                             ident)
                mm.then_inc(f.full.sem, 1)

        @block.scalar
        def _(act):
            c = counters()
            for n, nm in enumerate(("c", "c_ctx", "c_2")):
                act.dma_start(c_raw[:, n, :], a[nm].rearrange("a (p k) -> p (a k)", p=P)).then_inc(S("c_landed"), 16)
            act.dma_start(base[:, :], a["k_base"]).then_inc(S("in_landed"), 16)
            act.wait_ge(S("rows_zero"), 1)
            for dst, src in vec_copies:
                act.dma_start(dst, src).then_inc(S("vec_landed"), 16)
            act.dma_start(x_tok[:, 0], a["x"].rearrange("b (t p) d -> p (b t) d", p=P)).then_inc(S("x_landed"), 16)
            act.dma_start(x_tok[:, 1], a["ctx"].rearrange("b (t p) d -> p (b t) d", p=P)).then_inc(S("x_landed"), 16)
            act.wait_ge(S("cleared"), 5)
            act.wait_ge(S("c_landed"), 48)
            for n in range(3):
                nc.scalar.activation(cond[:, :, n], c_raw[:, n, :], ACT.Silu).then_inc(S("cond_ready"), 1)
            log_exp_tables()

            def rows_act(f, buf, it=0):
                f.full.wait(act, it)
                nc.scalar.copy(ada_rows[:, buf, :], PS[:, f.bank, :]).then_inc(f.free.sem, 1)

            def ada_act(name, it=0):
                for j in range(6):
                    rows_act(plan[f"ada_{name}_rows"][j], j % 3, it)

            ada_act("l0a")
            f = plan["lam"][0]
            f.full.wait(act)
            nc.scalar.activation(small[:, 2:4], PS[:, f.bank, 0:2], ACT.Exp).then_inc(f.free.sem, 1)
            ada_act("l0b")

            def moe_act(l, ns, ready):
                p = f"moe{l}_"
                norm_act(act, c, p + "norm", l, 1, ns, first=ready)
                act.dma_start(moe_wr, a["w_router"][l].rearrange("(k p) e -> p k e", p=P)).then_inc(S("moe_const"), 16)
                f = plan[p + "logit"][0]
                f.free.wait(act)
                nc.scalar.activation(moe_e[:, 0:2 * ns, :], moe_e[:, 0:2 * ns, :], ACT.Exp).then_inc(S("moe_exp"), 1)
                for i, f in enumerate(plan[p + "utok"]):
                    t, kq = i // 2, i % 2
                    copy_act(act, f, moe_utok[:, t, kq * 512:(kq + 1) * 512], PS[:, f.bank, :])
                for i, f in enumerate(plan[p + "gather"]):
                    s, k = i // KC, i % KC
                    if i % 2:
                        f.full.wait(act)
                        nc.scalar.copy(moe_xe[:, k, :, s, :], PS[:, f.bank, :].rearrange("p (e c) -> p e c", e=E))\
                            .then_inc(f.free.sem, 1)
                fs = plan[p + "experts"]
                with act.Fori(0, 4) as it:
                    for j in range(4):
                        fg, fu, ft, fd = fs[4 * j:4 * j + 4]
                        fg.full.wait(act, it)
                        nc.scalar.activation(x_sil[:, j % 2, :], PS[:, fg.bank, :], ACT.Silu).then_inc(fg.free.sem, 1)
                        fd.full.wait(act, it)
                        for s in range(ns):
                            for h in range(2):
                                r = 64 * h + 32 * s
                                ins = nc.scalar.copy(
                                    moe_y[32 * j:32 * j + 32, s, bass.ds(it, 1), h * 512:(h + 1) * 512].rearrange("p o n -> p (o n)"),
                                    PS[r:r + 32, fd.bank, :])
                        ins.then_inc(fd.free.sem, 1)
                log_exp_tables()

            if LAST >= 1:
                act.wait_ge(S("mod_ready"), 1)
                norm_act(act, c, "ab_norm", 0, 0, 2)
                fs = plan["ab_in"]
                for m in range(4):
                    copy_act(act, fs[m], ab_z[:, m, :], PS[:, fs[m].bank, :])
                ada_act(BETWEEN[0][0])
                for m in range(4):
                    f = fs[4 + m]
                    f.full.wait(act)
                    if m >= 2:
                        act.wait_ge(S("z_in"), m - 1)
                    nc.scalar.activation(ab_sg[:, m % 2, :], PS[:, f.bank, :], ACT.Sigmoid).then_inc(f.free.sem, 1)
                log_exp_tables()
                for g, dst in enumerate((ab_gin, ab_val, ab_gout)):
                    ada_act(BETWEEN[1 + g][0])
                    for m in range(4):
                        f = fs[8 + 4 * g + m]
                        copy_act(act, f, dst[:, m, :], PS[:, f.bank, :])
                stat_act(act, c, [(ab_z[:, m, :], Mark(S("z_centred"), m + 1)) for m in range(4)],
                         plan["ab_var"][0], 512)
                rsqrt_act(act, c, plan["ab_var"][0], 512, 512)
                for m in range(4):
                    act.wait_ge(S("z_normed"), m + 1)
                    nc.scalar.activation(ab_z[:, m, :], ab_z[:, m, :], ACT.Silu, bias=col("ln_b_b", m),
                                         scale=col("ln_b_g", m)).then_inc(S("yb_ready"), 1)
                log_exp_tables()
            if LAST >= 2:
                moe_act(0, 2, plan["ab_out"][-1].free)
            if LAST >= 3:
                plan["moe0_combine"][-1].free.wait(act)
                act.dma_start(hy_const, a["k_hyena"]).then_inc(S("hy_const"), 16)
                act.dma_start(hf_w1[0:33, :], a["hf_w1"][0]).then_inc(S("hy_const"), 16)
                act.dma_start(hf_w2[0:64, :], a["hf_w2"][0]).then_inc(S("hy_const"), 16)
                act.dma_start(hf_w3[0:64, :], a["hf_w3"][0]).then_inc(S("hy_const"), 16)
                for r in range(2):
                    act.wait_ge(S("hf_arg"), r + 1)
                    nc.scalar.activation(hf_x[0:64, :], hf_x[0:64, :], ACT.Sin).then_inc(S("hf_sin"), 1)
                log_exp_tables()
                for q, f in enumerate(plan["hf_freq"]):
                    copy_act(act, f, hf_F[:, q, :], PS[:, f.bank, :])
                norm_act(act, c, "cd_norm", 1, 0, 2)
                act.wait_ge(S("hp_pad"), 1)
                for i, f in enumerate(plan["hy_in"]):
                    copy_act(act, f, hy_p[:, i, 1:N + 1], PS[:, f.bank, 0:N])
                for t, f in enumerate(plan["hy_utok"]):
                    copy_act(act, f, hy_utok[:, t, :], PS[:, f.bank, :])
                plan["hy_out"][-1].full.wait(act)
                act.dma_start(da_const, a["k_axial"]).then_inc(S("da_const"), 16)
                act.wait_ge(S("hy_y"), 4)
                for i, f in enumerate(plan["qk_in"]):
                    width = N if i < 4 else 2 * N
                    f.full.wait(act)
                    nc.scalar.activation(da_sq[:, i, 0:width], PS[:, f.bank, 0:width], ACT.Square)\
                        .then_inc(S("qk_sq"), 1)
                    nc.scalar.copy(da_qk[:, i, 0:width], PS[:, f.bank, 0:width]).then_inc(f.free.sem, 1)
                for t, f in enumerate(plan["v_in"]):
                    copy_act(act, f, da_v[:, t, :], PS[:, f.bank, :])
                for i, f in enumerate(plan["qk_ms"]):
                    rsqrt_act(act, c, f, N if i < 4 else 2 * N, 64, dst=da_rs[:, i, :])

                def exps(i):
                    for j in range(2):
                        f = plan["da_scores"][2 * i + j]
                        act.wait_ge(S("da_nb"), 2 * i + j + 1)
                        if i >= 2:
                            act.wait_ge(S("da_a"), i - 1)
                        k = 2 * i + j
                        nc.scalar.activation(da_p[:, i % 2, j, :], PS[:, f.bank, :], ACT.Exp, scale=0.125,
                                             bias=stat8[:, 16 + k:17 + k], accum_out=stat8[:, 32 + k:33 + k])\
                            .then_inc(f.free.sem, 1)

                def turn_act(i):
                    f = plan["da_turn"][i]
                    h, qc = i // 2, i % 2
                    f.full.wait(act)
                    if h >= 2 and qc == 0:
                        plan["da_out"][h - 2].full.wait(act)
                    nc.scalar.copy(da_aT[:, h % 2, :, qc * P:(qc + 1) * P],
                                   PS[:, f.bank, :].rearrange("p (k q) -> p k q", k=4)).then_inc(f.free.sem, 1)

                exps(0)
                for i in range(8):
                    if i < 7:
                        exps(i + 1)
                    turn_act(i)
                    if i % 2:
                        f = plan["da_out"][i // 2]
                        copy_act(act, f, da_o[:, i // 2, :], PS[:, f.bank, 0:N])
                for h in range(4):
                    stat_act(act, c, [(da_o[:, h, :], plan["da_out"][h].free)], plan["da_sub"][h], N)
                    rsqrt_act(act, c, plan["da_sub"][h], N, P, eps_at=1, dst=da_rso[:, h, :])
            if LAST >= 4:
                moe_act(1, 1, plan["cd_out"][-1].free)

            def mla_act(i, ready):
                p, j = f"b{i}_", n_mla[i]
                lat = plan[p + "lat"]
                if j == 0:
                    ready.wait(act)
                    act.dma_start(pos_i, a["positions_2"].to_broadcast([P, N])).then_inc(S("pos"), 16)
                norm_act(act, c, p + "norm", i + 2, 0, 1, first=ready)
                if j == 0:
                    for r in range(4):
                        act.wait_ge(S("tab_arg"), r + 1)
                        nc.scalar.activation(rope_tab[:, r, :], rope_tab[:, r, :], ACT.Sin).then_inc(S("tab"), 1)
                    log_exp_tables()
                act.dma_start(ml_const, a["k_mla"]).then_inc(S("ml_const"), 16)
                stat_act(act, c, [(PS[:, lat[m].bank, 0:N], lat[m].full) for m in range(2)], plan[p + "ms"][0], N)
                stat_act(act, c, [(PS[:, lat[2].bank, 0:N], lat[2].full)], plan[p + "ms"][1], N)
                rsqrt_act(act, c, plan[p + "ms"][0], N, 256, dst=RS[:, 0:N])
                rsqrt_act(act, c, plan[p + "ms"][1], N, 128, dst=RS[:, N:2 * N])
                copy_act(act, lat[3], ml_kpe[0:64, :], PS[0:64, lat[3].bank, 0:N])
                for h in range(8):
                    f = plan[p + "qup"][2 * h]
                    copy_act(act, f, ml_qn[:, h, :], PS[:, f.bank, 0:N])
                    f = plan[p + "qup"][2 * h + 1]
                    copy_act(act, f, ml_qpe[0:64, h, :], PS[0:64, f.bank, 0:N])
                for m, f in enumerate(plan[p + "kvup"]):
                    if m < 8:
                        copy_act(act, f, ml_kn[:, m, :], PS[:, f.bank, 0:N])
                    else:
                        t, half = (m - 8) // 2, (m - 8) % 2
                        copy_act(act, f, ml_v[:, t, half * 512:(half + 1) * 512], PS[:, f.bank, :])

                def exps(i2):
                    width = (i2 % 2 + 1) * P
                    act.wait_ge(S("ml_nb"), 16 * j + i2 + 1)
                    nc.scalar.activation(ml_s[:, i2 % 4, 0:width], ml_s[:, i2 % 4, 0:width], ACT.Exp,
                                         bias=stat8[:, 16 + i2:17 + i2], accum_out=stat8[:, 32 + i2:33 + i2])\
                        .then_inc(S("ml_exp"), 1)

                act.wait_ge(S("pT_zero"), j + 1)
                for s in range(1, 16 + 6):
                    if s <= 16:
                        exps(s - 1)
                    if 4 <= s < 20:
                        i2 = s - 4
                        h, qc = i2 // 2, i2 % 2
                        f = plan[p + "turn"][i2]
                        if h >= 2 and qc == 0:
                            plan[p + "pv"][h - 2].full.wait(act)
                        copy_act(act, f, ml_pT[:, h % 2, 0:qc + 1, qc * P:(qc + 1) * P],
                                 PS[:, f.bank, 0:(qc + 1) * P].rearrange("p (k q) -> p k q", k=qc + 1))
                    if s >= 6 and s % 2 == 0:
                        f = plan[p + "pv"][(s - 6) // 2]
                        f.full.wait(act)
                        nc.scalar.copy(x_hi[:, (s - 6) // 2, :], PS[:, f.bank, 0:N])
                        copy_act(act, f, ml_o[:, (s - 6) // 2, :], PS[:, f.bank, 0:N])

            def stick_act(i, ready):
                p = f"b{i}_"
                norm_act(act, c, p + "norm", i + 2, 0, 1, first=ready, split="mixer")
                act.dma_start(st_const, a["k_stick"]).then_inc(S("st_const"), 16)

                def evacuate(name, m, f):
                    if name == p + "qk":
                        copy_act(act, f, st_qk[:, m, :], PS[:, f.bank, 0:N])
                    else:
                        copy_act(act, f, st_v[:, m % 2, (m // 2) * 512:(m // 2 + 1) * 512], PS[:, f.bank, :])

                split_act(act, [p + "qk", p + "v"], evacuate)
                for s in range(16 + 3):
                    if s < 16:
                        act.wait_ge(S("st_abs"), s + 1)
                        nc.scalar.activation(st_sp[:, s % 4, :], st_sp[:, s % 4, :], ACT.Exp, scale=-1.0)\
                            .then_inc(S("st_e"), 1)
                        act.wait_ge(S("st_e"), s + 1)
                        nc.scalar.activation(st_sp[:, s % 4, :], st_sp[:, s % 4, :], ACT.Ln, bias=one_col)\
                            .then_inc(S("st_l"), 1)
                    if 2 <= s <= 17:
                        k = s - 2
                        act.wait_ge(S("st_arg"), k + 1)
                        nc.scalar.activation(st_t[:, k % 4, :], st_t[:, k % 4, :], ACT.Exp).then_inc(S("st_a"), 1)
                    if s >= 4 and s % 2 == 0:
                        f = plan[p + "pv"][(s - 4) // 2]
                        f.full.wait(act)
                        nc.scalar.copy(x_hi[:, (s - 4) // 2, :], PS[:, f.bank, 0:N])
                        copy_act(act, f, st_o[:, (s - 4) // 2, :], PS[:, f.bank, 0:N])

            def ret_act(i, ready):
                p = f"b{i}_"
                norm_act(act, c, p + "norm", i + 2, 0, 1, first=ready, split="mixer")
                act.dma_start(rt_decay.rearrange("p h n -> p (h n)"), a["k_ret"]).then_inc(S("rt_const"), 16)

                def evacuate(name, m, f):
                    if name == p + "qk":
                        copy_act(act, f, rt_qk[:, m, :], PS[:, f.bank, 0:N])
                    elif name == p + "v":
                        copy_act(act, f, rt_v[:, m % 2, (m // 2) * 512:(m // 2 + 1) * 512], PS[:, f.bank, :])
                    else:
                        f.full.wait(act)
                        nc.scalar.activation(rt_g[:, m, :], PS[:, f.bank, 0:N], ACT.Silu).then_inc(f.free.sem, 1)

                split_act(act, [p + "qk", p + "v", p + "g"], evacuate)
                log_exp_tables()
                for m, f in enumerate(plan[p + "pv"]):
                    copy_act(act, f, rt_o[:, m, :], PS[:, f.bank, 0:N])
                for h in range(4):
                    stat_act(act, c, [(rt_o[:, 4 * h + q, :], plan[p + "pv"][4 * h + q].free) for q in range(4)],
                             plan[p + "ms"][h], N)
                    rsqrt_act(act, c, plan[p + "ms"][h], N, 512, dst=rt_rs[:, h, :])
                for m in range(16):
                    act.wait_ge(S("rt_o"), m + 1)
                    nc.scalar.copy(rt_o_hi[:, m, :], rt_o[:, m, :]).then_inc(S("rt_o_hi"), 1)

            def post_act(name_out, name, per):
                def evacuate(_, m, f):
                    w = per * N
                    copy_act(act, f, y_T[:, per * m:per * (m + 1), :].rearrange("p k t -> p (k t)"), PS[:, f.bank, 0:w])

                if per == 1:
                    split_act(act, [name_out], evacuate)
                else:
                    for m, f in enumerate(plan[name_out]):
                        evacuate(name_out, m, f)
                stat_act(act, c, [(y_T[:, k, :], plan[name_out][k // per].free) for k in range(KC)],
                         plan[name][0], N)
                rsqrt_act(act, c, plan[name][0], N, D)

            nh = 0
            ready = plan["moe1_combine"][-1].free if LAST >= 5 else None
            for i, kind in enumerate(KINDS[:max(0, LAST - 4)]):
                p = f"b{i}_"
                {"mla": mla_act, "stick": stick_act, "ret": ret_act}[kind](i, ready)
                post_act(p + "out", p + "post", 1)
                nh += 1
                norm_act(act, c, p + "fnorm", i + 2, 1, 1, first=h_chunks(nh), split="ffn")
                with act.Fori(0, 4) as it:
                    for n in range(16):
                        u, w, _ = quarter(p, n)
                        slot_free(act, i, n, it)
                        u.landed.wait(act, it)
                        nc.scalar.copy(w_hi[:, n % 4], w).then_inc(S("ffn_w_hi"), 1)
                        if 4 <= n < 12:
                            f = plan[p + "up"][n - 4]
                            f.full.wait(act, it)
                            nc.scalar.activation(ffn_h[:, n // 4 - 1, n % 4, :], PS[:, f.bank, 0:N], ACT.Relu)\
                                .then_inc(f.free.sem, 1)
                        if 5 <= n < 13:
                            k = n - 5
                            act.wait_ge(S("ffn_squared"), 32 * i + k + 1 + it * 8)
                            nc.scalar.copy(ffn_h_hi[:, k // 4, k % 4, :], ffn_h[:, k // 4, k % 4, :])\
                                .then_inc(S("ffn_h_hi"), 1)
                        if i < 3 and n in (8, 10, 14):
                            q = (8, 10, 14).index(n)
                            rows_act(plan[p + "ada_rows"][q], q, it)
                post_act(p + "down", p + "fpost", 2)
                nh += 1
                ready = h_chunks(nh)
                if i < 3:
                    act.wait_ge(S("mod_ready"), i + 2)

        @block.vector
        def _(dve):
            c = counters()
            ch = Chain(dve, S("dve_seq"))
            V_ = nc.vector
            TT, TS, STT = V_.tensor_tensor, V_.tensor_scalar, V_.scalar_tensor_tensor
            V_.memset(v_rows, 0.0).then_inc(S("rows_zero"), 1)
            def cols_dve(f, at, step, r0, n, it=0):
                f.full.wait(dve, it)
                src = PS[:, f.bank, :].rearrange("p (q j r) -> p q r j", q=4, j=4)[:, :, r0:r0 + n, :]
                dst = (MOD[:, bass.ds(it * step + at, 4 * n)] if step else MOD[:, at:at + 4 * n]).rearrange("p (q r) -> p q r", q=4)
                V_.tensor_reduce(dst, src, AX.X, ALU.add).then_inc(f.free.sem, 1)

            def gains_first(l):
                m = MOD[:, l * 96:l * 96 + 96].rearrange("p (i s) -> p i s", s=2)
                ch.do(TT(m, m, cols("b_ada", l * 48, 48).unsqueeze(2).to_broadcast([P, 48, 2]), ALU.add))
                for which, nm in ((0, "g_mix"), (1, "g_ffn")):
                    at = l * 96 + (3 * which + 1) * 16
                    g = cols(nm, l * KC, KC).unsqueeze(2).to_broadcast([P, KC, 2])
                    o = l * 32 + which * 16
                    ch.put(STT(AM[:, o:o + 16].rearrange("p (k s) -> p k s", s=2),
                               MOD[:, at:at + 16].rearrange("p (k s) -> p k s", s=2), 1.0, g, ALU.add, ALU.mult))
                ch.sync()

            def gains_second(i):
                at = 192 + i * 48
                ch.do(TT(MOD[:, at:at + 48], MOD[:, at:at + 48], cols("ada_b_2", i * 48, 48), ALU.add))
                for which in range(2):
                    o = 64 + i * 16 + which * 8
                    sc = at + (3 * which + 1) * 8
                    ch.put(STT(AM[:, o:o + 8], MOD[:, sc:sc + 8], 1.0, cols("norm_g", (i * 4 + 2 * which) * 8, 8),
                               ALU.add, ALU.mult))
                    ch.put(TT(GP[:, i, which, :], MOD[:, sc + 8:sc + 16], cols("norm_g", (i * 4 + 2 * which + 1) * 8, 8),
                              ALU.mult))
                ch.sync()
                ch.sync()

            for j, f in enumerate(plan["ada_l0a_cols"]):
                cols_dve(f, j * 8, 0, 0, 2)
            fs = plan["setup"]
            i = 0
            for s in range(2):
                for t in range(TC):
                    for kq in range(2):
                        f = fs[i]
                        f.full.wait(dve)
                        V_.tensor_copy(hT[:, 4 * kq:4 * kq + 4, s * N + t * P:s * N + (t + 1) * P],
                                       PS[:, f.bank, :].rearrange("p (k t) -> p k t", k=4)).then_inc(f.free.sem, 1)
                        i += 1
            for j in range(0, NVR, 4):
                f = fs[i]
                n = min(4 * P, NV - j * P)
                f.full.wait(dve)
                V_.tensor_copy(V[:, j * P:j * P + n], PS[:, f.bank, 0:n]).then_inc(f.free.sem, 1)
                i += 1
            for f in fs[8:]:
                f.free.wait(dve)
            TT(small[:, 0:1], col("lam_q1"), col("lam_k1"), ALU.mult).then_inc(S("lam_a"), 1)
            dve.wait_ge(S("lam_a"), 1)
            TT(small[:, 1:2], col("lam_q2"), col("lam_k2"), ALU.mult).then_inc(S("lam_prod"), 1)
            plan["lam"][0].free.wait(dve)
            ch.do(TT(small[:, 4:5], small[:, 3:4], small[:, 2:3], ALU.subtract))
            ch.do(TS(small[:, 5:6], small[:, 4:5], -LAM_INIT, None, ALU.add))
            ch.do(TS(small[:, 6:7], col("g_subln"), 1.0 - LAM_INIT, None, ALU.mult))

            for j, f in enumerate(plan["ada_l0b_cols"]):
                cols_dve(f, (6 + j) * 8, 0, 0, 2)
            for f in plan["ada_l0b_cols"][-2:]:
                f.free.wait(dve)
            gains_first(0)

            def ada_dve(n):
                name, layer, half = BETWEEN[n]
                cond_n, at = (2, 96) if layer == 1 else (1, 192)
                for j, f in enumerate(plan[f"ada_{name}_cols"]):
                    cols_dve(f, at + (half * 6 + j) * 4 * cond_n, 0, (0 if layer == 1 else 2), cond_n)
                if half:
                    for f in plan[f"ada_{name}_cols"][-2:]:
                        f.free.wait(dve)
                    if layer == 1:
                        gains_first(1)
                    else:
                        gains_second(0)

            TS(small[:, 7:8], small[:, 5:6], 1.0, None, ALU.mult).then_inc(S("mod_ready"), 1)

            def trig(x, k, rows, quarter):
                ch.do(TS(k, x, 1.0 / TWO_PI, 0.25 if quarter else 0.0, ALU.mult, ALU.add))
                ch.do(TS(k, k, ROUND, None, ALU.add))
                ch.do(TS(k, k, -ROUND, None, ALU.add))
                for part in (PI_A, PI_B, PI_C):
                    ch.do(STT(x, k, -part, x, ALU.mult, ALU.add))
                if quarter:
                    ch.do(TS(x, x, math.pi / 2, None, ALU.add))
                return TS(x, x, PI_SAFE, -PI_SAFE, ALU.min, ALU.max)

            def moe_dve(l, ns):
                p = f"moe{l}_"
                nt = 2 * ns
                norm_dve(dve, c, p + "norm", l, 1, ns)
                f = plan[p + "logit"][0]
                f.full.wait(dve)
                lg = PS[:, f.bank, 0:nt * E].rearrange("p (t e) -> p t e", t=nt)
                bc = lambda v: v[:, 0:nt].unsqueeze(2).to_broadcast([P, nt, E])
                ch.do(V_.tensor_reduce(moe_mx[:, 0:nt], lg, AX.X, ALU.max))
                TT(moe_e[:, 0:nt, :], lg, bc(moe_mx), ALU.subtract).then_inc(f.free.sem, 1)
                dve.wait_ge(S("moe_exp"), l + 1)
                ch.do(V_.tensor_reduce(moe_sm[:, 0:nt], moe_e[:, 0:nt, :], AX.X, ALU.add))
                ch.do(V_.reciprocal(moe_sm[:, 0:nt], moe_sm[:, 0:nt]))
                ch.put(TT(moe_aff[:, 0:nt, :], moe_e[:, 0:nt, :], bc(moe_sm), ALU.mult))
                TT(moe_byc[:, 0:nt * E].rearrange("p (t s e) -> p s t e", t=TC, s=ns),
                   moe_e[:, 0:nt, :].rearrange("p (s t) e -> p s t e", s=ns),
                   moe_sm[:, 0:nt].rearrange("p (s t) -> p s t", s=ns).unsqueeze(3).to_broadcast([P, ns, TC, E]),
                   ALU.mult).then_inc(S("moe_aff"), 1)
                dve.wait_ge(S("moe_aff"), l + 1)
                rows = ns * E
                f = plan[p + "affT"][0]
                f.full.wait(dve)
                V_.tensor_copy(moe_left[0:rows, 0, :], PS[0:rows, f.bank, 0:N]).then_inc(f.free.sem, 1)
                f.free.wait(dve)
                for r in range(CAP // 8):
                    ch.do(V_.max(moe_top[0:rows, :], moe_left[0:rows, r % 2, :]))
                    ch.do(V_.match_replace(moe_left[0:rows, (r + 1) % 2, :], moe_top[0:rows, :],
                                           moe_left[0:rows, r % 2, :], -1.0))
                ch.do(TS(moe_take[0:rows, :], moe_left[0:rows, 0, :], 0.0, None, ALU.is_lt))
                ch.do(V_.tensor_tensor_scan(moe_slot[0:rows, :], one_col[0:rows, :].to_broadcast([rows, N]),
                                            moe_take[0:rows, :], 0.0, ALU.mult, ALU.add))
                TT(moe_slot[0:rows, :], moe_slot[0:rows, :], moe_take[0:rows, :], ALU.mult).then_inc(S("moe_slot"), 1)
                f = plan[p + "slots"][0]
                f.full.wait(dve)
                for t in range(nt):
                    at = (t % 2) * rows + (t // 2) * E
                    ins = TT(moe_sel[:, t], iota.unsqueeze(1).to_broadcast([P, E, CAP]),
                             PS[:, f.bank, at:at + E].unsqueeze(2).to_broadcast([P, E, CAP]), ALU.is_equal)
                    ins.then_inc(S("moe_sel"), 1)
                dve.wait_ge(S("moe_sel"), (4 if l else 0) + nt)
                TS(moe_top[0:1, 0:1], moe_top[0:1, 0:1], 1.0, None, ALU.mult).then_inc(f.free.sem, 1)
                for t in range(nt):
                    TT(moe_selw[:, t], moe_sel[:, t], moe_aff[:, t].unsqueeze(2).to_broadcast([P, E, CAP]), ALU.mult)\
                        .then_inc(S("moe_selw"), 1)
                for i, f in enumerate(plan[p + "gather"]):
                    s, k = i // KC, i % KC
                    if i % 2 == 0:
                        f.full.wait(dve)
                        V_.tensor_copy(moe_xe[:, k, :, s, :], PS[:, f.bank, :].rearrange("p (e c) -> p e c", e=E))\
                            .then_inc(f.free.sem, 1)
                for t, f in enumerate(plan[p + "selT"]):
                    f.full.wait(dve)
                    V_.tensor_copy(moe_selT[:, t // 2, :, (t % 2) * P:(t % 2 + 1) * P],
                                   PS[:, f.bank, :].rearrange("p (q t) -> p q t", q=4)).then_inc(f.free.sem, 1)
                fs = plan[p + "experts"]
                with dve.Fori(0, 4) as it:
                    for j in range(4):
                        fg, fu, ft, fd = fs[4 * j:4 * j + 4]
                        fu.full.wait(dve, it)
                        fg.free.wait(dve, it)
                        TT(x_act[:, j % 2, :], x_sil[:, j % 2, :], PS[:, fu.bank, :], ALU.mult).then_inc(fu.free.sem, 1)
                        ft.full.wait(dve, it)
                        V_.tensor_copy(x_actT[:, j % 2].rearrange("p q t -> p (q t)"), PS[:, ft.bank, :])\
                            .then_inc(ft.free.sem, 1)
                for i, f in enumerate(plan[p + "combine"]):
                    s, m = i // KC, i % KC
                    t = slice(s * N, (s + 1) * N)
                    f.full.wait(dve)
                    STT(hT[:, m, t], PS[:, f.bank, 0:N], mod(l, 5, m, s), hT[:, m, t], ALU.mult, ALU.add)\
                        .then_inc(f.free.sem, 1)
                for f in plan[p + "combine"][-4:]:
                    f.free.wait(dve)

            if LAST >= 1:
                norm_dve(dve, c, "ab_norm", 0, 0, 2)
                dve.wait_ge(S("ab_pads"), 2)
                fs = plan["ab_in"]
                ada_dve(0)
                for m in range(4):
                    fs[m].free.wait(dve)
                    fs[4 + m].free.wait(dve)
                    TT(ab_zin[:, m, :, 15:15 + N], v512(ab_z[:, m, :]), v512(ab_sg[:, m % 2, :]), ALU.mult)\
                        .then_inc(S("z_in"), 1)
                for j in range(31):
                    if j in (0, 12, 24):
                        ada_dve(1 + j // 12)
                    for m in range(4):
                        src, w = ab_zin[:, m, :, j:j + N], col("conv_b", 4 * j + m)
                        dst = v512(ab_z[:, m, :])
                        if j == 0:
                            dve.wait_ge(S("z_in"), 4)
                            ch.put(TS(dst, src, w, col("conv_b_bias", m), ALU.mult, ALU.add))
                        else:
                            ch.sync(back=3)
                            ins = STT(dst, src, w, dst, ALU.mult, ALU.add)
                            if j < 30:
                                ch.put(ins)
                            else:
                                ins.then_inc(S("z_conv"), 1)
                                if m < 3:
                                    dve.wait_ge(S("dve_seq"), ch.n)
                for j in range(3):
                    for m in range(4):
                        if j == 0:
                            dve.wait_ge(S("ab_gv"), m + 1)
                            ch.put(TS(v512(ab_gin[:, m, :]), ab_gv[:, m, :, 0:N], col("conv_a", m), None, ALU.mult))
                        else:
                            ch.sync(back=3)
                            ch.put(STT(v512(ab_gin[:, m, :]), ab_gv[:, m, :, j:j + N], col("conv_a", 4 * j + m),
                                       v512(ab_gin[:, m, :]), ALU.mult, ALU.add))
                for m in range(4):
                    fs[16 + m].free.wait(dve)
                    ch.sync()
                    TT(ab_gin[:, m, :], ab_gin[:, m, :], ab_gout[:, m, :], ALU.mult).then_inc(S("ya_ready"), 1)
                f = plan["ab_mean"][0]
                f.full.wait(dve)
                TS(ab_mu, PS[:, f.bank, :], 1.0 / 512, None, ALU.mult).then_inc(f.free.sem, 1)
                f.free.wait(dve)
                dve.wait_ge(S("z_conv"), 4)
                for m in range(4):
                    TT(ab_z[:, m, :], ab_z[:, m, :], ab_mu, ALU.subtract).then_inc(S("z_centred"), 1)
                rsqrt_wait(dve, c)
                dve.wait_ge(S("z_centred"), 4)
                for m in range(4):
                    TT(ab_z[:, m, :], ab_z[:, m, :], RS[:, 0:512], ALU.mult).then_inc(S("z_normed"), 1)
                residual_dve(ch, "ab_out", 0, 2, 2)
                for f in plan["ab_out"][-4:]:
                    f.free.wait(dve)
            if LAST >= 2:
                moe_dve(0, 2)
            if LAST >= 3:
                for r in range(2):
                    f = plan["hf_mlp"][r]
                    f.full.wait(dve)
                    TS(hf_x[0:64, :], PS[0:64, f.bank, 0:N], col(("hf_b1", "hf_b2")[r])[0:64], col("hf_freq")[0:64],
                       ALU.add, ALU.mult).then_inc(f.free.sem, 1)
                    f.free.wait(dve)
                    trig(hf_x[0:64, :], hf_k[0:64, :], 64, False).then_inc(S("hf_arg"), 1)
                for t, f in enumerate(plan["hf_tok"]):
                    f.full.wait(dve)
                    TT(hf_tok[:, t, :], PS[:, f.bank, :], hy_decay[:, t, :], ALU.mult).then_inc(f.free.sem, 1)
                norm_dve(dve, c, "cd_norm", 1, 0, 2)
                orig = [4, 5, 6, 7, 8, 9, 10, 11, 0, 1, 2, 3]
                for g in range(3):
                    for j in range(3):
                        for m in range(4):
                            i = 4 * g + m
                            w = col("conv_d", j * 12 + orig[i])
                            if j == 0:
                                plan["hy_in"][i].free.wait(dve)
                                ch.put(TS(hy_z[:, i, :], hy_p[:, i, 0:N], w, None, ALU.mult))
                            else:
                                ch.sync(back=3)
                                ch.put(STT(hy_z[:, i, :], hy_p[:, i, j:j + N], w, hy_z[:, i, :], ALU.mult, ALU.add))
                    if g == 1:
                        ch.sync()
                        for m in range(4):
                            TT(hy_z[:, m, :], hy_z[:, m, :], hy_z[:, 4 + m, :], ALU.mult).then_inc(S("hy_u"), 1)
                fr = plan["hy_ufreq"]
                for fc in range(2):
                    re, im = PS[:, fr[fc].bank, :], PS[:, fr[2 + fc].bank, :]
                    fr[2 + fc].full.wait(dve)
                    plan["hf_freq"][2 + fc].free.wait(dve)
                    ch.sync()
                    dve.wait_ge(S("hy_u"), 4)
                    if fc:
                        dve.wait_ge(S("hy_Y"), 2)
                    ch.put(TT(hy_t[:, 0, :], re, hf_F[:, fc, :], ALU.mult))
                    ch.do(TT(hy_t[:, 1, :], im, hf_F[:, 2 + fc, :], ALU.mult))
                    TT(hy_Y[:, fc, :], hy_t[:, 0, :], hy_t[:, 1, :], ALU.subtract).then_inc(S("hy_Y"), 1)
                    dve.wait_ge(S("hy_Y"), 2 * fc + 1)
                    TT(hy_t[:, 0, :], re, hf_F[:, 2 + fc, :], ALU.mult).then_inc(fr[fc].free.sem, 1)
                    TT(hy_t[:, 1, :], im, hf_F[:, fc, :], ALU.mult).then_inc(fr[2 + fc].free.sem, 1)
                    fr[fc].free.wait(dve)
                    fr[2 + fc].free.wait(dve)
                    TT(hy_Y[:, 2 + fc, :], hy_t[:, 0, :], hy_t[:, 1, :], ALU.add).then_inc(S("hy_Y"), 1)
                for m, f in enumerate(plan["hy_out"]):
                    f.full.wait(dve)
                    STT(hy_y[:, m, :], hy_z[:, m, :], col("hf_bias", m), PS[:, f.bank, 0:N], ALU.mult, ALU.add)\
                        .then_inc(f.free.sem, 1)
                for m, f in enumerate(plan["hy_out"]):
                    f.free.wait(dve)
                    TT(hy_y[:, m, :], hy_y[:, m, :], hy_z[:, 8 + m, :], ALU.mult).then_inc(S("hy_y"), 1)
                for i in range(8):
                    width = N if i < 4 else 2 * N
                    rsqrt_wait(dve, c)
                    plan["qk_in"][i].free.wait(dve)
                    STT(da_qk[:, i, 0:width], da_qk[:, i, 0:width], col("g_q" if i < 4 else "g_k"), da_rs[:, i, 0:width],
                        ALU.mult, ALU.mult).then_inc(S("qk_n"), 1)
                for i, f in enumerate(plan["qk_rot"]):
                    f.full.wait(dve)
                    TT(da_sq[:, i, 0:N], PS[:, f.bank, 0:N], da_sin, ALU.mult).then_inc(f.free.sem, 1)
                    ch.do(TT(da_qk[:, i, 0:N], da_qk[:, i, 0:N], da_cos, ALU.mult))
                    f.free.wait(dve)
                    TT(da_qk[:, i, 0:N], da_qk[:, i, 0:N], da_sq[:, i, 0:N], ALU.add).then_inc(S("qk_rope"), 1)

                def da_max(i):
                    for j in range(2):
                        k = 2 * i + j
                        f = plan["da_scores"][k]
                        f.full.wait(dve)
                        ch.do(V_.tensor_reduce(stat8[:, k:k + 1], PS[:, f.bank, :], AX.X, ALU.max))
                        TS(stat8[:, 16 + k:17 + k], stat8[:, k:k + 1], -0.125, None, ALU.mult).then_inc(S("da_nb"), 1)

                dve.wait_ge(S("qk_rope"), 8)
                da_max(0)
                for i in range(8):
                    if i < 7:
                        da_max(i + 1)
                    f0, f1 = plan["da_scores"][2 * i:2 * i + 2]
                    f0.free.wait(dve)
                    f1.free.wait(dve)
                    r = stat8[:, 48 + 2 * i:50 + 2 * i]
                    ch.do(V_.reciprocal(r, stat8[:, 32 + 2 * i:34 + 2 * i]))
                    ch.put(TT(r[:, 1:2], r[:, 1:2], small[:, 5:6], ALU.mult))
                    if i >= 2:
                        plan["da_turn"][i - 2].full.wait(dve)
                    ch.do(TS(da_a[:, i % 2, :], da_p[:, i % 2, 0, :], r[:, 0:1], None, ALU.mult))
                    STT(da_a[:, i % 2, :], da_p[:, i % 2, 1, :], r[:, 1:2], da_a[:, i % 2, :], ALU.mult, ALU.add)\
                        .then_inc(S("da_a"), 1)
                for h in range(4):
                    rsqrt_wait(dve, c)
                    STT(da_o[:, h, :], da_o[:, h, :], small[:, 6:7], da_rso[:, h, :], ALU.mult, ALU.mult)\
                        .then_inc(S("da_o"), 1)
                residual_dve(ch, "cd_out", 1, 2, 1)
                for f in plan["cd_out"][-4:]:
                    f.free.wait(dve)
            if LAST >= 4:
                moe_dve(1, 1)

            def mla_dve(i):
                p, j = f"b{i}_", n_mla[i]
                lat = plan[p + "lat"]
                norm_dve(dve, c, p + "norm", i + 2, 0, 1)
                if j == 0:
                    dve.wait_ge(S("pos"), 16)
                    ch.do(V_.tensor_copy(pos_f, pos_i))
                    for r in range(4):
                        ch.do(TS(rope_tab[:, r, :], pos_f, invf[:, r // 2:r // 2 + 1], None, ALU.mult))
                        trig(rope_tab[:, r, :], rope_k, P, r % 2 == 0).then_inc(S("tab_arg"), 1)
                        dve.wait_ge(S("tab_arg"), r + 1)
                rsqrt_wait(dve, c)
                for m in range(2):
                    STT(ml_qlat[:, m, :], PS[:, lat[m].bank, 0:N], col("mla_q_norm_2", 2 * j + m), RS[:, 0:N],
                        ALU.mult, ALU.mult).then_inc(lat[m].free.sem, 1)
                rsqrt_wait(dve, c)
                STT(ml_kvlat, PS[:, lat[2].bank, 0:N], col("mla_kv_norm_2", j), RS[:, N:2 * N], ALU.mult, ALU.mult)\
                    .then_inc(lat[2].free.sem, 1)
                f = plan[p + "kper"][0]
                cos, sin = rope_tab[0:64, 0, :], rope_tab[0:64, 1, :]
                f.full.wait(dve)
                dve.wait_ge(S("tab"), 4)
                TT(ml_kt[0:64, :], PS[0:64, f.bank, 0:N], sin, ALU.mult).then_inc(f.free.sem, 1)
                lat[3].free.wait(dve)
                ch.do(TT(ml_kpe[0:64, :], ml_kpe[0:64, :], cos, ALU.mult))
                f.free.wait(dve)
                TT(ml_kpe[0:64, :], ml_kpe[0:64, :], ml_kt[0:64, :], ALU.add).then_inc(S("ml_rope"), 1)
                for r, f in enumerate(plan[p + "qrot"]):
                    pair = ml_qpe[0:64, 2 * r:2 * r + 2, :]
                    tmp = ml_qt[0:64, 2 * r:2 * r + 2, :]
                    f.full.wait(dve)
                    TT(tmp, PS[0:64, f.bank, :].rearrange("p (h t) -> p h t", h=2),
                       sin.unsqueeze(1).to_broadcast([64, 2, N]), ALU.mult).then_inc(f.free.sem, 1)
                    ch.do(TT(pair, pair, cos.unsqueeze(1).to_broadcast([64, 2, N]), ALU.mult))
                    f.free.wait(dve)
                    TT(pair, pair, tmp, ALU.add).then_inc(S("ml_rope"), 1)

                def soft_a(i2):
                    qc = i2 % 2
                    width = (qc + 1) * P
                    f = plan[p + "scores"][i2]
                    f.full.wait(dve)
                    if i2 >= 4:
                        plan[p + "turn"][i2 - 4].full.wait(dve)
                    s = ml_s[:, i2 % 4, 0:width]
                    STT(s, PS[:, f.bank, 0:width], mla_scale, ml_causal[:, qc, 0:width], ALU.mult, ALU.add)\
                        .then_inc(f.free.sem, 1)
                    f.free.wait(dve)
                    ch.do(V_.tensor_reduce(stat8[:, i2:i2 + 1], s, AX.X, ALU.max))
                    TS(stat8[:, 16 + i2:17 + i2], stat8[:, i2:i2 + 1], -1.0, None, ALU.mult).then_inc(S("ml_nb"), 1)

                def soft_b(i2):
                    width = (i2 % 2 + 1) * P
                    dve.wait_ge(S("ml_exp"), 16 * j + i2 + 1)
                    ch.do(V_.reciprocal(stat8[:, 48 + i2:49 + i2], stat8[:, 32 + i2:33 + i2]))
                    s = ml_s[:, i2 % 4, 0:width]
                    TS(s, s, stat8[:, 48 + i2:49 + i2], None, ALU.mult).then_inc(S("ml_p"), 1)

                for s in range(16 + 2):
                    if s < 16:
                        soft_a(s)
                    if s >= 2:
                        soft_b(s - 2)
                for m, f in enumerate(plan[p + "pv"]):
                    f.free.wait(dve)
                    TT(ml_o_lo[:, m, :], ml_o[:, m, :], x_hi[:, m, :].bitcast(F32), ALU.subtract).then_inc(S("x_lo"), 1)

            def stick_dve(i):
                p = f"b{i}_"
                norm_dve(dve, c, p + "norm", i + 2, 0, 1, split="mixer")
                split_dve(dve, [p + "qk", p + "v"])
                dve.wait_ge(S("st_const"), 16)
                for s in range(16 + 3):
                    if s < 16:
                        f = plan[p + "z"][s]
                        f.full.wait(dve)
                        if s >= 4:
                            k = s - 4
                            if k % 2:
                                plan[p + "pv"][k // 2].full.wait(dve)
                            else:
                                dve.wait_ge(S("st_pv"), k // 2 + 1)
                            plan[p + "suf"][k].full.wait(dve)
                        STT(st_t[:, s % 4, :], PS[:, f.bank, 0:384], 0.125, st_mask, ALU.mult, ALU.add)\
                            .then_inc(f.free.sem, 1)
                        f.free.wait(dve)
                        STT(st_sp[:, s % 4, :], st_t[:, s % 4, :], -1.0, st_t[:, s % 4, :], ALU.mult, ALU.max)\
                            .then_inc(S("st_abs"), 1)
                    if 1 <= s <= 16:
                        k = s - 1
                        dve.wait_ge(S("st_l"), k + 1)
                        STT(st_sp[:, k % 4, :], st_t[:, k % 4, :], 0.0, st_sp[:, k % 4, :], ALU.max, ALU.add)\
                            .then_inc(S("st_sp"), 1)
                    if 2 <= s <= 17:
                        k = s - 2
                        f = plan[p + "suf"][k]
                        f.full.wait(dve)
                        TT(st_t[:, k % 4, :], st_t[:, k % 4, :], PS[:, f.bank, 0:384], ALU.subtract)\
                            .then_inc(f.free.sem, 1)
                        f.free.wait(dve)
                        TS(st_t[:, k % 4, :], st_t[:, k % 4, :], 0.0, None, ALU.min).then_inc(S("st_arg"), 1)
                for m, f in enumerate(plan[p + "pv"]):
                    f.free.wait(dve)
                    TT(st_o_lo[:, m, :], st_o[:, m, :], x_hi[:, m, :].bitcast(F32), ALU.subtract).then_inc(S("x_lo"), 1)

            def ret_dve(i):
                p = f"b{i}_"
                norm_dve(dve, c, p + "norm", i + 2, 0, 1, split="mixer")
                cos, sin = rope_tab[:, 2, :], rope_tab[:, 3, :]

                def rotate(name, m, f):
                    if name != p + "qk" or m % 2 == 0:
                        return
                    r = m // 2
                    x1, x2 = rt_qk[:, m - 1, :], rt_qk[:, m, :]
                    plan[name][m - 1].free.wait(dve)
                    f.free.wait(dve)
                    if r:
                        dve.wait_ge(S("rt_rope"), r)
                    ch.put(TT(rt_t[:, 0, :], x1, sin, ALU.mult))
                    ch.put(TT(rt_t[:, 1, :], x2, sin, ALU.mult))
                    ch.put(TT(x1, x1, cos, ALU.mult))
                    ch.put(TT(x2, x2, cos, ALU.mult))
                    ch.sync()
                    ch.put(TT(x1, x1, rt_t[:, 1, :], ALU.subtract))
                    TT(x2, x2, rt_t[:, 0, :], ALU.add).then_inc(S("rt_rope"), 1)
                    ch.sync()

                split_dve(dve, [p + "qk", p + "v", p + "g"], rotate)
                dve.wait_ge(S("rt_const"), 16)
                for h, f in enumerate(plan[p + "s"]):
                    f.full.wait(dve)
                    TT(rt_s[:, h, :], PS[:, f.bank, 0:384], rt_decay[:, h, :], ALU.mult).then_inc(f.free.sem, 1)
                for h in range(4):
                    rsqrt_wait(dve, c)
                    for q in range(4):
                        m = 4 * h + q
                        ch.do(STT(rt_o[:, m, :], rt_o[:, m, :], col("ret_gn_g_2", m), rt_rs[:, h, :], ALU.mult, ALU.mult))
                        plan[p + "g"][m].free.wait(dve)
                        TT(rt_o[:, m, :], rt_o[:, m, :], rt_g[:, m, :], ALU.mult).then_inc(S("rt_o"), 1)
                for m in range(16):
                    dve.wait_ge(S("rt_o_hi"), m + 1)
                    TT(rt_o_lo[:, m, :], rt_o[:, m, :], rt_o_hi[:, m, :].bitcast(F32), ALU.subtract)\
                        .then_inc(S("rt_o_lo"), 1)

            def post_dve(i, name, which):
                rsqrt_wait(dve, c)
                for m in range(KC):
                    ch.put(STT(y_T[:, m, :], y_T[:, m, :], GP[:, i, which, m:m + 1], RS[:, 0:N], ALU.mult, ALU.mult))
                for m in range(KC):
                    ch.sync(back=KC - 1 - m)
                    TT(hT[:, m, 0:N], hT[:, m, 0:N], y_T[:, m, :], ALU.add).then_inc(S("h_done"), 1)

            nh = 0
            for i, kind in enumerate(KINDS[:max(0, LAST - 4)]):
                p = f"b{i}_"
                {"mla": mla_dve, "stick": stick_dve, "ret": ret_dve}[kind](i)
                split_dve(dve, [p + "out"])
                post_dve(i, p + "post", 0)
                nh += 1
                dve.wait_ge(S("h_done"), KC * nh)
                norm_dve(dve, c, p + "fnorm", i + 2, 1, 1, split="ffn")
                fu = plan[p + "up"]
                with dve.Fori(0, 4) as it:
                    for n in range(16):
                        _, w, w_lo = quarter(p, n)
                        dve.wait_ge(S("ffn_w_hi"), 64 * i + n + 1 + it * 16)
                        TT(w_lo, w, w_hi[:, n % 4].bitcast(F32), ALU.subtract).then_inc(S("ffn_w_lo"), 1)
                        if 4 <= n < 12:
                            h = ffn_h[:, n // 4 - 1, n % 4, :]
                            fu[n - 4].free.wait(dve, it)
                            TT(h, h, h, ALU.mult).then_inc(S("ffn_squared"), 1)
                        if 5 <= n < 13:
                            k = n - 5
                            h = ffn_h[:, k // 4, k % 4, :]
                            dve.wait_ge(S("ffn_h_hi"), 32 * i + k + 1 + it * 8)
                            TT(ffn_h_lo[:, k // 4, k % 4, :], h, ffn_h_hi[:, k // 4, k % 4, :].bitcast(F32), ALU.subtract)\
                                .then_inc(S("ffn_h_lo"), 1)
                        if i < 3 and n in (10, 12, 15):
                            q = (10, 12, 15).index(n)
                            cols_dve(plan[p + "ada_cols"][q], 192 + (i + 1) * 48 + 4 * q, 12, 2, 1, it)
                if i < 3:
                    plan[p + "ada_cols"][-1].free.wait(dve, 3)
                    gains_second(i + 1)
                    TS(small[:, 7:8], small[:, 5:6], 1.0, None, ALU.mult).then_inc(S("mod_ready"), 1)
                post_dve(i, p + "fpost", 1)
                nh += 1
                dve.wait_ge(S("h_done"), KC * nh)
            TS(small[:, 8:9], small[:, 5:6], 1.0, None, ALU.mult).then_inc(S("h_final"), 1)
            for i, f in enumerate(plan["final"]):
                t, kq = i // 2, i % 2
                f.full.wait(dve)
                ins = V_.tensor_copy(out_tok[:, t, kq * 512:(kq + 1) * 512], PS[:, f.bank, :])
                if kq == 1:
                    ins.then_inc(S("out_ready"), 1)
                else:
                    ins.then_inc(f.free.sem, 1)

        @block.gpsimd
        def _(pool):
            c = counters()
            nc.gpsimd.memset(ones[:, :], 1.0).then_inc(S("cleared"), 1)
            nc.gpsimd.memset(zeros_bf[:, :], 0.0).then_inc(S("cleared"), 1)
            nc.gpsimd.memset(cond[:, :, :], 0.0).then_inc(S("cleared"), 1)
            nc.gpsimd.memset(small[:, 9:10], EPS).then_inc(S("cleared"), 1)
            nc.gpsimd.memset(small[:, 10:11], SUBLN_EPS).then_inc(S("cleared"), 1)

            def moe_pool(l, ns):
                p = f"moe{l}_"
                fs = plan[p + "experts"]
                for f in plan[p + "gather"][-4:]:
                    f.free.wait(pool)
                if ns == 1:
                    nc.gpsimd.memset(x_cur[:, :, :, CAP:2 * CAP], 0.0).then_inc(S("x_zero"), 1)
                    pool.wait_ge(S("x_zero"), 1)
                with pool.Fori(0, 4) as it:
                    for j in range(4):
                        fs[4 * ((j + 2) % 4) + 1].full.wait(pool, it if j >= 2 else it - 1)
                        nc.gpsimd.tensor_copy(
                            x_cur[:, j % 2, :, 0:CAP * ns].rearrange("p k (s c) -> p k s c", s=ns),
                            moe_xe[:, :, bass.ds(it * 4 + j, 1), 0:ns, :].rearrange("p k o s c -> p k (o s) c"))\
                            .then_inc(S("x_cur"), 1)

            if LAST >= 1:
                pool.wait_ge(S("mod_ready"), 1)
                nc.gpsimd.memset(ab_gv, 0.0).then_inc(S("ab_pads"), 1)
                nc.gpsimd.memset(ab_zin, 0.0).then_inc(S("ab_pads"), 1)
                fs = plan["ab_in"]
                pool.wait_ge(S("ab_pads"), 2)
                for m in range(4):
                    fs[8 + m].free.wait(pool)
                    fs[12 + m].free.wait(pool)
                    nc.gpsimd.tensor_tensor(ab_gv[:, m, :, 1:N + 1], v512(ab_gin[:, m, :]), v512(ab_val[:, m, :]),
                                            ALU.mult).then_inc(S("ab_gv"), 1)
            if LAST >= 2:
                moe_pool(0, 2)
            if LAST >= 3:
                plan["moe0_combine"][-1].free.wait(pool)
                nc.gpsimd.memset(hy_p, 0.0).then_inc(S("hp_pad"), 1)
            if LAST >= 4:
                moe_pool(1, 1)
            for i, kind in enumerate(KINDS[:max(0, LAST - 4)]):
                p = f"b{i}_"
                if kind == "mla":
                    if i == 0:
                        plan["moe1_combine"][-1].free.wait(pool)
                    else:
                        pool.wait_ge(S("h_done"), 2 * KC * i)
                    nc.gpsimd.memset(ml_pT, 0.0).then_inc(S("pT_zero"), 1)


def kernel(**inputs):
    import numpy as _np
    import concourse.bacc as _bacc
    from concourse import mybir as _mybir
    from concourse.bass_utils import run_bass_kernel_spmd as _run

    nc = _bacc.Bacc("TRN2", target_bir_lowering=False, num_devices=1)
    arrays, aps = {}, {}
    given = {name: _np.ascontiguousarray(inputs[name]) for name in _PARAMS}
    given["c_ctx"] = given["c_ctx"].reshape(1, D)
    for name, v in {**given, **shape_constants()}.items():
        if name.startswith("k_"):
            v = _np.ascontiguousarray(v, _np.float32)
        arrays[f"in_{name}"] = v
        aps[name] = nc.dram_tensor(f"in_{name}", v.shape, _mybir.dt.from_np(v.dtype), kind="ExternalInput").ap()
    out = nc.dram_tensor("out", (1, N, D), _mybir.dt.float32, kind="ExternalOutput").ap()
    block_program(nc, aps, out)
    r = _run(nc, [arrays], core_ids=[0])
    return r.results[0]["out"]
```
